# Optimizing a Trainium2 kernel written in Bass

```python
import functools
import jax
import jax.numpy as jnp
from jax import lax
import numpy as np

D_MODEL = 1024
BATCH = 1
SEQ = 512
DEPTH = 2
DEC_BATCH = 8
DEC_SEQ = 4
PAST_LEN = 2048
PAGE_SIZE = 128

LRU_WIDTH = D_MODEL // 2
LRU_BLOCKS = 8
LRU_BLOCK = LRU_WIDTH // LRU_BLOCKS
CONV_W = 4
LRU_C = 8.0
N_HEADS = 8
HEAD_DIM = 64
ATT_WIDTH = N_HEADS * HEAD_DIM
N_KV = 2
Q_PER_KV = N_HEADS // N_KV
ROPE_DIM = HEAD_DIM // 4
ROPE_THETA = 500000.0
IDX_HEADS = 4
IDX_DIM = 64
TOP_K = 256
Q_BLOCK = 128
D_FF = 2816
N_MOD = 9
RMS_EPS = 1e-6
IN_SIZES = (LRU_WIDTH, LRU_WIDTH, ATT_WIDTH, N_KV * HEAD_DIM, N_KV * HEAD_DIM, IDX_HEADS * IDX_DIM, IDX_DIM, IDX_HEADS)
IN_COLS = sum(IN_SIZES)

kernel_name = 'hymba_rglru_dsa_macaron_decoder_step'

F32 = jnp.float32

def rms_norm(x, g):
    x32 = x.astype(F32)
    y = x32 * lax.rsqrt(jnp.mean(x32 * x32, axis=-1, keepdims=True) + RMS_EPS)
    return (y * g.astype(F32)).astype(x.dtype)

def swiglu(h, w_gu, w_dn):
    g, u = jnp.split(h @ w_gu, 2, axis=-1)
    return (jax.nn.silu(g) * u) @ w_dn

def rope_partial(x, pos):
    half = ROPE_DIM // 2
    freqs = ROPE_THETA ** (-(jnp.arange(half, dtype=F32) / half))
    ang = pos.astype(F32)[:, None] * freqs[None, :]
    cos = jnp.cos(ang)[None, :, None, :]
    sin = jnp.sin(ang)[None, :, None, :]
    xr = x[..., :ROPE_DIM].astype(F32)
    x1, x2 = xr[..., :half], xr[..., half:]
    rot = jnp.concatenate([x1 * cos - x2 * sin, x2 * cos + x1 * sin], axis=-1).astype(x.dtype)
    return jnp.concatenate([rot, x[..., ROPE_DIM:]], axis=-1)

def split_cols(t):
    parts, start = [], 0
    for n in IN_SIZES:
        parts.append(t[..., start:start + n])
        start += n
    return parts

def project(h, w_in, pos):
    B, T = h.shape[:2]
    xl, gl, q, k, v, qi, ki, wi = split_cols(h @ w_in)
    q = rope_partial(q.reshape(B, T, N_HEADS, HEAD_DIM), pos)
    k = rope_partial(k.reshape(B, T, N_KV, HEAD_DIM), pos)
    v = v.reshape(B, T, N_KV, HEAD_DIM)
    qi = rope_partial(qi.reshape(B, T, IDX_HEADS, IDX_DIM), pos)
    ki = rope_partial(ki.reshape(B, T, 1, IDX_DIM), pos)[:, :, 0]
    return xl, gl, q, k, v, qi, ki, wi

def causal_conv(x, buf, w, b):
    T = x.shape[1]
    xp = jnp.concatenate([buf.astype(x.dtype), x], axis=1)
    out = b
    for j in range(CONV_W):
        out = out + xp[:, j:j + T] * w[j]
    return out, xp[:, -(CONV_W - 1):]

def rg_lru(xc, h0, wa, ba, wx, bx, lam):
    B, T, _ = xc.shape
    x32 = xc.astype(F32)
    xb = x32.reshape(B, T, LRU_BLOCKS, LRU_BLOCK)
    r = jax.nn.sigmoid(jnp.einsum('btni,nij->btnj', xb, wa.astype(F32)).reshape(B, T, LRU_WIDTH) + ba.astype(F32))
    i = jax.nn.sigmoid(jnp.einsum('btni,nij->btnj', xb, wx.astype(F32)).reshape(B, T, LRU_WIDTH) + bx.astype(F32))
    log_a = -LRU_C * r * jax.nn.softplus(-lam.astype(F32))
    a = jnp.exp(log_a)
    bt = jnp.sqrt(-jnp.expm1(2.0 * log_a)) * (i * x32)

    def step(h, ab):
        h = ab[0] * h + ab[1]
        return h, h

    hT, hs = lax.scan(step, h0, (jnp.swapaxes(a, 0, 1), jnp.swapaxes(bt, 0, 1)))
    return jnp.swapaxes(hs, 0, 1), hT

def select_keys(qi, wi, ki, q_pos, n_sel):
    dots = jnp.einsum('bthd,bsd->bths', qi, ki).astype(F32) * (IDX_DIM ** -0.5)
    score = jnp.einsum('bths,bth->bts', jax.nn.relu(dots), wi.astype(F32) * (IDX_HEADS ** -0.5))
    causal = jnp.arange(ki.shape[1])[None, :] <= q_pos[:, None]
    score = jnp.where(causal[None], score, -jnp.inf)
    _, idx = lax.top_k(score, n_sel)
    valid = idx <= q_pos[None, :, None]
    return idx, valid

def sparse_attend(q, k_sel, v_sel, valid):
    B, T = q.shape[:2]
    qg = q.reshape(B, T, N_KV, Q_PER_KV, HEAD_DIM)
    s = jnp.einsum('btkgd,btskd->btkgs', qg, k_sel).astype(F32) * (HEAD_DIM ** -0.5)
    s = jnp.where(valid[:, :, None, None, :], s, -jnp.inf)
    p = jax.nn.softmax(s, axis=-1).astype(v_sel.dtype)
    o = jnp.einsum('btkgs,btskd->btkgd', p, v_sel)
    return o.reshape(B, T, ATT_WIDTH)

def gather_rows(t, idx):
    return jax.vmap(lambda tt, ii: tt[ii])(t, idx)

def prompt_attention(q, k, v, qi, ki, wi):
    B, S = q.shape[:2]
    n_sel = min(TOP_K, S // 4)
    nblk = S // Q_BLOCK

    def blk(args):
        j, qb, qib, wib = args
        pos = j * Q_BLOCK + jnp.arange(Q_BLOCK, dtype=jnp.int32)
        idx, valid = select_keys(qib, wib, ki, pos, n_sel)
        flat = idx.reshape(B, Q_BLOCK * n_sel)
        ks = gather_rows(k, flat).reshape(B, Q_BLOCK, n_sel, N_KV, HEAD_DIM)
        vs = gather_rows(v, flat).reshape(B, Q_BLOCK, n_sel, N_KV, HEAD_DIM)
        return sparse_attend(qb, ks, vs, valid)

    def to_blocks(t):
        return jnp.moveaxis(t.reshape(B, nblk, Q_BLOCK, *t.shape[2:]), 1, 0)

    out = lax.map(blk, (jnp.arange(nblk, dtype=jnp.int32), to_blocks(q), to_blocks(qi), to_blocks(wi)))
    return jnp.moveaxis(out, 0, 1).reshape(B, S, ATT_WIDTH)

def sample_attention(q, k, v, qi, ki, wi, cache_k, cache_v, cache_kidx, page_table, layer):
    DB, DS = q.shape[:2]
    page = cache_k.shape[2]
    past_len = page_table.shape[1] * page
    n_sel = min(TOP_K, (past_len + DS) // 4)
    ki_past = cache_kidx[layer, page_table].reshape(DB, past_len, IDX_DIM).astype(ki.dtype)
    ki_all = jnp.concatenate([ki_past, ki], axis=1)
    q_pos = past_len + jnp.arange(DS, dtype=jnp.int32)
    idx, valid = select_keys(qi, wi, ki_all, q_pos, n_sel)
    in_past = (idx < past_len)[..., None, None]
    pidx = jnp.minimum(idx, past_len - 1)
    phys = page_table[jnp.arange(DB)[:, None, None], pidx // page]
    off = pidx % page
    nidx = jnp.clip(idx - past_len, 0, DS - 1).reshape(DB, DS * n_sel)
    k_new = gather_rows(k, nidx).reshape(DB, DS, n_sel, N_KV, HEAD_DIM)
    v_new = gather_rows(v, nidx).reshape(DB, DS, n_sel, N_KV, HEAD_DIM)
    ks = jnp.where(in_past, cache_k[layer, phys, off].astype(k.dtype), k_new)
    vs = jnp.where(in_past, cache_v[layer, phys, off].astype(v.dtype), v_new)
    return sparse_attend(q, ks, vs, valid)

def layer_forward(x, c, pos, lw, conv_buf, h0, attn_fn):
    (w_ada_l, b_ada_l, g, w_gu, w_dn, w_in_l, cw, cb, wa, ba, wx, bx, lam, w_o) = lw
    mod = (c @ w_ada_l + b_ada_l).reshape(c.shape[0], N_MOD, -1)
    sh1, sc1, gt1, sh2, sc2, gt2, sh3, sc3, gt3 = [mod[:, m][:, None, :] for m in range(N_MOD)]
    f = swiglu(rms_norm(x, g[0]) * (1 + sc1) + sh1, w_gu[0], w_dn[0])
    x = x + 0.5 * gt1 * rms_norm(f, g[1])
    h = rms_norm(x, g[2]) * (1 + sc2) + sh2
    xl, gl, q, k, v, qi, ki, wi = project(h, w_in_l, pos)
    xc, new_buf = causal_conv(xl, conv_buf, cw, cb)
    hs, hT = rg_lru(xc, h0, wa, ba, wx, bx, lam)
    y_lru = (hs * jax.nn.gelu(gl.astype(F32))).astype(h.dtype)
    y_att = attn_fn(q, k, v, qi, ki, wi)
    y = jnp.concatenate([y_lru, y_att.astype(h.dtype)], axis=-1) @ w_o
    x = x + gt2 * rms_norm(y, g[3])
    f = swiglu(rms_norm(x, g[4]) * (1 + sc3) + sh3, w_gu[1], w_dn[1])
    x = x + 0.5 * gt3 * rms_norm(f, g[5])
    return x, (k, v, ki, hT, new_buf)

def setup_inputs(seed: int = 0) -> dict:
    key = jax.random.key(seed)
    ks = jax.random.split(key, 24)
    n_pages = PAST_LEN // PAGE_SIZE
    n_used = DEC_BATCH * n_pages
    n_pool = n_used + n_used // 4
    nrm = jax.random.normal
    page_table = jax.random.permutation(ks[0], n_pool)[:n_used].reshape(DEC_BATCH, n_pages).astype(jnp.int32)
    a0 = jax.random.uniform(ks[1], (DEPTH, LRU_WIDTH), F32, 0.9, 0.999)
    a = a0 ** (1.0 / LRU_C)
    lru_lambda = jnp.log(a) - jnp.log1p(-a)
    return {
        'x_prompt': nrm(ks[2], (BATCH, SEQ, D_MODEL), F32),
        'x_sample': nrm(ks[3], (DEC_BATCH, DEC_SEQ, D_MODEL), F32),
        'c_prompt': nrm(ks[4], (BATCH, D_MODEL), F32),
        'c_sample': nrm(ks[5], (DEC_BATCH, D_MODEL), F32),
        'cache_k': nrm(ks[6], (DEPTH, n_pool, PAGE_SIZE, N_KV, HEAD_DIM), F32),
        'cache_v': nrm(ks[7], (DEPTH, n_pool, PAGE_SIZE, N_KV, HEAD_DIM), F32),
        'cache_kidx': nrm(ks[8], (DEPTH, n_pool, PAGE_SIZE, IDX_DIM), F32),
        'state_h': 0.5 * nrm(ks[9], (DEPTH, DEC_BATCH, LRU_WIDTH), F32),
        'state_conv': nrm(ks[10], (DEPTH, DEC_BATCH, CONV_W - 1, LRU_WIDTH), F32),
        'page_table': page_table,
        'w_ada': 0.3 * D_MODEL ** -0.5 * nrm(ks[11], (DEPTH, D_MODEL, N_MOD * D_MODEL), F32),
        'b_ada': 0.02 * nrm(ks[12], (DEPTH, N_MOD * D_MODEL), F32),
        'norm_g': 1.0 + 0.05 * nrm(ks[13], (DEPTH, 6, D_MODEL), F32),
        'ffn_w_gu': D_MODEL ** -0.5 * nrm(ks[14], (DEPTH, 2, D_MODEL, 2 * D_FF), F32),
        'ffn_w_down': D_FF ** -0.5 * nrm(ks[15], (DEPTH, 2, D_FF, D_MODEL), F32),
        'w_in': D_MODEL ** -0.5 * nrm(ks[16], (DEPTH, D_MODEL, IN_COLS), F32),
        'conv_w': CONV_W ** -0.5 * nrm(ks[17], (DEPTH, CONV_W, LRU_WIDTH), F32),
        'conv_b': 0.02 * nrm(ks[18], (DEPTH, LRU_WIDTH), F32),
        'lru_wa': LRU_BLOCK ** -0.5 * nrm(ks[19], (DEPTH, LRU_BLOCKS, LRU_BLOCK, LRU_BLOCK), F32),
        'lru_ba': 0.02 * nrm(ks[20], (DEPTH, LRU_WIDTH), F32),
        'lru_wx': LRU_BLOCK ** -0.5 * nrm(ks[21], (DEPTH, LRU_BLOCKS, LRU_BLOCK, LRU_BLOCK), F32),
        'lru_bx': 0.02 * nrm(ks[22], (DEPTH, LRU_WIDTH), F32),
        'lru_lambda': lru_lambda,
        'w_out': D_MODEL ** -0.5 * nrm(ks[23], (DEPTH, D_MODEL, D_MODEL), F32),
    }

def reference(x_prompt, x_sample, c_prompt, c_sample, cache_k, cache_v, cache_kidx, state_h, state_conv, page_table,
              w_ada, b_ada, norm_g, ffn_w_gu, ffn_w_down, w_in, conv_w, conv_b, lru_wa, lru_ba, lru_wx, lru_bx,
              lru_lambda, w_out):
    B, S = x_prompt.shape[:2]
    DB, DS = x_sample.shape[:2]
    past_len = page_table.shape[1] * cache_k.shape[2]
    pos_p = jnp.arange(S, dtype=jnp.int32)
    pos_s = past_len + jnp.arange(DS, dtype=jnp.int32)
    yp, ys = x_prompt, x_sample
    kp, vp, kip, hp, cp = [], [], [], [], []
    kS, vS, kiS, hS, cS = [], [], [], [], []
    for l in range(DEPTH):
        lw = (w_ada[l], b_ada[l], norm_g[l], ffn_w_gu[l], ffn_w_down[l], w_in[l], conv_w[l], conv_b[l],
              lru_wa[l], lru_ba[l], lru_wx[l], lru_bx[l], lru_lambda[l], w_out[l])
        buf0 = jnp.zeros((B, CONV_W - 1, LRU_WIDTH), x_prompt.dtype)
        h0 = jnp.zeros((B, LRU_WIDTH), F32)
        yp, (k1, v1, ki1, h1, c1) = layer_forward(yp, c_prompt, pos_p, lw, buf0, h0, prompt_attention)
        attn_s = functools.partial(sample_attention, cache_k=cache_k, cache_v=cache_v, cache_kidx=cache_kidx,
                                   page_table=page_table, layer=l)
        ys, (k2, v2, ki2, h2, c2) = layer_forward(ys, c_sample, pos_s, lw, state_conv[l],
                                                  state_h[l].astype(F32), attn_s)
        kp.append(k1); vp.append(v1); kip.append(ki1); hp.append(h1.astype(x_prompt.dtype)); cp.append(c1)
        kS.append(k2); vS.append(v2); kiS.append(ki2); hS.append(h2.astype(state_h.dtype)); cS.append(c2.astype(state_conv.dtype))
    return (yp, ys, jnp.stack(kp), jnp.stack(vp), jnp.stack(kip), jnp.stack(hp), jnp.stack(cp),
            jnp.stack(kS), jnp.stack(vS), jnp.stack(kiS), jnp.stack(hS), jnp.stack(cS))


_drawn_inputs = setup_inputs


def setup_inputs(seed=0):
    import zlib

    import numpy as np

    out = dict(_drawn_inputs(seed))
    spreads = {}
    factors = {'lru_ba': 8.0, 'lru_bx': 6.237}
    for name, (base, spread) in spreads.items():
        noise = np.random.default_rng([zlib.crc32(name.encode()), seed]).standard_normal(out[name].shape)
        drawn = base * np.exp(spread * noise) if base else spread * noise
        out[name] = jnp.asarray(drawn.astype(out[name].dtype))
    for name, factor in factors.items():
        out[name] = (out[name] * factor).astype(out[name].dtype)
    return out
```

```python
from contextlib import ExitStack, contextmanager

import numpy as np

import concourse.bass as bass
from concourse import mybir

F32 = mybir.dt.float32
I32 = mybir.dt.int32
ALU = mybir.AluOpType
ACT = mybir.ActivationFunctionType
AX = mybir.AxisListType
RMAX = bass.bass_isa.ReduceOp.max

P = 128
DEPTH, D, SEQ, NSEQ, STEPS = 2, 1024, 512, 8, 4
NS = NSEQ * STEPS
T = SEQ + NS
TH = T // 2
DC = D // P
D_FF = 2816
FC = D_FF // P
LC = 4
CONV = 4
HEADS, HD, NKV = 8, 64, 2
IH = 4
NMOD = 9
NC_ = 1 + NSEQ
MC = NMOD * DC
IN_COLS = 2116
PC = IN_COLS // P
LAST = IN_COLS - PC * P
XL, GL, QQ, KK, VV, QI, KW = 0, 4, 8, 12, 13, 14, 16
PAGES, PAGE, POOL = 16, 128, 160
NB = PAGES + 1
TILES = SEQ // P
SEL_P, SEL_S = 128, 256
EPS = 1e-6
NEG = -1.0e30
TAKEN = -3.0e38
ROPED = [QQ, QQ + 1, QQ + 2, QQ + 3, KK, QI, QI + 1, KW]
GELU_C = float(np.sqrt(2.0 / np.pi))
SW = 3 + STEPS
XPW = 3 + SEQ + NSEQ * SW

C_ID, C_ONE, C_SWAP, C_COS, C_SIN = 0, P, 2 * P, 3 * P, 3 * P + T
C_TRI = C_SIN + T
C_MS = C_TRI + P
C_SEL = C_MS + NS
C_ALL = C_SEL + IH * P
V_BADA, V_G, V_CW, V_CB, V_BA, V_BX, V_LAM = 0, 72, 120, 136, 140, 144, 148
V_ALL = 152
ST_H, ST_C, ST_ALL = 0, LC * NSEQ, LC * NSEQ * 4

U_ADA, U_GU, U_IN, U_OUT = MC // 4, FC // 2, PC // 4, DC // 4
W_USES = U_ADA + 2 * U_GU + U_IN + U_OUT
K_ADA, K_GU1 = 0, U_ADA
K_IN = K_GU1 + U_GU
K_OUT = K_IN + U_IN
K_GU2 = K_OUT + U_OUT
D_USES = DC

DVE_STEPS = 381


class Signal:

    def __init__(self, ctx, nc, name, per, unit=1, start=0):
        self.sem = ctx.enter_context(nc.semaphore(name))
        self.per, self.unit, self.start = per, unit, start

    def at(self, layer, k):
        return layer * (self.per * self.unit) + (k * self.unit + self.start)


def hold(eng, passed, sem, value):
    eng.wait_ge(sem, value)
    eng.sem_inc(passed, 1)


class Steps:

    def __init__(self, eng, sem, per, layer, passed):
        self.passed = passed
        self.eng, self.sem, self.per, self.layer, self.n, self.shift = eng, sem, per, layer, 0, 0

    def link(self, ins):
        self.n += 1
        ins.then_inc(self.sem, 1)
        self.eng.wait_ge(self.sem, self.layer * self.per + (self.n + self.shift))

    def link_hold(self, ins):
        self.n += 1
        ins.then_inc(self.sem, 1)
        hold(self.eng, self.passed, self.sem, self.layer * self.per + (self.n + self.shift))

    @contextmanager
    def loop(self, times, body_steps):
        first = self.n
        with self.eng.Fori(0, times) as i:
            self.shift = i * body_steps
            yield i
        assert self.n - first == body_steps, (self.n - first, body_steps)
        self.n = first + times * body_steps
        self.shift = 0


def decoder(nc, a):
    with ExitStack() as ctx:
        def sb(name, shape, dt=F32):
            return ctx.enter_context(nc.sbuf_tensor("sb_" + name, shape, dt))

        def sig(name, per, unit=1, start=0):
            return Signal(ctx, nc, name, per, unit, start)

        ps = ctx.enter_context(nc.psum_tensor("ps", [P, 8, 512], F32))

        x = sb("x", [P, DC, T])
        h = sb("h", [P, DC, T])
        rinv = sb("rinv", [P, T])
        arena = sb("arena", [P, FC * T])
        act = arena[:, :].rearrange("p (f t) -> p f t", f=FC)
        proj = sb("proj", [P, PC + 1, T])
        y = sb("y", [P, DC, T])
        wslot = [sb(f"wslot{i}", [P, 2 * DC * P]) for i in range(2)]
        dslot = [sb(f"dslot{i}", [P, FC, P]) for i in range(2)]
        w_last = sb("w_last", [P, DC, P])
        cst = sb("cst", [P, C_ALL])
        vec = sb("vec", [P, V_ALL])
        state = sb("state", [P, ST_ALL])
        cT = sb("cT", [P, DC, NC_])
        mod = sb("mod", [P, MC, NC_])
        gain = sb("gain", [P, DC, NC_])
        pages = sb("pages", [1, NSEQ * PAGES], I32)
        gates = sb("gates", [P, 2, LC, P])
        small = sb("small", [P, 12, LC])
        eps = sb("eps", [P, 1])
        hout = sb("hout", [P, LC, NC_])
        cout = sb("cout", [P, LC, 3 * NC_])

        sq = proj[:, 0:DC, :]
        tsil = y[:, 0:2, :]

        ident, ones, swap = cst[:, C_ID:C_ID + P], cst[:, C_ONE:C_ONE + P], cst[:, C_SWAP:C_SWAP + P]
        cosT, sinT, tri = cst[:, C_COS:C_COS + T], cst[:, C_SIN:C_SIN + T], cst[:, C_TRI:C_TRI + P]
        mask_new = cst[0:NS, C_MS:C_MS + NS]
        sel = cst[:, C_SEL:C_SEL + IH * P].rearrange("p (h m) -> p h m", h=IH)

        at = [0]

        def carve(*shape):
            n = int(np.prod(shape))
            v = arena[:, at[0]:at[0] + n]
            at[0] += n
            if len(shape) == 2:
                v = v.rearrange("p (a b) -> p a b", a=shape[0])
            if len(shape) == 3:
                v = v.rearrange("p (a b c) -> p a b c", a=shape[0], b=shape[1])
            return v

        xp = carve(LC, XPW)
        xc, ta, tb, tc = carve(LC, T), h[:, 0:LC, :], h[:, LC:DC, :], carve(LC, T)
        th = xp[:, :, 0:T]
        at[0] = 0
        kd = carve(3, SEQ)
        bias_p = carve(TILES, SEQ)
        kpage = [carve(PAGES, PAGE) for _ in range(2)]
        vpage = [h[:, 0:4, :].rearrange("p a b -> p (a b)")[:, 0:PAGES * PAGE].rearrange("p (a b) -> p a b", a=PAGES),
                 h[:, 4:8, :].rearrange("p a b -> p (a b)")[:, 0:PAGES * PAGE].rearrange("p (a b) -> p a b", a=PAGES)]
        top8 = carve(8)
        nmax = carve(HEADS)
        den = carve(HEADS)
        cbuf = carve(NSEQ, 16)
        qiS = carve(NSEQ, 16)
        qS = carve(NSEQ, 32)
        vtok = carve(TILES + 1, P)
        wtok = carve(TILES, IH)
        at_common = at[0]
        score = carve(SEQ)
        work = carve(SEQ)
        prob = [carve(SEQ) for _ in range(2)]
        probT = [carve(SEQ) for _ in range(2)]
        ytok = score
        assert at[0] <= FC * T, at[0]
        pflat = proj[:, 0:8, :].rearrange("p a b -> p (a b)")
        sT = pflat[:, 0:NSEQ * NB * 32]
        sT3 = sT.rearrange("p (s j c) -> p s j c", s=NSEQ, j=NB)
        at[0] = at_common
        scT = carve(NB, NS)
        maskT = carve(NB, NS)
        relu = carve(PAGES, 16)
        mx = carve(NSEQ * 32)
        mxa = carve(NSEQ * 32)
        rden = carve(NSEQ * 32)
        pages_ki = [carve(PAGES, PAGE) for _ in range(0)]
        assert at[0] <= FC * T, at[0]
        scS = pflat[0:NS, 0:PAGES * P + NS]
        wkS = pflat[0:NS, 2176:2176 + PAGES * P + NS]
        kiT = kpage

        s_in = sig("s_in", 0)
        w_full = [sig(f"w_full{i}", W_USES, 2 * 16) for i in range(2)]
        w_free = [sig(f"w_free{i}", W_USES, 1, 1) for i in range(2)]
        d_full = [sig(f"d_full{i}", D_USES, 16) for i in range(2)]
        d_free = [sig(f"d_free{i}", D_USES, 1, 1) for i in range(2)]
        last_full = sig("last_full", 1, 16)
        vec_full = sig("vec_full", 2, 16)
        vec_free = sig("vec_free", 1, 1, 1)
        gate_full = sig("gate_full", 16, 16)
        ki_full = [sig(f"ki_full{i}", 4 * PAGES, 16) for i in range(2)]
        kp_full = [sig(f"kp_full{i}", 4 * PAGES, 16) for i in range(2)]
        vp_full = [sig(f"vp_full{i}", 4 * PAGES, 16) for i in range(2)]
        arena_free = sig("arena_free", 1)
        ki_used = [sig(f"ki_used{i}", 4, 1, 1) for i in range(2)]
        kp_used = [sig(f"kp_used{i}", 4, 1, 1) for i in range(2)]
        vp_used = [sig(f"vp_used{i}", 4, 1, 1) for i in range(2)]
        ada_read = sig("ada_read", NMOD, 1, 1)
        ss_ready = sig("ss_ready", 6)
        sq_ready = sig("sq_ready", 3 * DC)
        root_ready = sig("root_ready", 6)
        xn_ready = sig("xn_ready", 3 * DC)
        h_act = sig("h_act", 3 * DC)
        h_dve = sig("h_dve", 3)
        tanh_ready = sig("tanh_ready", 2 * FC)
        act_ready = sig("act_ready", 2 * FC, 1, 2)
        dn_read = sig("dn_read", 2 * DC, 1, 2)
        res_done = sig("res_done", 3, 1, 1)
        pj_ready = sig("pj_ready", PC // 2 + 1)
        pj_read = sig("pj_read", PC + 1, 1, 2)
        sw_ready = sig("sw_ready", 8)
        rope_done = sig("rope_done", 8)
        tok_pe = sig("tok_pe", 1)
        tok_read = sig("tok_read", 1)
        conv_done = sig("conv_done", 1)
        gz_ready = sig("gz_ready", LC)
        lam_in = sig("lam_in", 1)
        lam_exp = sig("lam_exp", 1)
        gate_tanh = sig("gate_tanh", LC, 1, 1)
        loga = sig("loga", 1)
        decay = sig("decay", 1)
        radicand = sig("radicand", 1)
        root_b = sig("root_b", 1)
        gelu_in = sig("gelu_in", 1)
        gelu_tanh = sig("gelu_tanh", 1)
        outs_ready = sig("outs_ready", 2)
        outs_done = sig("outs_done", 5, 16)
        q_ready = sig("q_ready", 1)
        dots = sig("dots", (TILES - 1) * IH)
        dots_read = sig("dots_read", (TILES - 1) * IH, 1, 2)
        s_pe = sig("s_pe", TILES * HEADS)
        s_masked = sig("s_masked", TILES * HEADS, 1, 2)
        s_exp = sig("s_exp", TILES * HEADS)
        t_pe = sig("t_pe", TILES * HEADS)
        t_read = sig("t_read", TILES * HEADS, 1, 2)
        pv_p = sig("pv_p", TILES * HEADS)
        o_read = sig("o_read", TILES, 1, 1)
        yt_pe = sig("yt_pe", TILES)
        yt_read = sig("yt_read", TILES, 1, 1)
        wb_pe = sig("wb_pe", 1)
        id_pe = sig("id_pe", 1)
        id_read = sig("id_read", NSEQ + 1, 1, 2)
        scT_pe = sig("scT_pe", 1)
        topk_done = sig("topk_done", 1)
        mT_pe = sig("mT_pe", 1)
        ks_pe = sig("ks_pe", 1)
        ks_read = sig("ks_read", NSEQ + 1, 1, 2)
        max_in = sig("max_in", 1)
        pool_max = sig("pool_max", 1)
        sub_done = sig("sub_done", 1)
        exp_s = sig("exp_s", 1)
        sums = sig("sums", 1)
        den_pe = sig("den_pe", 1)
        ysample = sig("ysample", 1)
        wo_ready = sig("wo_ready", DC // 2)
        wo_read = sig("wo_read", DC, 1, 2)
        dve_step = ctx.enter_context(nc.semaphore("dve_step"))
        eps_ready = sig("eps_ready", 0)
        cleared = sig("cleared", 0)
        passed = [ctx.enter_context(nc.semaphore(f"passed_{e}")) for e in ("sp", "pe", "pool", "dve")]
        y_out = sig("y_out", 0)

        block = ctx.enter_context(nc.Block())

        def halves(pair):
            return ps[:, 2 * pair:2 * pair + 2, 0:TH]

        def tok2(v):
            return v.rearrange("p (b t) -> p b t", b=2)

        def layer_of(ap, l):
            return ap[bass.ds(l, 1)]

        @block.sync
        def _(sp):
            sp.dma_start(cst[:, :], a["cst"]).then_inc(s_in.sem, 16)
            sp.dma_start(x[:, :, :], a["xT"]).then_inc(s_in.sem, 16)
            sp.dma_start(cT[:, :, :], a["cT"]).then_inc(s_in.sem, 16)
            sp.dma_start(pages[:, :], a["page_table"]).then_inc(s_in.sem, 16)
            sp.wait_ge(s_in.sem, 64)
            sp.wait_ge(cleared.sem, 2)
            with sp.Fori(0, DEPTH) as l:
                sp.wait_ge(vec_free.sem, vec_free.at(l, 0))
                sp.dma_start(vec[:, :], layer_of(a["vec"], l).rearrange("a p n -> (a p) n")).then_inc(vec_full.sem, 16)
                sp.dma_start(state[:, :], layer_of(a["state"], l).rearrange("a p n -> (a p) n")).then_inc(vec_full.sem, 16)
                sp.wait_ge(gate_tanh.sem, gate_tanh.at(l, 0))
                for g, name in enumerate(("lru_wa", "lru_wx")):
                    for b in range(8):
                        half = (b % 2) * HD
                        sp.dma_start(gates[half:half + HD, g, b // 2, half:half + HD],
                                     layer_of(a[name], l)[:, b].rearrange("a i j -> (a i) j")).then_inc(gate_full.sem, 16)

                def wide(use, i, src):
                    sp.wait_ge(w_free[i].sem, w_free[i].at(l, use))
                    dst = wslot[i][:, :].rearrange("p (c n) -> p c n", c=DC)
                    for c in (0, DC // 2):
                        sp.dma_start(dst[:, c:c + DC // 2, :], src[:, c:c + DC // 2, :]).then_inc(w_full[i].sem, 16)

                def rows(ap):
                    return ap.rearrange("a (c p) n -> p (a c) n", p=P)

                ada, w_in, w_out = (layer_of(a[n], l) for n in ("w_ada", "w_in", "w_out"))
                with sp.Fori(0, U_ADA) as u:
                    for i in range(2):
                        wide(K_ADA + u, i, rows(ada[:, :, bass.ds(u * (4 * P) + i * 2 * P, 2 * P)]))

                def ffn_loads(f, k0):
                    gu = layer_of(a["ffn_w_gu"], l)[:, f]
                    dn = layer_of(a["ffn_w_down"], l)[:, f]
                    with sp.Fori(0, U_GU) as u:
                        for i in range(2):
                            sp.wait_ge(w_free[i].sem, w_free[i].at(l, k0 + u))
                            col = u * (2 * P) + i * P
                            both = gu.rearrange("a (c p) (m n) -> p (a c) m n", p=P, m=2)[:, :, :, bass.ds(col, P)]
                            dst = wslot[i][:, :].rearrange("p (c m n) -> p c m n", c=DC, m=2)
                            sp.dma_start(dst[:, :, 0, :], both[:, :, 0, :]).then_inc(w_full[i].sem, 16)
                            sp.dma_start(dst[:, :, 1, :], both[:, :, 1, :]).then_inc(w_full[i].sem, 16)
                    with sp.Fori(0, DC // 2) as u:
                        for i in range(2):
                            sp.wait_ge(d_free[i].sem, d_free[i].at(l, f * (DC // 2) + u))
                            sp.dma_start(dslot[i][:, :, :], rows(dn[:, :, bass.ds(u * (2 * P) + i * P, P)]))\
                                .then_inc(d_full[i].sem, 16)

                ffn_loads(0, K_GU1)
                with sp.Fori(0, U_IN) as u:
                    for i in range(2):
                        wide(K_IN + u, i, rows(w_in[:, :, bass.ds(u * (4 * P) + i * 2 * P, 2 * P)]))
                sp.wait_ge(pj_read.sem, pj_read.at(l, 0))
                sp.dma_start(w_last[:, :, 0:LAST], rows(w_in[:, :, PC * P:IN_COLS])).then_inc(last_full.sem, 16)

                def w_out_loads(u):
                    for i in range(2):
                        wide(K_OUT + u, i, rows(w_out[:, :, (2 * u + i) * 2 * P:(2 * u + i + 1) * 2 * P]))

                hold(sp, passed[0], rope_done.sem, rope_done.at(l, 8))
                sp.wait_ge(pj_read.sem, pj_read.at(l, PC + 1))
                for name, c, n in (("kT", KK, P), ("vT", VV, P), ("kiT", KW, HD)):
                    sp.dma_start(layer_of(a[name], l).rearrange("a p t -> (a p) t"), proj[0:n, c, :])\
                        .then_inc(outs_done.sem, 16)
                sp.wait_ge(outs_ready.sem, outs_ready.at(l, 1))
                sp.dma_start(layer_of(a["convT"], l).rearrange("a p c n -> (a p) c n"), cout[:, :, :])\
                    .then_inc(outs_done.sem, 16)
                sp.wait_ge(outs_ready.sem, outs_ready.at(l, 2))
                sp.dma_start(layer_of(a["hT"], l).rearrange("a p c n -> (a p) c n"), hout[:, :, :])\
                    .then_inc(outs_done.sem, 16)

                def page_loads(tensor, width, buf, full, used, before):
                    with sp.Fori(0, NSEQ // 2) as s:
                        for i in range(2):
                            before(i, s)
                            with sp.Fori(0, PAGES) as j:
                                page = sp.value_load(pages[0:1, bass.ds(s * (2 * PAGES) + (i * PAGES) + j, 1)],
                                                     min_val=0, max_val=POOL - 1)
                                src = layer_of(tensor, l)[:, bass.ds(page, 1)].rearrange("a b p n -> (a b p) n")
                                sp.dma_start(buf[i][0:width, bass.ds(j, 1), :].rearrange("p a n -> p (a n)"), src)\
                                    .then_inc(full[i].sem, 16)

                hold(sp, passed[0], arena_free.sem, arena_free.at(l, 1))
                page_loads(a["kiT_cache"], HD, kiT, ki_full, ki_used,
                           lambda i, s: hold(sp, passed[0], ki_used[i].sem, ki_used[i].at(l, s)) )
                page_loads(a["kT_cache"], P, kpage, kp_full, kp_used,
                           lambda i, s: (hold(sp, passed[0], ki_used[i].sem, ki_used[i].at(l, 4)),
                                         hold(sp, passed[0], kp_used[i].sem, kp_used[i].at(l, s))))
                w_out_loads(0)
                page_loads(a["v_cache"], P, vpage, vp_full, vp_used,
                           lambda i, s: hold(sp, passed[0], vp_used[i].sem, vp_used[i].at(l, s)))
                for u in range(1, U_OUT):
                    w_out_loads(u)
                ffn_loads(1, K_GU2)
            sp.wait_ge(res_done.sem, res_done.at(DEPTH - 1, 3))
            sp.dma_start(a["yT"], x[:, :, :]).then_inc(y_out.sem, 16)
            sp.wait_ge(y_out.sem, 16)
            sp.wait_ge(outs_done.sem, outs_done.at(DEPTH - 1, 5))


        @block.tensor
        def _(pe):
            mm = nc.tensor.matmul

            def sums_of_squares(squares, l, k):
                for c in range(DC):
                    pe.wait_ge(squares.sem, squares.at(l, k + c + 1))
                    for b in range(2):
                        last = mm(ps[:, 6 + b, 0:TH], ones, sq[:, c, b * TH:(b + 1) * TH],
                                  start=(c == 0), stop=(c == DC - 1))
                last.then_inc(ss_ready.sem, 1)

            def product(pair, weights, moving):
                n = len(weights)
                m = weights[0].shape[-1]
                for b in range(2):
                    for kc in range(n):
                        last = mm(ps[0:m, 2 * pair + b, 0:TH], weights[kc], moving[kc][:, b * TH:(b + 1) * TH],
                                  start=(kc == 0), stop=(kc == n - 1))
                return last

            hs = [h[:, kc, :] for kc in range(DC)]

            def ffn(l, f, k0):
                pe.wait_ge(h_dve.sem, h_dve.at(l, 1 if f == 0 else 3))
                hold(pe, passed[1], h_act.sem, h_act.at(l, DC if f == 0 else 3 * DC))
                with pe.Fori(0, U_GU) as u:
                    for i in range(2):
                        w = wslot[i][:, :].rearrange("p (c m n) -> p c m n", c=DC, m=2)
                        k = u * 2 + (f * FC + i)
                        pe.wait_ge(w_full[i].sem, w_full[i].at(l, k0 + 1 + u))
                        pe.wait_ge(act_ready.sem, act_ready.at(l, k + 1 - 2))
                        product(2 * i, [w[:, kc, 0, :] for kc in range(DC)], hs)
                        product(2 * i + 1, [w[:, kc, 1, :] for kc in range(DC)], hs).then_inc(w_free[i].sem, 1)
                hold(pe, passed[1], act_ready.sem, act_ready.at(l, (f + 1) * FC))
                with pe.Fori(0, DC // 2) as u:
                    for i in range(2):
                        k = u * 2 + (f * DC + i)
                        pe.wait_ge(d_full[i].sem, d_full[i].at(l, u + (f * (DC // 2) + 1)))
                        pe.wait_ge(dn_read.sem, dn_read.at(l, k + 1 - 2))
                        product(i, [dslot[i][:, kc, :] for kc in range(FC)], [act[:, kc, :] for kc in range(FC)])\
                            .then_inc(d_free[i].sem, 1)

            for s in (*w_free, *d_free, *ki_used, *kp_used, *vp_used):
                pe.sem_inc(s.sem, s.start)
            pe.wait_ge(s_in.sem, 64)
            with pe.Fori(0, DEPTH) as l:
                with pe.Fori(0, NMOD) as g:
                    pe.wait_ge(ada_read.sem, ada_read.at(l, g))
                    for v in range(4):
                        i = v % 2
                        pe.wait_ge(w_full[i].sem, w_full[i].at(l, g * 2 + (v // 2 + 1)))
                        w = wslot[i][:, :].rearrange("p (c n) -> p c n", c=DC)
                        for m in range(2):
                            col = (2 * v + m) * NC_
                            for kc in range(DC):
                                last = mm(ps[:, 0, col:col + NC_], w[:, kc, m * P:(m + 1) * P], cT[:, kc, :],
                                          start=(kc == 0), stop=(kc == DC - 1))
                        last.then_inc(w_free[i].sem, 1)
                pe.wait_ge(ada_read.sem, ada_read.at(l, NMOD))

                sums_of_squares(sq_ready, l, 0)
                ffn(l, 0, K_GU1)
                sums_of_squares(dn_read, l, 0)
                sums_of_squares(sq_ready, l, 8)

                pe.wait_ge(h_dve.sem, h_dve.at(l, 2))
                hold(pe, passed[1], h_act.sem, h_act.at(l, 2 * DC))
                with pe.Fori(0, U_IN) as u:
                    for v in range(4):
                        i = v // 2
                        w = wslot[i][:, :].rearrange("p (c n) -> p c n", c=DC)
                        if v % 2 == 0:
                            pe.wait_ge(w_full[i].sem, w_full[i].at(l, u + (K_IN + 1)))
                        pe.wait_ge(pj_read.sem, pj_read.at(l, u * 4 + (v + 1 - 2)))
                        last = product(v % 2, [w[:, kc, (v % 2) * P:(v % 2 + 1) * P] for kc in range(DC)], hs)
                        last.then_inc((pj_ready, w_free[i])[v % 2].sem, 1)
                pe.wait_ge(last_full.sem, last_full.at(l, 1))
                pe.wait_ge(pj_read.sem, pj_read.at(l, PC + 1 - 2))
                product(0, [w_last[:, kc, :] for kc in range(DC)], hs).then_inc(pj_ready.sem, 1)

                for n, c in enumerate(ROPED):
                    pe.wait_ge(pj_read.sem, pj_read.at(l, PC + 1 if c == KW else c + 1))
                    if n >= 2:
                        pe.wait_ge(rope_done.sem, rope_done.at(l, n - 1))
                    product(2 + n % 2, [swap], [proj[:, c, :]]).then_inc(sw_ready.sem, 1)
                pe.wait_ge(pj_read.sem, pj_read.at(l, PC + 1))
                for j in range(TILES):
                    nc.tensor.transpose(ps[:, 0, j * P:(j + 1) * P], proj[:, VV, j * P:(j + 1) * P], ident)
                nc.tensor.transpose(ps[0:NS, 1, 0:P], proj[:, VV, SEQ:T], ident)
                pe.wait_ge(rope_done.sem, rope_done.at(l, len(ROPED)))
                for j in range(TILES):
                    last = nc.tensor.transpose(ps[:, 4, j * P:(j + 1) * P], proj[:, KW, j * P:(j + 1) * P], ident)
                for hd in range(IH):
                    last = mm(ps[:, 5, hd * NS:(hd + 1) * NS], sel[:, hd, :], proj[:, KW, SEQ:T], start=True, stop=True)
                last.then_inc(tok_pe.sem, 1)

                pe.wait_ge(tok_read.sem, tok_read.at(l, 1))
                pe.wait_ge(gate_full.sem, gate_full.at(l, 16))
                pe.wait_ge(conv_done.sem, conv_done.at(l, 1))
                for c in range(LC):
                    if c >= 2:
                        pe.wait_ge(gate_tanh.sem, gate_tanh.at(l, c - 1))
                    product(2 * (c % 2), [gates[:, 0, c, :]], [xc[:, c, :]])
                    last = product(2 * (c % 2) + 1, [gates[:, 1, c, :]], [xc[:, c, :]])
                    last.then_inc(gz_ready.sem, 1)
                pe.wait_ge(gate_tanh.sem, gate_tanh.at(l, LC))

                pe.wait_ge(q_ready.sem, q_ready.at(l, 1))
                head_keys = lambda half, kv, j0, j1: (proj[half * HD:(half + 1) * HD, KK, j0:j1] if half == kv
                                                      else kd[half * HD:(half + 1) * HD, kv, j0:j1])

                def scores(n):
                    i, hd = divmod(n, HEADS)
                    half = hd % 2
                    pe.wait_ge(s_masked.sem, s_masked.at(l, n + 1 - 2))
                    mm(ps[:, 4 + n % 2, 0:(i + 1) * P],
                       proj[half * HD:(half + 1) * HD, QQ + hd // 2, i * P:(i + 1) * P],
                       head_keys(half, hd // (HEADS // NKV), 0, (i + 1) * P), start=True, stop=True)\
                        .then_inc(s_pe.sem, 1)

                def index_dots(i):
                    for hd in range(IH):
                        half, k = hd % 2, (i - 1) * IH + hd
                        pe.wait_ge(dots_read.sem, dots_read.at(l, k + 1 - 2))
                        keys = proj[0:HD, KW, 0:(i + 1) * P] if half == 0 else kd[HD:P, 2, 0:(i + 1) * P]
                        mm(ps[:, hd % 2, 0:(i + 1) * P],
                           proj[half * HD:(half + 1) * HD, QI + hd // 2, i * P:(i + 1) * P], keys,
                           start=True, stop=True).then_inc(dots.sem, 1)

                scores(0)
                for i in range(TILES):
                    if i >= 1:
                        index_dots(i)
                    for hd in range(HEADS):
                        n = i * HEADS + hd
                        if n + 1 < TILES * HEADS:
                            scores(n + 1)
                        pe.wait_ge(s_exp.sem, s_exp.at(l, n + 1))
                        pe.wait_ge(t_read.sem, t_read.at(l, n + 1 - 2))
                        for j in range(i + 1):
                            last = nc.tensor.transpose(ps[:, 6 + n % 2, j * P:(j + 1) * P],
                                                       prob[n % 2][:, j * P:(j + 1) * P], ident)
                        last.then_inc(t_pe.sem, 1)
                        pe.wait_ge(t_read.sem, t_read.at(l, n + 1))
                        if hd == 0:
                            pe.wait_ge(o_read.sem, o_read.at(l, i))
                        kv = hd // (HEADS // NKV)
                        for j in range(i + 1):
                            last = mm(ps[:, 2, hd * HD:(hd + 1) * HD], probT[n % 2][:, j * P:(j + 1) * P],
                                      vtok[:, j, kv * HD:(kv + 1) * HD], start=(j == 0), stop=(j == i))
                        last.then_inc(pv_p.sem, 1)
                    pe.wait_ge(o_read.sem, o_read.at(l, i + 1))
                    pe.wait_ge(yt_read.sem, yt_read.at(l, i))
                    for c in range(4):
                        last = nc.tensor.transpose(ps[:, 3, c * P:(c + 1) * P], ytok[:, c * P:(c + 1) * P], ident)
                    last.then_inc(yt_pe.sem, 1)
                hold(pe, passed[1], yt_read.sem, yt_read.at(l, TILES))

                with pe.Fori(0, NSEQ // 2) as s:
                    for i in range(2):
                        pe.wait_ge(ki_full[i].sem, ki_full[i].at(l, s * PAGES + PAGES))
                        pe.wait_ge(id_read.sem, id_read.at(l, s * 2 + (i + 1 - 2)))
                        for j in range(PAGES):
                            last = mm(ps[:, i, j * 16:(j + 1) * 16], kiT[i][0:HD, j, :],
                                      qiS[0:HD, bass.ds(s * 2 + i, 1), :].rearrange("p a c -> p (a c)"),
                                      start=True, stop=True)
                        last.then_inc(ki_used[i].sem, 1)
                for s in range(NSEQ):
                    last = mm(ps[0:NS, 2, s * 16:(s + 1) * 16], proj[0:HD, KW, SEQ:T], qiS[0:HD, s, :],
                              start=True, stop=True)
                last.then_inc(id_pe.sem, 1)
                pe.wait_ge(id_read.sem, id_read.at(l, NSEQ + 1))
                for j in range(PAGES):
                    nc.tensor.transpose(ps[0:NS, 3 + j // 4, (j % 4) * P:(j % 4 + 1) * P], scT[:, j, :], ident)
                nc.tensor.transpose(ps[0:NS, 7, 0:NS], scT[0:NS, PAGES, :], ident[0:NS, 0:NS])\
                    .then_inc(scT_pe.sem, 1)
                hold(pe, passed[1], topk_done.sem, topk_done.at(l, 1))
                for j in range(PAGES):
                    nc.tensor.transpose(ps[:, 0, j * NS:(j + 1) * NS], wkS[:, j * P:(j + 1) * P], ident[0:NS, 0:NS])
                nc.tensor.transpose(ps[0:NS, 1, 0:NS], wkS[:, PAGES * P:PAGES * P + NS], ident[0:NS, 0:NS])\
                    .then_inc(mT_pe.sem, 1)
                with pe.Fori(0, NSEQ // 2) as s:
                    for i in range(2):
                        pe.wait_ge(kp_full[i].sem, kp_full[i].at(l, s * PAGES + PAGES))
                        pe.wait_ge(ks_read.sem, ks_read.at(l, s * 2 + (i + 1 - 2)))
                        for j in range(PAGES):
                            last = mm(ps[:, 2 + i, j * 32:(j + 1) * 32], kpage[i][:, j, :],
                                      qS[:, bass.ds(s * 2 + i, 1), :].rearrange("p a c -> p (a c)"),
                                      start=True, stop=True)
                        last.then_inc(kp_used[i].sem, 1)
                for s in range(NSEQ):
                    last = mm(ps[0:NS, 4, s * 32:(s + 1) * 32], proj[:, KK, SEQ:T], qS[:, s, :], start=True, stop=True)
                last.then_inc(ks_pe.sem, 1)
                pe.wait_ge(sums.sem, sums.at(l, 1))
                mm(ps[:, 5, 0:NSEQ * 32], ones, mx, start=True, stop=True).then_inc(den_pe.sem, 1)
                with pe.Fori(0, NSEQ // 2) as s:
                    for i in range(2):
                        pe.wait_ge(vp_full[i].sem, vp_full[i].at(l, s * PAGES + PAGES))
                        out = ps[:, 6, bass.ds(s * 64 + i * 32, 32)]
                        for j in range(PAGES):
                            last = mm(out, vpage[i][:, j, :],
                                      sT3[:, bass.ds(s * 2 + i, 1), j, :].rearrange("p a c -> p (a c)"),
                                      start=(j == 0), stop=False)
                        mm(out, vtok[0:NS, TILES, :],
                           sT3[0:NS, bass.ds(s * 2 + i, 1), PAGES, :].rearrange("p a c -> p (a c)"),
                           start=False, stop=True).then_inc(vp_used[i].sem, 1)

                hold(pe, passed[1], ysample.sem, ysample.at(l, 1))
                with pe.Fori(0, U_OUT) as u:
                    for v in range(4):
                        i = v // 2
                        w = wslot[i][:, :].rearrange("p (c n) -> p c n", c=DC)
                        if v % 2 == 0:
                            pe.wait_ge(w_full[i].sem, w_full[i].at(l, u + (K_OUT + 1)))
                        pe.wait_ge(wo_read.sem, wo_read.at(l, u * 4 + (v + 1 - 2)))
                        last = product(v % 2, [w[:, kc, (v % 2) * P:(v % 2 + 1) * P] for kc in range(DC)],
                                       [y[:, kc, :] for kc in range(DC)])
                        last.then_inc((wo_ready, w_free[i])[v % 2].sem, 1)
                sums_of_squares(wo_read, l, 0)
                sums_of_squares(sq_ready, l, 16)
                ffn(l, 1, K_GU2)
                sums_of_squares(dn_read, l, 8)

        @block.scalar
        def _(sc):
            act_fn = nc.scalar.activation

            def squares_of_x(l, k):
                for c in range(DC):
                    act_fn(sq[:, c, :], x[:, c, :], ACT.Square).then_inc(sq_ready.sem, 1)

            def root(l, k):
                sc.wait_ge(ss_ready.sem, ss_ready.at(l, k + 1))
                act_fn(tok2(rinv[:, :]), halves(3), ACT.Sqrt, bias=eps[:, 0:1], scale=1.0 / D).then_inc(root_ready.sem, 1)

            def gain_and_shift(l, k, shift):
                for c in range(DC):
                    sc.wait_ge(xn_ready.sem, xn_ready.at(l, k * DC + c + 1))
                    act_fn(h[:, c, 0:SEQ], h[:, c, 0:SEQ], ACT.Identity, bias=mod[:, shift * DC + c, 0:1],
                           scale=gain[:, c, 0:1]).then_inc(h_act.sem, 1)

            def take(pair, c, read):
                act_fn(tok2(h[:, c, :]), halves(pair), ACT.Copy)
                act_fn(tok2(sq[:, c, :]), halves(pair), ACT.Square).then_inc(read.sem, 1)

            def ffn(l, f, k0):
                with sc.Fori(0, U_GU) as u:
                    for i in range(2):
                        k = u * 2 + (f * FC + i)
                        sc.wait_ge(w_free[i].sem, w_free[i].at(l, u + (k0 + 1)))
                        sc.wait_ge(act_ready.sem, act_ready.at(l, k + 1 - 2))
                        act_fn(tok2(tsil[:, i, :]), halves(2 * i), ACT.Tanh, scale=0.5).then_inc(tanh_ready.sem, 1)
                for m in range(DC):
                    i = m % 2
                    sc.wait_ge(d_free[i].sem, d_free[i].at(l, f * (DC // 2) + m // 2 + 1))
                    take(i, m, dn_read)

            for s in (dn_read, pj_read, wo_read, t_read, yt_read, gate_tanh):
                sc.sem_inc(s.sem, s.start)
            sc.wait_ge(s_in.sem, 64)
            sc.wait_ge(eps_ready.sem, 1)
            with sc.Fori(0, DEPTH) as l:
                sc.wait_ge(res_done.sem, res_done.at(l, 0))
                squares_of_x(l, 0)
                root(l, 0)
                gain_and_shift(l, 0, 0)
                ffn(l, 0, K_GU1)
                root(l, 1)
                sc.wait_ge(res_done.sem, res_done.at(l, 1))
                squares_of_x(l, 2)
                root(l, 2)
                gain_and_shift(l, 1, 3)

                with sc.Fori(0, U_IN) as u:
                    for v in range(4):
                        if v % 2 == 0:
                            sc.wait_ge(pj_ready.sem, pj_ready.at(l, u * 2 + (v // 2 + 1)))
                        else:
                            sc.wait_ge(w_free[v // 2].sem, w_free[v // 2].at(l, u + (K_IN + 1)))
                        dst = proj[:, bass.ds(u * 4 + v, 1), :].rearrange("p a (b t) -> p (a b) t", b=2)
                        act_fn(dst, halves(v % 2), ACT.Copy).then_inc(pj_read.sem, 1)
                sc.wait_ge(pj_ready.sem, pj_ready.at(l, PC // 2 + 1))
                act_fn(tok2(proj[:, KW, :]), halves(0), ACT.Copy).then_inc(pj_read.sem, 1)

                sc.wait_ge(lam_in.sem, lam_in.at(l, 1))
                act_fn(small[:, 2, :], small[:, 1, :], ACT.Exp, scale=-1.0).then_inc(lam_exp.sem, 1)
                for c in range(LC):
                    sc.wait_ge(gz_ready.sem, gz_ready.at(l, c + 1))
                    act_fn(tok2(ta[:, c, :]), halves(2 * (c % 2)), ACT.Tanh, bias=small[:, 10, c:c + 1], scale=0.5)
                    act_fn(tok2(tb[:, c, :]), halves(2 * (c % 2) + 1), ACT.Tanh, bias=small[:, 11, c:c + 1], scale=0.5)\
                        .then_inc(gate_tanh.sem, 1)
                sc.wait_ge(loga.sem, loga.at(l, 1))
                act_fn(ta[:, :, :], tc[:, :, :], ACT.Exp)
                act_fn(th[:, :, :], tc[:, :, :], ACT.Tanh, scale=-1.0).then_inc(decay.sem, 1)
                sc.wait_ge(radicand.sem, radicand.at(l, 1))
                act_fn(th[:, :, :], th[:, :, :], ACT.Sqrt).then_inc(root_b.sem, 1)
                sc.wait_ge(gelu_in.sem, gelu_in.at(l, 1))
                act_fn(tc[:, :, :], tc[:, :, :], ACT.Tanh).then_inc(gelu_tanh.sem, 1)

                def transposed(n):
                    i = n // HEADS
                    sc.wait_ge(t_pe.sem, t_pe.at(l, n + 1))
                    if n >= 2:
                        sc.wait_ge(pv_p.sem, pv_p.at(l, n - 1))
                    act_fn(probT[n % 2][:, 0:(i + 1) * P], ps[:, 6 + n % 2, 0:(i + 1) * P], ACT.Copy)\
                        .then_inc(t_read.sem, 1)

                for n in range(TILES * HEADS):
                    i, hd = divmod(n, HEADS)
                    sc.wait_ge(s_masked.sem, s_masked.at(l, n + 1))
                    act_fn(prob[n % 2][:, 0:(i + 1) * P], prob[n % 2][:, 0:(i + 1) * P], ACT.Exp,
                           bias=nmax[:, hd:hd + 1], scale=HD ** -0.5, accum_out=den[:, hd:hd + 1])\
                        .then_inc(s_exp.sem, 1)
                    transposed(n)
                    if hd == HEADS - 1:
                        sc.wait_ge(yt_pe.sem, yt_pe.at(l, i + 1))
                        act_fn(y[:, LC:DC, i * P:(i + 1) * P], ps[:, 3, :].rearrange("p (c t) -> p c t", c=4), ACT.Copy)\
                            .then_inc(yt_read.sem, 1)

                sc.wait_ge(sub_done.sem, sub_done.at(l, 1))
                act_fn(sT, sT, ACT.Exp, scale=HD ** -0.5).then_inc(exp_s.sem, 1)

                with sc.Fori(0, U_OUT) as u:
                    for v in range(4):
                        if v % 2 == 0:
                            sc.wait_ge(wo_ready.sem, wo_ready.at(l, u * 2 + (v // 2 + 1)))
                        else:
                            sc.wait_ge(w_free[v // 2].sem, w_free[v // 2].at(l, u + (K_OUT + 1)))
                        for dst, fn in ((h, ACT.Copy), (sq, ACT.Square)):
                            last = act_fn(dst[:, bass.ds(u * 4 + v, 1), :].rearrange("p a (b t) -> p (a b) t", b=2),
                                          halves(v % 2), fn)
                        last.then_inc(wo_read.sem, 1)
                root(l, 3)
                sc.wait_ge(res_done.sem, res_done.at(l, 2))
                squares_of_x(l, 4)
                root(l, 4)
                gain_and_shift(l, 2, 6)
                ffn(l, 1, K_GU2)
                root(l, 5)
                sc.wait_ge(outs_done.sem, outs_done.at(l, 5))

        @block.gpsimd
        def _(pool):
            with pool.Fori(0, DEPTH) as l:
                hold(pool, passed[2], max_in.sem, max_in.at(l, 1))
                nc.gpsimd.partition_all_reduce(mxa, mx, P, RMAX).then_inc(pool_max.sem, 1)

        @block.vector
        def _(dve):
            v = nc.vector
            v.memset(eps[:, :], EPS).then_inc(eps_ready.sem, 1)
            v.memset(gates[:, :, :, :], 0.0).then_inc(cleared.sem, 1)
            v.memset(w_last[:, :, :], 0.0).then_inc(cleared.sem, 1)
            for s in (vec_free, ada_read, act_ready, dots_read, s_masked, o_read, res_done, id_read, ks_read):
                dve.sem_inc(s.sem, s.start)
            dve.wait_ge(s_in.sem, 64)
            with dve.Fori(0, DEPTH) as l:
                st = Steps(dve, dve_step, DVE_STEPS, l, passed[3])

                def steps_of(ap):
                    return ap.rearrange("p c (s t) -> p c s t", t=STEPS)

                def each_step(m):
                    return m[:, :, 1:NC_].unsqueeze(3).to_broadcast([P, DC, NSEQ, STEPS])

                def norm_g(k):
                    return vec[:, V_G + k * DC:V_G + (k + 1) * DC].unsqueeze(2).to_broadcast([P, DC, NC_])

                def pre_norm(k, r, scale, shift):
                    st.link(v.scalar_tensor_tensor(gain[:, :, :], mod[:, scale * DC:(scale + 1) * DC, :], 1.0,
                                                   norm_g(r), ALU.add, ALU.mult))
                    dve.wait_ge(root_ready.sem, root_ready.at(l, r + 1))
                    st.link(v.reciprocal(rinv[:, :], rinv[:, :]))
                    for c in range(DC):
                        v.tensor_tensor(h[:, c, :], x[:, c, :], rinv[:, :], ALU.mult).then_inc(xn_ready.sem, 1)
                    dve.wait_ge(xn_ready.sem, xn_ready.at(l, (k + 1) * DC))
                    hn = steps_of(h[:, :, SEQ:T])
                    st.link(v.tensor_tensor(hn, hn, each_step(gain), ALU.mult))
                    v.tensor_tensor(hn, hn, each_step(mod[:, shift * DC:(shift + 1) * DC, :]), ALU.add)\
                        .then_inc(h_dve.sem, 1)

                def residual(k, r, gate, factor):
                    dve.wait_ge(h_act.sem, h_act.at(l, DC * (1, 2, 3)[k]))
                    st.link(v.scalar_tensor_tensor(gain[:, :, :], mod[:, gate * DC:(gate + 1) * DC, :], factor,
                                                   norm_g(r), ALU.mult, ALU.mult))
                    dve.wait_ge(root_ready.sem, root_ready.at(l, r + 1))
                    st.link(v.reciprocal(rinv[:, :], rinv[:, :]))
                    st.link(v.tensor_tensor(h[:, :, :], h[:, :, :], rinv[:, :].unsqueeze(1).to_broadcast([P, DC, T]),
                                            ALU.mult))
                    hn, xs = steps_of(h[:, :, SEQ:T]), steps_of(x[:, :, SEQ:T])
                    st.link(v.tensor_tensor(hn, hn, each_step(gain), ALU.mult))
                    v.tensor_tensor(xs, xs, hn, ALU.add)
                    for c in range(DC):
                        last = v.scalar_tensor_tensor(x[:, c, 0:SEQ], h[:, c, 0:SEQ], gain[:, c, 0:1], x[:, c, 0:SEQ],
                                                      ALU.mult, ALU.add)
                    last.then_inc(res_done.sem, 1)
                    dve.wait_ge(res_done.sem, res_done.at(l, k + 1))

                def swiglu(f):
                    with st.loop(U_GU, 2) as u:
                        for i in range(2):
                            dve.wait_ge(tanh_ready.sem, tanh_ready.at(l, u * 2 + (f * FC + i + 1)))
                            st.link(v.scalar_tensor_tensor(tok2(tsil[:, i, :]), tok2(tsil[:, i, :]), 1.0, halves(2 * i),
                                                           ALU.add, ALU.mult))
                            v.scalar_tensor_tensor(
                                act[:, bass.ds(u * 2 + i, 1), :].rearrange("p a (b t) -> p (a b) t", b=2),
                                tok2(tsil[:, i, :]), 0.5, halves(2 * i + 1), ALU.mult, ALU.mult)\
                                .then_inc(act_ready.sem, 1)

                def take_top(values, rounds):
                    with st.loop(rounds, 2):
                        st.link_hold(v.max(top8[0:values.shape[0], :], values))
                        st.link_hold(v.match_replace(values, top8[0:values.shape[0], :], values, TAKEN))

                hold(dve, passed[3], vec_full.sem, vec_full.at(l, 2))
                with dve.Fori(0, NMOD) as g:
                    dve.wait_ge(w_free[1].sem, w_free[1].at(l, g * 2 + 2))
                    v.tensor_tensor(mod[:, bass.ds(g * DC, DC), :],
                                    ps[:, 0, 0:DC * NC_].rearrange("p (m c) -> p m c", c=NC_),
                                    vec[:, bass.ds(g * DC + V_BADA, DC)].unsqueeze(2).to_broadcast([P, DC, NC_]),
                                    ALU.add).then_inc(ada_read.sem, 1)
                dve.wait_ge(ada_read.sem, ada_read.at(l, NMOD))

                pre_norm(0, 0, 1, 0)
                swiglu(0)
                residual(0, 1, 2, 0.5)
                pre_norm(1, 2, 4, 3)

                lam = vec[:, V_LAM:V_LAM + LC]
                neg, z, z2, poly = small[:, 0, :], small[:, 3, :], small[:, 4, :], small[:, 5, :]
                st.link(v.tensor_scalar(neg, lam, -1.0, None, ALU.mult))
                v.tensor_tensor(small[:, 1, :], neg, lam, ALU.max).then_inc(lam_in.sem, 1)
                v.tensor_scalar(small[:, 10, :], vec[:, V_BA:V_BA + LC], 0.5, None, ALU.mult)
                v.tensor_scalar(small[:, 11, :], vec[:, V_BX:V_BX + LC], 0.5, None, ALU.mult)
                dve.wait_ge(lam_exp.sem, lam_exp.at(l, 1))
                st.link(v.tensor_scalar(z2, small[:, 2, :], 2.0, None, ALU.add))
                st.link(v.reciprocal(z2, z2))
                st.link(v.tensor_tensor(z, small[:, 2, :], z2, ALU.mult))
                st.link(v.tensor_tensor(z2, z, z, ALU.mult))
                st.link(v.tensor_scalar(poly, z2, 1.0 / 19, 1.0 / 17, ALU.mult, ALU.add))
                for n in (15, 13, 11, 9, 7, 5, 3, 1):
                    st.link(v.tensor_tensor(poly, poly, z2, ALU.mult))
                    st.link(v.tensor_scalar(poly, poly, 1.0 / n, None, ALU.add))
                st.link(v.tensor_tensor(poly, poly, z, ALU.mult))
                st.link(v.tensor_scalar(neg, neg, 0.0, None, ALU.max))
                st.link(v.scalar_tensor_tensor(poly, poly, 2.0, neg, ALU.mult, ALU.add))
                st.link(v.tensor_scalar(small[:, 6, :], poly, -0.5 * 8.0, None, ALU.mult))

                tmp = y[:, DC - 1, :]
                for n, c in enumerate(ROPED):
                    rows = HD if c == KW else P
                    dve.wait_ge(sw_ready.sem, sw_ready.at(l, n + 1))
                    st.link(v.tensor_tensor(tok2(tmp[0:rows, :]), ps[0:rows, 4 + 2 * (n % 2):6 + 2 * (n % 2), 0:TH],
                                            tok2(sinT[0:rows, :]), ALU.mult))
                    st.link(v.tensor_tensor(proj[0:rows, c, :], proj[0:rows, c, :], cosT[0:rows, :], ALU.mult))
                    v.tensor_tensor(proj[0:rows, c, :], proj[0:rows, c, :], tmp[0:rows, :], ALU.add)\
                        .then_inc(rope_done.sem, 1)
                    dve.wait_ge(rope_done.sem, rope_done.at(l, n + 1))

                dve.wait_ge(tok_pe.sem, tok_pe.at(l, 1))
                v.tensor_copy(vtok[:, 0:TILES, :], ps[:, 0, :].rearrange("p (j d) -> p j d", d=P))
                v.tensor_copy(vtok[0:NS, TILES, :], ps[0:NS, 1, 0:P])
                w_scale = HD ** -0.5 * IH ** -0.5
                v.tensor_scalar(wtok, ps[:, 4, :].rearrange("p (j d) -> p j d", d=P)[:, :, HD:HD + IH], w_scale, None,
                                ALU.mult)
                for hd in range(IH):
                    last = v.tensor_scalar(cbuf[:, :, hd * STEPS:(hd + 1) * STEPS],
                                           ps[:, 5, hd * NS:(hd + 1) * NS].rearrange("p (s t) -> p s t", t=STEPS),
                                           w_scale, None, ALU.mult)
                last.then_inc(tok_read.sem, 1)

                xs = xp[:, :, 3 + SEQ:XPW].rearrange("p c (s w) -> p c s w", w=SW)
                xcs = xc[:, :, SEQ:T].rearrange("p c (s t) -> p c s t", t=STEPS)
                v.memset(xp[:, :, 0:3], 0.0)
                v.tensor_copy(xp[:, :, 3:3 + SEQ], proj[:, XL:XL + LC, 0:SEQ])
                v.tensor_copy(xs[:, :, :, 3:SW], steps_of(proj[:, XL:XL + LC, SEQ:T]))
                st.link(v.tensor_copy(xs[:, :, :, 0:3],
                                      state[:, ST_C:ST_ALL].rearrange("p (c s w) -> p c s w", c=LC, w=3)))
                v.tensor_copy(cout[:, :, 0:3], xp[:, :, SEQ:SEQ + 3])
                v.tensor_copy(cout[:, :, 3:3 * NC_].rearrange("p c (s w) -> p c s w", w=3), xs[:, :, :, STEPS:SW])\
                    .then_inc(outs_ready.sem, 1)
                for j in range(CONV):
                    for c in range(LC):
                        tap = vec[:, V_CW + j * LC + c:V_CW + j * LC + c + 1]
                        for dst, src in ((xc[:, c, 0:SEQ], xp[:, c, j:j + SEQ]), (xcs[:, c], xs[:, c, :, j:j + STEPS])):
                            if j == 0:
                                last = v.tensor_scalar(dst, src, tap, vec[:, V_CB + c:V_CB + c + 1], ALU.mult, ALU.add)
                            else:
                                last = v.scalar_tensor_tensor(dst, src, tap, dst, ALU.mult, ALU.add)
                    if j < CONV - 1:
                        st.link(last)
                last.then_inc(conv_done.sem, 1)

                dve.wait_ge(gate_tanh.sem, gate_tanh.at(l, LC))
                for c in range(LC):
                    last = v.tensor_scalar(tc[:, c, :], ta[:, c, :], 1.0, small[:, 6, c:c + 1], ALU.add, ALU.mult)
                last.then_inc(loga.sem, 1)
                st.link(v.scalar_tensor_tensor(tb, tb, 1.0, xc, ALU.add, ALU.mult))
                dve.wait_ge(decay.sem, decay.at(l, 1))
                st.link(v.tensor_tensor(tc, ta, ta, ALU.mult))
                v.scalar_tensor_tensor(th, tc, 1.0, th, ALU.add, ALU.mult).then_inc(radicand.sem, 1)
                gl = proj[:, GL:GL + LC, :]
                dve.wait_ge(radicand.sem, radicand.at(l, 1))
                st.link(v.tensor_tensor(tc, gl, gl, ALU.mult))
                st.link(v.tensor_scalar(tc, tc, GELU_C * 0.044715, GELU_C, ALU.mult, ALU.add))
                v.tensor_tensor(tc, tc, gl, ALU.mult).then_inc(gelu_in.sem, 1)
                dve.wait_ge(root_b.sem, root_b.at(l, 1))
                st.link(v.scalar_tensor_tensor(tb, tb, 0.5, th, ALU.mult, ALU.mult))
                for c in range(LC):
                    v.tensor_tensor_scan(xc[:, c, 0:SEQ], ta[:, c, 0:SEQ], tb[:, c, 0:SEQ], 0.0, ALU.mult, ALU.add)
                tas, tbs = steps_of(ta[:, :, SEQ:T]), steps_of(tb[:, :, SEQ:T])
                before = state[:, ST_H:ST_H + LC * NSEQ].rearrange("p (c s) -> p c s", c=LC)
                for t in range(STEPS):
                    st.link(v.tensor_tensor(xcs[:, :, :, t], tas[:, :, :, t], before, ALU.mult))
                    st.link(v.tensor_tensor(xcs[:, :, :, t], xcs[:, :, :, t], tbs[:, :, :, t], ALU.add))
                    before = xcs[:, :, :, t]
                v.tensor_copy(hout[:, :, 0:1], xc[:, :, SEQ - 1:SEQ])
                v.tensor_copy(hout[:, :, 1:NC_], xcs[:, :, :, STEPS - 1]).then_inc(outs_ready.sem, 1)
                dve.wait_ge(gelu_tanh.sem, gelu_tanh.at(l, 1))
                st.link(v.scalar_tensor_tensor(tc, tc, 1.0, gl, ALU.add, ALU.mult))
                v.scalar_tensor_tensor(y[:, 0:LC, :], tc, 0.5, xc, ALU.mult, ALU.mult).then_inc(arena_free.sem, 1)
                dve.wait_ge(arena_free.sem, arena_free.at(l, 1))

                v.tensor_copy(kd[HD:P, 0, :], proj[0:HD, KK, 0:SEQ])
                v.tensor_copy(kd[0:HD, 1, :], proj[HD:P, KK, 0:SEQ])
                v.tensor_copy(kd[HD:P, 2, :], proj[0:HD, KW, 0:SEQ])
                for hd in range(IH):
                    half = hd % 2
                    v.tensor_copy(qiS[0:HD, :, hd * STEPS:(hd + 1) * STEPS],
                                  proj[half * HD:(half + 1) * HD, QI + hd // 2, SEQ:T].rearrange("p (s t) -> p s t", t=STEPS))
                st.link(v.memset(qS, 0.0))
                for hd in range(HEADS):
                    half, kv = hd % 2, hd // (HEADS // NKV)
                    v.tensor_copy(qS[kv * HD:(kv + 1) * HD, :, hd * STEPS:(hd + 1) * STEPS],
                                  proj[half * HD:(half + 1) * HD, QQ + hd // 2, SEQ:T].rearrange("p (s t) -> p s t", t=STEPS))
                v.tensor_copy(bias_p[:, 0, 0:P], tri).then_inc(q_ready.sem, 1)
                dve.wait_ge(q_ready.sem, q_ready.at(l, 1))

                for i in range(TILES):
                    span = (i + 1) * P
                    if i >= 1:
                        dve.wait_ge(yt_pe.sem, yt_pe.at(l, i))
                        for hd in range(IH):
                            k = (i - 1) * IH + hd
                            dve.wait_ge(dots.sem, dots.at(l, k + 1))
                            dst = (score if hd == 0 else work)[:, 0:span]
                            v.tensor_scalar(dst, ps[:, hd % 2, 0:span], 0.0, wtok[:, i, hd:hd + 1], ALU.max, ALU.mult)\
                                .then_inc(dots_read.sem, 1)
                            dve.wait_ge(dots_read.sem, dots_read.at(l, k + 1))
                            if hd:
                                st.link(v.tensor_tensor(score[:, 0:span], score[:, 0:span], work[:, 0:span], ALU.add))
                        st.link_hold(v.tensor_tensor(score[:, i * P:span], score[:, i * P:span], tri, ALU.add))
                        take_top(score[:, 0:span], SEL_P // 8)
                        st.link(v.tensor_scalar(bias_p[:, i, 0:span], score[:, 0:span], 0.5 * TAKEN, NEG, ALU.is_gt,
                                                ALU.mult))
                    for hd in range(HEADS):
                        n = i * HEADS + hd
                        dve.wait_ge(s_pe.sem, s_pe.at(l, n + 1))
                        if n >= 2:
                            dve.wait_ge(t_pe.sem, t_pe.at(l, n - 1))
                        st.link(v.tensor_tensor(prob[n % 2][:, 0:span], ps[:, 4 + n % 2, 0:span], bias_p[:, i, 0:span],
                                                ALU.add))
                        st.link(v.tensor_reduce(nmax[:, hd:hd + 1], prob[n % 2][:, 0:span], AX.X, ALU.max))
                        v.tensor_scalar(nmax[:, hd:hd + 1], nmax[:, hd:hd + 1], -(HD ** -0.5), None, ALU.mult)\
                            .then_inc(s_masked.sem, 1)
                    dve.wait_ge(pv_p.sem, pv_p.at(l, (i + 1) * HEADS))
                    st.link(v.reciprocal(den[:, :], den[:, :]))
                    v.tensor_tensor(ytok.rearrange("p (h d) -> p h d", d=HD), ps[:, 2, :].rearrange("p (h d) -> p h d", d=HD),
                                    den.unsqueeze(2).to_broadcast([P, HEADS, HD]), ALU.mult).then_inc(o_read.sem, 1)
                hold(dve, passed[3], yt_pe.sem, yt_pe.at(l, TILES))

                with st.loop(NSEQ // 2, 2) as s:
                    for i in range(2):
                        dve.wait_ge(ki_used[i].sem, ki_used[i].at(l, s + 1))
                        c16 = cbuf[:, bass.ds(s * 2 + i, 1), :].to_broadcast([P, PAGES, 16])
                        v.scalar_tensor_tensor(relu, ps[:, i, 0:PAGES * 16].rearrange("p (j c) -> p j c", c=16), 0.0,
                                               c16, ALU.max, ALU.mult).then_inc(id_read.sem, 1)
                        dve.wait_ge(id_read.sem, id_read.at(l, s * 2 + (i + 1)))
                        st.link(v.tensor_reduce(scT[:, 0:PAGES, bass.ds(s * (2 * STEPS) + i * STEPS, STEPS)],
                                                relu.rearrange("p j (h t) -> p j t h", t=STEPS), AX.X, ALU.add))
                dve.wait_ge(id_pe.sem, id_pe.at(l, 1))
                st.link(v.scalar_tensor_tensor(relu[0:NS, 0:NSEQ, :],
                                               ps[0:NS, 2, 0:NSEQ * 16].rearrange("p (s c) -> p s c", c=16), 0.0,
                                               cbuf[0:NS, :, :], ALU.max, ALU.mult))
                v.tensor_reduce(scT[0:NS, PAGES, :].rearrange("p (s t) -> p s t", t=STEPS),
                                relu[0:NS, 0:NSEQ, :].rearrange("p s (h t) -> p s t h", t=STEPS), AX.X, ALU.add)\
                    .then_inc(id_read.sem, 1)
                dve.wait_ge(scT_pe.sem, scT_pe.at(l, 1))
                v.tensor_copy(scS[:, 0:PAGES * P].rearrange("p (b k) -> p b k", b=4), ps[0:NS, 3:7, :])
                st.link_hold(v.tensor_tensor(scS[:, PAGES * P:PAGES * P + NS], ps[0:NS, 7, 0:NS], mask_new, ALU.add))
                take_top(scS, SEL_S // 8)
                v.tensor_scalar(wkS, scS, 0.5 * TAKEN, NEG, ALU.is_gt, ALU.mult).then_inc(topk_done.sem, 1)
                dve.wait_ge(mT_pe.sem, mT_pe.at(l, 1))
                v.tensor_copy(maskT[:, 0:PAGES, :], ps[:, 0, :].rearrange("p (j c) -> p j c", c=NS))
                v.tensor_copy(maskT[0:NS, PAGES, :], ps[0:NS, 1, 0:NS])
                st.link_hold(v.memset(sT3[:, :, PAGES, :], NEG))
                with dve.Fori(0, NSEQ // 2) as s:
                    for i in range(2):
                        dve.wait_ge(kp_used[i].sem, kp_used[i].at(l, s + 1))
                        m4 = maskT[:, 0:PAGES, bass.ds(s * (2 * STEPS) + i * STEPS, STEPS)].unsqueeze(2)\
                            .to_broadcast([P, PAGES, HEADS, STEPS])
                        dst = sT3[:, bass.ds(s * 2 + i, 1), 0:PAGES, :].rearrange("p a j (h t) -> p (a j) h t", t=STEPS)
                        v.tensor_tensor(dst, ps[:, 2 + i, :].rearrange("p (j h t) -> p j h t", j=PAGES, t=STEPS), m4,
                                        ALU.add).then_inc(ks_read.sem, 1)
                dve.wait_ge(ks_pe.sem, ks_pe.at(l, 1))
                v.tensor_tensor(sT3[0:NS, :, PAGES, :].rearrange("p s (h t) -> p s h t", t=STEPS),
                                ps[0:NS, 4, 0:NSEQ * 32].rearrange("p (s h t) -> p s h t", s=NSEQ, t=STEPS),
                                maskT[0:NS, PAGES, :].rearrange("p (s t) -> p s t", t=STEPS).unsqueeze(2)
                                .to_broadcast([NS, NSEQ, HEADS, STEPS]), ALU.add).then_inc(ks_read.sem, 1)
                dve.wait_ge(ks_read.sem, ks_read.at(l, NSEQ + 1))
                mx3, mxa3 = (m.rearrange("p (s c) -> p s c", s=NSEQ) for m in (mx, mxa))
                v.tensor_reduce(mx3, sT3.rearrange("p s j c -> p s c j"), AX.X, ALU.max).then_inc(max_in.sem, 1)
                dve.wait_ge(pool_max.sem, pool_max.at(l, 1))
                v.tensor_tensor(sT3, sT3, mxa3.unsqueeze(2).to_broadcast([P, NSEQ, NB, 32]), ALU.subtract)\
                    .then_inc(sub_done.sem, 1)
                dve.wait_ge(exp_s.sem, exp_s.at(l, 1))
                v.tensor_reduce(mx3, sT3.rearrange("p s j c -> p s c j"), AX.X, ALU.add).then_inc(sums.sem, 1)
                dve.wait_ge(den_pe.sem, den_pe.at(l, 1))
                st.link(v.reciprocal(rden, ps[:, 5, 0:NSEQ * 32]))
                for i in range(2):
                    dve.wait_ge(vp_used[i].sem, vp_used[i].at(l, NSEQ // 2))
                for hd in range(HEADS):
                    half, kv = hd % 2, hd // (HEADS // NKV)
                    src = slice(kv * HD, (kv + 1) * HD)
                    last = v.tensor_tensor(
                        y[half * HD:(half + 1) * HD, LC + hd // 2, SEQ:T].rearrange("p (s t) -> p s t", t=STEPS),
                        ps[src, 6, 0:NSEQ * 32].rearrange("p (s c) -> p s c", s=NSEQ)[:, :, hd * STEPS:(hd + 1) * STEPS],
                        rden[src, :].rearrange("p (s c) -> p s c", s=NSEQ)[:, :, hd * STEPS:(hd + 1) * STEPS], ALU.mult)
                last.then_inc(ysample.sem, 1)

                residual(1, 3, 5, 1.0)
                pre_norm(2, 4, 7, 6)
                swiglu(1)
                residual(2, 5, 8, 0.5)
                dve.sem_inc(vec_free.sem, 1)
                dve.wait_ge(outs_done.sem, outs_done.at(l, 5))
                assert st.n == DVE_STEPS, st.n


def rope_tables():
    half = HD // 8
    freqs = np.float32(500000.0) ** (-(np.arange(half, dtype=np.float32) / np.float32(half)))
    pos = np.concatenate([np.arange(SEQ), np.tile(PAGES * PAGE + np.arange(STEPS), NSEQ)]).astype(np.float32)
    ang = freqs.astype(np.float32)[:, None] * pos[None, :]
    cos, sin = np.ones((HD, T), np.float32), np.zeros((HD, T), np.float32)
    cos[0:half] = cos[half:2 * half] = np.cos(ang)
    sin[0:half], sin[half:2 * half] = -np.sin(ang), np.sin(ang)
    return np.tile(cos, (2, 1)), np.tile(sin, (2, 1))


def constants():
    c = np.zeros((P, C_ALL), np.float32)
    c[:, C_ID:C_ID + P] = np.eye(P)
    c[:, C_ONE:C_ONE + P] = 1.0
    half = HD // 8
    for b in (0, HD):
        for r in range(half):
            c[b + half + r, C_SWAP + b + r] = c[b + r, C_SWAP + b + half + r] = 1.0
    c[:, C_COS:C_COS + T], c[:, C_SIN:C_SIN + T] = rope_tables()
    c[:, C_TRI:C_TRI + P] = np.where(np.arange(P)[None, :] <= np.arange(P)[:, None], 0.0, NEG)
    s, t = np.divmod(np.arange(NS), STEPS)
    c[0:NS, C_MS:C_MS + NS] = np.where((s[None, :] == s[:, None]) & (t[None, :] <= t[:, None]), 0.0, NEG)
    for hd in range(IH):
        c[HD + hd, C_SEL + hd * P:C_SEL + (hd + 1) * P] = 1.0
    return c


def by_partition(a, lead):
    s = a.shape
    a = a.reshape(*s[:lead], s[lead] // P, P, *s[lead + 1:])
    return np.ascontiguousarray(np.swapaxes(a, lead, lead + 1))


OUTS = {"yT": (P, DC, T), "kT": (DEPTH, P, T), "vT": (DEPTH, P, T), "kiT": (DEPTH, HD, T),
        "convT": (DEPTH, P, LC, 3 * NC_), "hT": (DEPTH, P, LC, NC_)}


def kernel(**inputs):
    import concourse.bacc as bacc
    from concourse.bass_utils import run_bass_kernel_spmd

    i = {k: np.asarray(v) for k, v in inputs.items()}
    flat = i["x_sample"].reshape(NS, D)
    feat = lambda v: by_partition(v.reshape(DEPTH, -1, P).transpose(0, 1, 2).reshape(DEPTH, -1), 1)
    arrays = {
        "cst": constants(),
        "xT": by_partition(np.concatenate([i["x_prompt"][0], flat]).T, 0),
        "cT": by_partition(np.concatenate([i["c_prompt"], i["c_sample"]]).T, 0),
        "page_table": i["page_table"].reshape(1, -1),
        "vec": np.concatenate([feat(i[k]) for k in ("b_ada", "norm_g", "conv_w", "conv_b", "lru_ba", "lru_bx",
                                                    "lru_lambda")], axis=2),
        "state": np.concatenate([
            by_partition(i["state_h"].transpose(0, 2, 1), 1).reshape(DEPTH, P, -1),
            by_partition(i["state_conv"].transpose(0, 3, 1, 2), 1).reshape(DEPTH, P, -1)], axis=2),
        "kT_cache": np.ascontiguousarray(i["cache_k"].reshape(DEPTH, POOL, PAGE, P).transpose(0, 1, 3, 2)),
        "v_cache": i["cache_v"].reshape(DEPTH, POOL, PAGE, P),
        "kiT_cache": np.ascontiguousarray(i["cache_kidx"].transpose(0, 1, 3, 2)),
    }
    arrays |= {k: i[k] for k in ("w_ada", "ffn_w_gu", "ffn_w_down", "w_in", "w_out", "lru_wa", "lru_wx")}
    nc = bacc.Bacc("TRN2", target_bir_lowering=False, num_devices=1)
    arrays = {k: np.ascontiguousarray(v) for k, v in arrays.items()}
    a = {k: nc.dram_tensor(k, v.shape, mybir.dt.from_np(v.dtype), kind="ExternalInput").ap() for k, v in arrays.items()}
    a |= {k: nc.dram_tensor(k, s, F32, kind="ExternalOutput").ap() for k, s in OUTS.items()}
    decoder(nc, a)
    r = run_bass_kernel_spmd(nc, [arrays], core_ids=[0]).results[0]

    def tokens(v):
        return v.transpose(2, 1, 0).reshape(v.shape[2], -1)

    y = tokens(r["yT"])
    k, v, ki = (r[n].transpose(0, 2, 1) for n in ("kT", "vT", "kiT"))
    heads = lambda t, lead: t.reshape(*lead, NKV, HD)
    hT = r["hT"].transpose(0, 3, 2, 1).reshape(DEPTH, NC_, -1)
    conv = r["convT"].reshape(DEPTH, P, LC, NC_, 3).transpose(0, 3, 4, 2, 1).reshape(DEPTH, NC_, 3, -1)
    outs = (y[:SEQ].reshape(1, SEQ, D), y[SEQ:].reshape(NSEQ, STEPS, D),
            heads(k[:, :SEQ], (DEPTH, 1, SEQ)), heads(v[:, :SEQ], (DEPTH, 1, SEQ)), ki[:, :SEQ].reshape(DEPTH, 1, SEQ, HD),
            hT[:, 0:1], conv[:, 0:1],
            heads(k[:, SEQ:], (DEPTH, NSEQ, STEPS)), heads(v[:, SEQ:], (DEPTH, NSEQ, STEPS)),
            ki[:, SEQ:].reshape(DEPTH, NSEQ, STEPS, HD), hT[:, 1:], conv[:, 1:])
    return tuple(np.ascontiguousarray(o) for o in outs)
```

```python
from contextlib import ExitStack, contextmanager

import numpy as np

import concourse.bass as bass
from concourse import mybir

F32 = mybir.dt.float32
I32 = mybir.dt.int32
ALU = mybir.AluOpType
ACT = mybir.ActivationFunctionType
AX = mybir.AxisListType
RMAX = bass.bass_isa.ReduceOp.max

P = 128
DEPTH, D, SEQ, NSEQ, STEPS = 2, 1024, 512, 8, 4
NS = NSEQ * STEPS
T = SEQ + NS
TH = T // 2
DC = D // P
D_FF = 2816
FC = D_FF // P
LC = 4
CONV = 4
HEADS, HD, NKV = 8, 64, 2
IH = 4
NMOD = 9
NC_ = 1 + NSEQ
MC = NMOD * DC
IN_COLS = 2116
PC = IN_COLS // P
LAST = IN_COLS - PC * P
XL, GL, QQ, KK, VV, QI, KW = 0, 4, 8, 12, 13, 14, 16
PAGES, PAGE, POOL = 16, 128, 160
NB = PAGES + 1
TILES = SEQ // P
SEL_P, SEL_S = 128, 256
EPS = 1e-6
NEG = -1.0e30
TAKEN = -3.0e38
ROPED = [QQ, QQ + 1, QQ + 2, QQ + 3, KK, QI, QI + 1, KW]
GELU_C = float(np.sqrt(2.0 / np.pi))
SW = 3 + STEPS
XPW = 3 + SEQ + NSEQ * SW

C_ID, C_ONE, C_SWAP, C_COS, C_SIN = 0, P, 2 * P, 3 * P, 3 * P + T
C_TRI = C_SIN + T
C_MS = C_TRI + P
C_SEL = C_MS + NS
C_ALL = C_SEL + IH * P
V_BADA, V_G, V_CW, V_CB, V_BA, V_BX, V_LAM = 0, 72, 120, 136, 140, 144, 148
V_ALL = 152
ST_H, ST_C, ST_ALL = 0, LC * NSEQ, LC * NSEQ * 4

RING = 4
ADA_PARTS = ((0, 2), (2, 5), (5, NMOD))
RPF = DC // RING
U_GU = FC // 2
K_ADA0 = 0
K_GU1 = K_ADA0 + 2 * RPF
K_ADA1 = K_GU1 + U_GU
K_IN = K_ADA1 + 3 * RPF
K_ADA2 = K_IN + PC // RING
K_OUT = K_ADA2 + 4 * RPF
K_GU2 = K_OUT + DC // RING
W_USES = K_GU2 + U_GU
ARENA = FC * T + 2048
D_USES = DC
KREC = PAGE + PAGE // 2

DVE_STEPS = 325



class Signal:

    def __init__(self, ctx, nc, name, per, unit=1, start=0):
        self.sem = ctx.enter_context(nc.semaphore(name))
        self.per, self.unit, self.start = per, unit, start

    def at(self, layer, k):
        return layer * (self.per * self.unit) + (k * self.unit + self.start)


def hold(eng, passed, sem, value):
    eng.wait_ge(sem, value)
    eng.sem_inc(passed, 1)


class Steps:

    def __init__(self, eng, sem, per, layer, passed):
        self.passed = passed
        self.eng, self.sem, self.per, self.layer, self.n, self.shift = eng, sem, per, layer, 0, 0

    def mark(self, ins):
        self.n += 1
        ins.then_inc(self.sem, 1)
        return self.n

    def need(self, n):
        self.eng.wait_ge(self.sem, self.layer * self.per + (n + self.shift))

    def need_hold(self, n):
        hold(self.eng, self.passed, self.sem, self.layer * self.per + (n + self.shift))

    def link(self, ins):
        self.need(self.mark(ins))

    def link_hold(self, ins):
        self.need_hold(self.mark(ins))

    @contextmanager
    def loop(self, times, body_steps, start=0):
        first = self.n
        with self.eng.Fori(start, start + times) as i:
            self.shift = i * body_steps + (-start * body_steps)
            yield i
        assert self.n - first == body_steps, (self.n - first, body_steps)
        self.n = first + times * body_steps
        self.shift = 0


def decoder(nc, a):
    with ExitStack() as ctx:
        def sb(name, shape, dt=F32):
            return ctx.enter_context(nc.sbuf_tensor("sb_" + name, shape, dt))

        def sig(name, per, unit=1, start=0):
            return Signal(ctx, nc, name, per, unit, start)

        ps = ctx.enter_context(nc.psum_tensor("ps", [P, 8, 512], F32))

        x = sb("x", [P, DC, T])
        h = sb("h", [P, DC, T])
        rinv = sb("rinv", [P, T])
        arena = sb("arena", [P, ARENA])
        act = arena[:, 0:FC * T].rearrange("p (f t) -> p f t", f=FC)
        proj = sb("proj", [P, PC + 1, T])
        y = sb("y", [P, DC, T])
        wslot = [sb(f"wslot{i}", [P, DC, P]) for i in range(RING)]
        down = sb("down", [P, 2 * PAGES * KREC])
        dslot = [down[:, i * FC * P:(i + 1) * FC * P].rearrange("p (f n) -> p f n", f=FC) for i in range(2)]
        cst = sb("cst", [P, C_ALL])
        vec = sb("vec", [P, V_ALL])
        state = sb("state", [P, ST_ALL])
        cT = sb("cT", [P, DC, NC_])
        mod = sb("mod", [P, MC, NC_])
        gain = sb("gain", [P, DC, NC_])
        pages = sb("pages", [1, NSEQ * PAGES], I32)
        gates = sb("gates", [P, 2, LC, P])
        small = sb("small", [P, 12, LC])
        eps = sb("eps", [P, 1])
        hout = sb("hout", [P, LC, NC_])
        cout = sb("cout", [P, LC, 3 * NC_])

        sq = proj[:, 0:DC, :]
        tsil = y[:, 0:2, :]
        w_last = y[:, 2, :][:, 0:DC * LAST].rearrange("p (c n) -> p c n", c=DC)
        rtmp = [y[:, DC - 1, :], y[:, DC - 2, :]]

        ident, ones, swap = cst[:, C_ID:C_ID + P], cst[:, C_ONE:C_ONE + P], cst[:, C_SWAP:C_SWAP + P]
        cosT, sinT, tri = cst[:, C_COS:C_COS + T], cst[:, C_SIN:C_SIN + T], cst[:, C_TRI:C_TRI + P]
        mask_new = cst[0:NS, C_MS:C_MS + NS]
        sel = cst[:, C_SEL:C_SEL + IH * P].rearrange("p (h m) -> p h m", h=IH)

        at = [0]

        def carve(*shape):
            n = int(np.prod(shape))
            v = arena[:, at[0]:at[0] + n]
            at[0] += n
            if len(shape) == 2:
                v = v.rearrange("p (a b) -> p a b", a=shape[0])
            if len(shape) == 3:
                v = v.rearrange("p (a b c) -> p a b c", a=shape[0], b=shape[1])
            return v

        xp, xc, tc = carve(LC, XPW), carve(LC, T), carve(LC, T)
        ta, tb = y[:, 0:LC, :], y[:, LC:DC, :]
        th = xp[:, :, 0:T]
        lru_end, at[0] = at[0], 0
        kd = carve(3, SEQ)
        bias_p = carve(TILES, SEQ)
        arena_v = [carve(PAGES, PAGE) for _ in range(3)]
        assert at[0] >= lru_end
        top8 = carve(4, 8)
        nmax = carve(HEADS)
        den = carve(2, HEADS)
        cbuf = carve(NSEQ, 16)
        qiS = carve(NSEQ, 2, 16)
        qS = carve(NSEQ, 32)
        vtok = carve(TILES + 1, P)
        wtok = carve(TILES, IH)
        rden = carve(NSEQ * 32)
        mxa = rden
        at_common = at[0]
        scT = carve(2 * PAGES + 1, NS)
        relu = carve(2 * PAGES, 16)
        work = [carve(SEQ) for _ in range(2)]
        assert at[0] <= ARENA, (at[0], ARENA)
        at[0] = at_common
        prob = [carve(SEQ) for _ in range(2)]
        probT = [carve(SEQ) for _ in range(2)]
        ytok = carve(SEQ)
        assert at[0] <= ARENA, (at[0], ARENA)
        maskT = rinv[:, :].rearrange("p (j c) -> p j c", c=NS)
        kpage = [down[:, i * PAGES * KREC:(i + 1) * PAGES * KREC].rearrange("p (j n) -> p j n", j=PAGES)
                 for i in range(2)]
        pflat = proj[:, 0:8, :].rearrange("p a b -> p (a b)")
        in_proj = [pflat[:, i * 2048:(i + 1) * 2048].rearrange("p (j n) -> p j n", j=PAGES) for i in range(2)]
        in_down = [down[:, i * 2048:(i + 1) * 2048].rearrange("p (j n) -> p j n", j=PAGES) for i in range(3)]
        vpage = in_proj + arena_v + in_down
        V_POOL = 5
        mx = pflat[:, 4096:4096 + NSEQ * 32]
        sT = h[:, :, :].rearrange("p a b -> p (a b)")
        sT3 = sT.rearrange("p (s j c) -> p s j c", s=NSEQ, j=NB)
        scS = y[0:NS, LC:DC, :].rearrange("p a b -> p (a b)")[:, 0:PAGES * P + NS]

        s_in = sig("s_in", 0)
        w_full = [sig(f"w_full{i}", W_USES, 16) for i in range(RING)]
        w_free = [sig(f"w_free{i}", W_USES, 1, 1) for i in range(RING)]
        d_full = [sig(f"d_full{i}", DC, 16) for i in range(2)]
        d_free = [sig(f"d_free{i}", DC, 1, 1) for i in range(2)]
        last_full = sig("last_full", 1, 16)
        vec_full = sig("vec_full", 2, 16)
        vec_free = sig("vec_free", 1, 1, 1)
        gate_full = sig("gate_full", 16, 16)
        kp_full = [sig(f"kp_full{i}", 4 * PAGES, 16) for i in range(2)]
        kp_used = [sig(f"kp_used{i}", 4, 1, 1) for i in range(2)]
        vp_full = [sig(f"vp_full{i}", PAGES, 16) for i in range(NSEQ)]
        pv_s = sig("pv_s", NSEQ)
        arena_free = sig("arena_free", 1)
        ada_read = sig("ada_read", NMOD, 1, 1)
        ss_ready = sig("ss_ready", 6)
        sq_ready = sig("sq_ready", 3 * DC)
        root_ready = sig("root_ready", 6)
        xn_ready = sig("xn_ready", 3 * DC)
        h_act = sig("h_act", 3 * DC)
        h_dve = sig("h_dve", 3)
        tanh_ready = sig("tanh_ready", 2 * FC)
        act_ready = sig("act_ready", 2 * FC, 1, 2)
        dn_read = sig("dn_read", 2 * DC, 1, 2)
        res_done = sig("res_done", 3, 1, 1)
        kw_pe = sig("kw_pe", 1)
        pj_read = sig("pj_read", PC + 1, 1, 2)
        sw_ready = sig("sw_ready", 8)
        rope_done = sig("rope_done", 8)
        tok_pe = sig("tok_pe", 1)
        tok_read = sig("tok_read", 1)
        qs_ready = sig("qs_ready", 1)
        conv_done = sig("conv_done", 1)
        gz_ready = sig("gz_ready", LC)
        lam_in = sig("lam_in", 1)
        lam_exp = sig("lam_exp", 1)
        gate_tanh = sig("gate_tanh", LC, 1, 1)
        loga = sig("loga", 1)
        decay = sig("decay", 1)
        radicand = sig("radicand", 1)
        root_b = sig("root_b", 1)
        gelu_in = sig("gelu_in", 1)
        gelu_tanh = sig("gelu_tanh", 1)
        outs_ready = sig("outs_ready", 2)
        kv_stored = sig("kv_stored", 3, 16)
        states_stored = sig("states_stored", 2, 16)
        id_read = sig("id_read", NSEQ, 1, 2)
        ks_read = sig("ks_read", NSEQ, 1, 2)
        new_pe = sig("new_pe", 1)
        q_ready = sig("q_ready", 1)
        dots = sig("dots", (TILES - 1) * IH)
        relu_ready = sig("relu_ready", (TILES - 1) * IH, 1, 2)
        idx_sum = sig("idx_sum", (TILES - 1) * IH, 1, 2)
        idx_part = sig("idx_part", NSEQ, 1, 1)
        scT_pe = sig("scT_pe", 1)
        scS_ready = sig("scS_ready", 1)
        s_pe = sig("s_pe", TILES * HEADS)
        s_masked = sig("s_masked", TILES * HEADS, 1, 2)
        s_exp = sig("s_exp", TILES * HEADS)
        t_pe = sig("t_pe", TILES * HEADS)
        t_read = sig("t_read", TILES * HEADS, 1, 2)
        pv_p = sig("pv_p", TILES * HEADS)
        o_read = sig("o_read", TILES, 1, 2)
        yt_pe = sig("yt_pe", TILES)
        yt_read = sig("yt_read", TILES, 1, 1)
        topk_done = sig("topk_done", 1)
        mT_pe = sig("mT_pe", 1)
        yp_done = sig("yp_done", 1)
        max_in = sig("max_in", 1)
        pool_max = sig("pool_max", 1)
        sub_done = sig("sub_done", 1)
        exp_s = sig("exp_s", 1)
        sums = sig("sums", 1)
        den_pe = sig("den_pe", 1)
        ysample = sig("ysample", 1)
        wo_read = sig("wo_read", DC, 1, 2)
        dve_step = ctx.enter_context(nc.semaphore("dve_step"))
        eps_ready = sig("eps_ready", 0)
        cleared = sig("cleared", 0)
        passed = [ctx.enter_context(nc.semaphore(f"passed_{e}")) for e in ("sp", "pe", "pool", "dve")]
        y_out = sig("y_out", 0)
        DOTS = [(hd, i) for hd in range(IH) for i in range(1, TILES)]

        block = ctx.enter_context(nc.Block())

        def halves(pair):
            return ps[:, 2 * pair:2 * pair + 2, 0:TH]

        def tok2(v):
            return v.rearrange("p (b t) -> p b t", b=2)

        def layer_of(ap, l):
            return ap[bass.ds(l, 1)]

        def load_page(eng, tensor, l, seq_page, dst, full):
            page = eng.value_load(pages[0:1, bass.ds(seq_page, 1)], min_val=0, max_val=POOL - 1)
            src = layer_of(tensor, l)[:, bass.ds(page, 1)].rearrange("a b p n -> (a b p) n")
            eng.dma_start(dst.rearrange("p a n -> p (a n)"), src).then_inc(full.sem, 16)

        def key_loads(eng, i, l, pair):
            who = passed[0] if i == 0 else passed[2]
            if isinstance(pair, int):
                for n in range(2):
                    hold(eng, who, d_free[n].sem, d_free[n].at(l, DC // 2))
            hold(eng, who, kp_used[i].sem, kp_used[i].at(l, pair))
            with eng.Fori(0, PAGES) as j:
                load_page(eng, a["key_pages"], l, pair * (2 * PAGES) + (j + i * PAGES),
                          kpage[i][:, bass.ds(j, 1), :], kp_full[i])

        @block.sync
        def _(sp):
            sp.dma_start(cT[:, :, :], a["cT"]).then_inc(s_in.sem, 16)
            sp.dma_start(x[:, :, :], a["xT"]).then_inc(s_in.sem, 16)
            sp.dma_start(cst[:, :], a["cst"]).then_inc(s_in.sem, 16)
            sp.dma_start(pages[:, :], a["page_table"]).then_inc(s_in.sem, 16)
            sp.wait_ge(s_in.sem, 64)
            sp.wait_ge(cleared.sem, 2)
            with sp.Fori(0, DEPTH) as l:

                def rows(ap):
                    return ap.rearrange("a (c p) n -> p (a c) n", p=P)

                ada, w_in, w_out = (layer_of(a[n], l) for n in ("w_ada", "w_in", "w_out"))

                def piece(use, i, src):
                    sp.wait_ge(w_free[i].sem, w_free[i].at(l, use))
                    sp.dma_start(wslot[i][:, :, :], src).then_inc(w_full[i].sem, 16)

                def pieces(use, rounds, src, first=0):
                    with sp.Fori(0, rounds) as u:
                        for i in range(RING):
                            piece(use + u, i, rows(src[:, :, bass.ds(u * (RING * P) + (first + i) * P, P)]))

                def ffn_loads(f, k0, between):
                    gu = layer_of(a["ffn_w_gu"], l)[:, f]
                    dn = layer_of(a["ffn_w_down"], l)[:, f]
                    with sp.Fori(0, U_GU) as u:
                        for i in range(RING):
                            piece(k0 + u, i, rows(gu[:, :, bass.ds(u * (2 * P) + (i // 2) * P + (i % 2) * D_FF, P)]))

                    def down_loads(u):
                        for i in range(2):
                            sp.wait_ge(d_free[i].sem, d_free[i].at(l, u + f * (DC // 2)))
                            sp.dma_start(dslot[i], rows(dn[:, :, bass.ds(u * (2 * P) + i * P, P)]))\
                                .then_inc(d_full[i].sem, 16)

                    down_loads(0)
                    between()
                    with sp.Fori(1, DC // 2) as u:
                        down_loads(u)

                sp.wait_ge(vec_free.sem, vec_free.at(l, 0))
                sp.dma_start(vec[:, :], layer_of(a["vec"], l).rearrange("a p n -> (a p) n")).then_inc(vec_full.sem, 16)
                sp.dma_start(state[:, :], layer_of(a["state"], l).rearrange("a p n -> (a p) n")).then_inc(vec_full.sem, 16)
                pieces(K_ADA0, RPF * 2, ada)
                ffn_loads(0, K_GU1, lambda: pieces(K_ADA1, RPF * 3, ada, first=2 * DC))
                sp.wait_ge(gate_tanh.sem, gate_tanh.at(l, 0))
                for g, name in enumerate(("lru_wa", "lru_wx")):
                    for b in range(8):
                        half = (b % 2) * HD
                        sp.dma_start(gates[half:half + HD, g, b // 2, half:half + HD],
                                     layer_of(a[name], l)[:, b].rearrange("a i j -> (a i) j")).then_inc(gate_full.sem, 16)
                sp.dma_start(w_last, rows(w_in[:, :, PC * P:IN_COLS])).then_inc(last_full.sem, 16)
                pieces(K_IN, PC // RING, w_in)

                key_loads(sp, 0, l, 0)
                sp.wait_ge(rope_done.sem, rope_done.at(l, 8))
                hold(sp, passed[0], pj_read.sem, pj_read.at(l, PC + 1))
                for name, c, n in (("kT", KK, P), ("vT", VV, P), ("kiT", KW, HD)):
                    sp.dma_start(layer_of(a[name], l).rearrange("a p t -> (a p) t"), proj[0:n, c, :])\
                        .then_inc(kv_stored.sem, 16)
                with sp.Fori(1, NSEQ // 2) as pair:
                    key_loads(sp, 0, l, pair)
                pieces(K_ADA2, RPF, ada, first=5 * DC)
                sp.wait_ge(kp_used[0].sem, kp_used[0].at(l, 4))
                hold(sp, passed[0], kp_used[1].sem, kp_used[1].at(l, 4))
                for n, s in enumerate(range(V_POOL, NSEQ)):
                    with sp.Fori(0, PAGES) as j:
                        load_page(sp, a["v_cache"], l, s * PAGES + j, vpage[s][:, bass.ds(j, 1), :], vp_full[s])
                    pieces(K_ADA2 + (n + 1) * RPF, RPF, ada, first=(6 + n) * DC)
                pieces(K_OUT, DC // RING, w_out)
                ffn_loads(1, K_GU2, lambda: None)
            sp.wait_ge(res_done.sem, res_done.at(DEPTH - 1, 3))
            sp.dma_start(a["yT"], x[:, :, :]).then_inc(y_out.sem, 16)
            sp.wait_ge(y_out.sem, 16)
            sp.wait_ge(kv_stored.sem, kv_stored.at(DEPTH - 1, 3))
            sp.wait_ge(states_stored.sem, states_stored.at(DEPTH - 1, 2))

        @block.tensor
        def _(pe):
            mm = nc.tensor.matmul

            def sums_of_squares(squares, l, k):
                for c in range(DC):
                    pe.wait_ge(squares.sem, squares.at(l, k + c + 1))
                    for b in range(2):
                        last = mm(ps[:, 6 + b, 0:TH], ones, sq[:, c, b * TH:(b + 1) * TH],
                                  start=(c == 0), stop=(c == DC - 1))
                last.then_inc(ss_ready.sem, 1)

            def product(pair, weights, moving):
                n = len(weights)
                m = weights[0].shape[-1]
                for b in range(2):
                    for kc in range(n):
                        last = mm(ps[0:m, 2 * pair + b, 0:TH], weights[kc], moving[kc][:, b * TH:(b + 1) * TH],
                                  start=(kc == 0), stop=(kc == n - 1))
                return last

            hs = [h[:, kc, :] for kc in range(DC)]

            def slot(i):
                return [wslot[i][:, kc, :] for kc in range(DC)]

            def ada_chunk(l, use, m):
                r, i = divmod(m, RING)
                pe.wait_ge(w_full[i].sem, w_full[i].at(l, use + (r + 1)))
                for kc in range(DC):
                    last = mm(ps[:, 0, m * NC_:(m + 1) * NC_], wslot[i][:, kc, :], cT[:, kc, :],
                              start=(kc == 0), stop=(kc == DC - 1))
                last.then_inc(w_free[i].sem, 1)

            def ada(l, use, first, after):
                with pe.Fori(first, after) as g:
                    pe.wait_ge(ada_read.sem, ada_read.at(l, g))
                    for m in range(DC):
                        ada_chunk(l, g * RPF + (use - first * RPF), m)
                hold(pe, passed[1], ada_read.sem, ada_read.at(l, after))

            def ffn(l, f, k0, between):
                pe.wait_ge(h_dve.sem, h_dve.at(l, 1 if f == 0 else 3))
                hold(pe, passed[1], h_act.sem, h_act.at(l, DC if f == 0 else 3 * DC))
                with pe.Fori(0, U_GU) as u:
                    for i in range(2):
                        k = u * 2 + (f * FC + i)
                        pe.wait_ge(act_ready.sem, act_ready.at(l, k + 1 - 2))
                        for n in range(2):
                            j = 2 * i + n
                            pe.wait_ge(w_full[j].sem, w_full[j].at(l, k0 + 1 + u))
                            product(j, slot(j), hs).then_inc(w_free[j].sem, 1)
                hold(pe, passed[1], act_ready.sem, act_ready.at(l, (f + 1) * FC - 1))
                between()
                hold(pe, passed[1], act_ready.sem, act_ready.at(l, (f + 1) * FC))
                with pe.Fori(0, DC // 2) as u:
                    for i in range(2):
                        k = u * 2 + (f * DC + i)
                        pe.wait_ge(d_full[i].sem, d_full[i].at(l, u + (f * (DC // 2) + 1)))
                        pe.wait_ge(dn_read.sem, dn_read.at(l, k + 1 - 2))
                        product(1 + i, [dslot[i][:, kc, :] for kc in range(FC)], [act[:, kc, :] for kc in range(FC)])\
                            .then_inc(d_free[i].sem, 1)

            for s in (*w_free, *d_free, *kp_used):
                pe.sem_inc(s.sem, s.start)
            pe.wait_ge(s_in.sem, 64)
            pe.wait_ge(cleared.sem, 2)
            with pe.Fori(0, DEPTH) as l:
                ada(l, K_ADA0, 0, 2)
                sums_of_squares(sq_ready, l, 0)
                ffn(l, 0, K_GU1, lambda: ada(l, K_ADA1, 2, 5))
                sums_of_squares(dn_read, l, 0)
                sums_of_squares(sq_ready, l, 8)

                pe.wait_ge(h_dve.sem, h_dve.at(l, 2))
                hold(pe, passed[1], h_act.sem, h_act.at(l, 2 * DC))
                with pe.Fori(0, PC // RING) as u:
                    for i in range(RING):
                        pe.wait_ge(w_full[i].sem, w_full[i].at(l, u + (K_IN + 1)))
                        pe.wait_ge(pj_read.sem, pj_read.at(l, u * RING + (i + 1 - 2)))
                        product(i % 2, slot(i), hs).then_inc(w_free[i].sem, 1)
                pe.wait_ge(last_full.sem, last_full.at(l, 1))
                pe.wait_ge(pj_read.sem, pj_read.at(l, PC + 1 - 2))
                product(0, [w_last[:, kc, :] for kc in range(DC)], hs).then_inc(kw_pe.sem, 1)

                for n, c in enumerate(ROPED):
                    pe.wait_ge(pj_read.sem, pj_read.at(l, PC + 1 if c == KW else c + 1))
                    if n >= 2:
                        pe.wait_ge(rope_done.sem, rope_done.at(l, n - 1))
                    product(2 + n % 2, [swap], [proj[:, c, :]]).then_inc(sw_ready.sem, 1)
                pe.wait_ge(pj_read.sem, pj_read.at(l, PC + 1))
                for j in range(TILES):
                    nc.tensor.transpose(ps[:, 0, j * P:(j + 1) * P], proj[:, VV, j * P:(j + 1) * P], ident)
                nc.tensor.transpose(ps[0:NS, 1, 0:P], proj[:, VV, SEQ:T], ident)
                pe.wait_ge(rope_done.sem, rope_done.at(l, len(ROPED)))
                for j in range(TILES):
                    last = nc.tensor.transpose(ps[:, 4, j * P:(j + 1) * P], proj[:, KW, j * P:(j + 1) * P], ident)
                for hd in range(IH):
                    last = mm(ps[:, 5, hd * NS:(hd + 1) * NS], sel[:, hd, :], proj[:, KW, SEQ:T], start=True, stop=True)
                last.then_inc(tok_pe.sem, 1)

                pe.wait_ge(tok_read.sem, tok_read.at(l, 1))
                pe.wait_ge(gate_full.sem, gate_full.at(l, 16))
                pe.wait_ge(conv_done.sem, conv_done.at(l, 1))
                for c in range(LC):
                    if c >= 2:
                        pe.wait_ge(gate_tanh.sem, gate_tanh.at(l, c - 1))
                    product(2 * (c % 2), [gates[:, 0, c, :]], [xc[:, c, :]])
                    last = product(2 * (c % 2) + 1, [gates[:, 1, c, :]], [xc[:, c, :]])
                    last.then_inc(gz_ready.sem, 1)

                def page_products(pair):
                    for i in range(2):
                        pe.wait_ge(kp_full[i].sem, kp_full[i].at(l, pair * PAGES + PAGES))
                        pe.wait_ge(id_read.sem, id_read.at(l, pair * 2 + (i + 1 - 2)))
                        hold(pe, passed[1], ks_read.sem, ks_read.at(l, pair * 2 + (i + 1 - 2)))
                        for j in range(PAGES):
                            mm(ps[0:HD, 4 + i, j * 32:(j + 1) * 32], kpage[i][:, j, P:KREC],
                               qiS[:, bass.ds(pair * 2 + i, 1), :, :].rearrange("p a e c -> p (a e c)"), start=True, stop=True)
                            last = mm(ps[:, 6 + i, j * 32:(j + 1) * 32], kpage[i][:, j, 0:P],
                                      qS[:, bass.ds(pair * 2 + i, 1), :].rearrange("p a c -> p (a c)"), start=True, stop=True)
                        last.then_inc(kp_used[i].sem, 1)

                pe.wait_ge(qs_ready.sem, qs_ready.at(l, 1))
                hold(pe, passed[1], gate_tanh.sem, gate_tanh.at(l, LC))
                page_products(0)
                for s in range(NSEQ):
                    mm(ps[0:NS, 2, s * 16:(s + 1) * 16], proj[0:HD, KW, SEQ:T], qiS[0:HD, s, 0, :],
                       start=True, stop=True)
                    last = mm(ps[0:NS, 3, s * 32:(s + 1) * 32], proj[:, KK, SEQ:T], qS[:, s, :], start=True, stop=True)
                last.then_inc(new_pe.sem, 1)

                pe.wait_ge(q_ready.sem, q_ready.at(l, 1))
                for k, (hd, i) in enumerate(DOTS):
                    half, span = hd % 2, (i + 1) * P
                    pe.wait_ge(relu_ready.sem, relu_ready.at(l, k + 1 - 2))
                    keys = proj[0:HD, KW, 0:span] if half == 0 else kd[HD:P, 2, 0:span]
                    mm(ps[:, k % 2, 0:span], proj[half * HD:(half + 1) * HD, QI + hd // 2, i * P:(i + 1) * P], keys,
                       start=True, stop=True).then_inc(dots.sem, 1)
                hold(pe, passed[1], relu_ready.sem, relu_ready.at(l, len(DOTS)))
                with pe.Fori(1, NSEQ // 2) as pair:
                    page_products(pair)
                pe.wait_ge(idx_part.sem, idx_part.at(l, NSEQ))
                hold(pe, passed[1], ks_read.sem, ks_read.at(l, NSEQ))
                for j in range(2 * PAGES):
                    nc.tensor.transpose(ps[0:NS, 4 + j // 8, (j % 8) * HD:(j % 8 + 1) * HD], scT[0:HD, j, :],
                                        ident[0:HD, 0:HD])
                nc.tensor.transpose(ps[0:NS, 2, 0:NS], scT[0:NS, 2 * PAGES, :], ident[0:NS, 0:NS])\
                    .then_inc(scT_pe.sem, 1)

                head_keys = lambda half, kv, j0, j1: (proj[half * HD:(half + 1) * HD, KK, j0:j1] if half == kv
                                                      else kd[half * HD:(half + 1) * HD, kv, j0:j1])
                pe.wait_ge(scS_ready.sem, scS_ready.at(l, 1))

                def scores(n):
                    i, hd = divmod(n, HEADS)
                    half = hd % 2
                    pe.wait_ge(s_masked.sem, s_masked.at(l, n + 1 - 2))
                    mm(ps[:, 4 + n % 2, 0:(i + 1) * P],
                       proj[half * HD:(half + 1) * HD, QQ + hd // 2, i * P:(i + 1) * P],
                       head_keys(half, hd // (HEADS // NKV), 0, (i + 1) * P), start=True, stop=True)\
                        .then_inc(s_pe.sem, 1)

                def transposes(n):
                    pe.wait_ge(s_exp.sem, s_exp.at(l, n + 1))
                    pe.wait_ge(t_read.sem, t_read.at(l, n + 1 - 2))
                    for j in range(n // HEADS + 1):
                        last = nc.tensor.transpose(ps[:, 6 + n % 2, j * P:(j + 1) * P],
                                                   prob[n % 2][:, j * P:(j + 1) * P], ident)
                    last.then_inc(t_pe.sem, 1)

                def values(n):
                    i, hd = divmod(n, HEADS)
                    kv = hd // (HEADS // NKV)
                    pe.wait_ge(t_read.sem, t_read.at(l, n + 1))
                    if hd == 0:
                        pe.wait_ge(o_read.sem, o_read.at(l, i + 1 - 2))
                    for j in range(i + 1):
                        last = mm(ps[:, 2 + i % 2, hd * HD:(hd + 1) * HD], probT[n % 2][:, j * P:(j + 1) * P],
                                  vtok[:, j, kv * HD:(kv + 1) * HD], start=(j == 0), stop=(j == i))
                    last.then_inc(pv_p.sem, 1)

                def output(i):
                    pe.wait_ge(o_read.sem, o_read.at(l, i + 1))
                    pe.wait_ge(yt_read.sem, yt_read.at(l, i))
                    for c in range(4):
                        last = nc.tensor.transpose(ps[:, 1, c * P:(c + 1) * P], ytok[:, c * P:(c + 1) * P], ident)
                    last.then_inc(yt_pe.sem, 1)

                scores(0)
                for n in range(TILES * HEADS):
                    if n + 1 < TILES * HEADS:
                        scores(n + 1)
                    transposes(n)
                    if n:
                        values(n - 1)
                    i, hd = divmod(n, HEADS)
                    if i and hd == 3:
                        output(i - 1)
                    if hd == 0:
                        pe.wait_ge(ada_read.sem, ada_read.at(l, 5 + i))
                    ada_chunk(l, K_ADA2 + i * RPF, hd)
                values(TILES * HEADS - 1)
                output(TILES - 1)

                pe.wait_ge(s_masked.sem, s_masked.at(l, TILES * HEADS))
                hold(pe, passed[1], topk_done.sem, topk_done.at(l, 1))
                for j in range(PAGES):
                    nc.tensor.transpose(ps[:, 4, j * NS:(j + 1) * NS], scS[:, j * P:(j + 1) * P], ident[0:NS, 0:NS])
                nc.tensor.transpose(ps[0:NS, 5, 0:NS], scS[:, PAGES * P:PAGES * P + NS], ident[0:NS, 0:NS])\
                    .then_inc(mT_pe.sem, 1)
                pe.wait_ge(t_read.sem, t_read.at(l, TILES * HEADS))
                pe.wait_ge(sums.sem, sums.at(l, 1))
                mm(ps[:, 6, 0:NSEQ * 32], ones, mx, start=True, stop=True).then_inc(den_pe.sem, 1)
                for s in range(NSEQ):
                    pe.wait_ge(vp_full[s].sem, vp_full[s].at(l, PAGES))
                    out = ps[:, 7, s * 32:(s + 1) * 32]
                    for j in range(PAGES):
                        mm(out, vpage[s][:, j, :], sT3[:, s, j, :], start=(j == 0), stop=False)
                    mm(out, vtok[0:NS, TILES, :], sT3[0:NS, s, PAGES, :], start=False, stop=True)\
                        .then_inc(pv_s.sem, 1)

                pe.wait_ge(ada_read.sem, ada_read.at(l, NMOD))
                pe.wait_ge(yp_done.sem, yp_done.at(l, 1))
                hold(pe, passed[1], ysample.sem, ysample.at(l, 1))
                with pe.Fori(0, DC // RING) as u:
                    for i in range(RING):
                        pe.wait_ge(w_full[i].sem, w_full[i].at(l, u + (K_OUT + 1)))
                        pe.wait_ge(wo_read.sem, wo_read.at(l, u * RING + (i + 1 - 2)))
                        product(i % 2, slot(i), [y[:, kc, :] for kc in range(DC)]).then_inc(w_free[i].sem, 1)
                sums_of_squares(wo_read, l, 0)
                sums_of_squares(sq_ready, l, 16)
                ffn(l, 1, K_GU2, lambda: None)
                sums_of_squares(dn_read, l, 8)

        @block.scalar
        def _(sc):
            act_fn = nc.scalar.activation

            def squares_of_x(l, k):
                for c in range(DC):
                    act_fn(sq[:, c, :], x[:, c, :], ACT.Square).then_inc(sq_ready.sem, 1)

            def root(l, k):
                sc.wait_ge(ss_ready.sem, ss_ready.at(l, k + 1))
                act_fn(tok2(rinv[:, :]), halves(3), ACT.Sqrt, bias=eps[:, 0:1], scale=1.0 / D).then_inc(root_ready.sem, 1)

            def gain_and_shift(l, k, shift):
                for c in range(DC):
                    sc.wait_ge(xn_ready.sem, xn_ready.at(l, k * DC + c + 1))
                    act_fn(h[:, c, 0:SEQ], h[:, c, 0:SEQ], ACT.Identity, bias=mod[:, shift * DC + c, 0:1],
                           scale=gain[:, c, 0:1]).then_inc(h_act.sem, 1)

            def ffn(l, f, k0):
                with sc.Fori(0, U_GU) as u:
                    for i in range(2):
                        k = u * 2 + (f * FC + i)
                        sc.wait_ge(w_free[2 * i].sem, w_free[2 * i].at(l, u + (k0 + 1)))
                        sc.wait_ge(act_ready.sem, act_ready.at(l, k + 1 - 2))
                        act_fn(tok2(tsil[:, i, :]), halves(2 * i), ACT.Tanh, scale=0.5).then_inc(tanh_ready.sem, 1)
                for m in range(DC):
                    i = m % 2
                    sc.wait_ge(d_free[i].sem, d_free[i].at(l, f * (DC // 2) + m // 2 + 1))
                    act_fn(tok2(h[:, m, :]), halves(1 + i), ACT.Copy)
                    act_fn(tok2(sq[:, m, :]), halves(1 + i), ACT.Square).then_inc(dn_read.sem, 1)

            for s in (dn_read, pj_read, wo_read, t_read, yt_read, gate_tanh, relu_ready, ks_read):
                sc.sem_inc(s.sem, s.start)
            sc.wait_ge(s_in.sem, 64)
            sc.wait_ge(eps_ready.sem, 1)
            with sc.Fori(0, DEPTH) as l:
                sc.wait_ge(res_done.sem, res_done.at(l, 0))
                squares_of_x(l, 0)
                root(l, 0)
                gain_and_shift(l, 0, 0)
                ffn(l, 0, K_GU1)
                root(l, 1)
                sc.wait_ge(res_done.sem, res_done.at(l, 1))
                squares_of_x(l, 2)
                root(l, 2)
                gain_and_shift(l, 1, 3)

                with sc.Fori(0, PC // RING) as u:
                    for i in range(RING):
                        sc.wait_ge(w_free[i].sem, w_free[i].at(l, u + (K_IN + 1)))
                        dst = proj[:, bass.ds(u * RING + i, 1), :].rearrange("p a (b t) -> p (a b) t", b=2)
                        act_fn(dst, halves(i % 2), ACT.Copy).then_inc(pj_read.sem, 1)
                sc.wait_ge(kw_pe.sem, kw_pe.at(l, 1))
                act_fn(tok2(proj[0:LAST, KW, :]), ps[0:LAST, 0:2, 0:TH], ACT.Copy).then_inc(pj_read.sem, 1)

                sc.wait_ge(lam_in.sem, lam_in.at(l, 1))
                act_fn(small[:, 2, :], small[:, 1, :], ACT.Exp, scale=-1.0).then_inc(lam_exp.sem, 1)
                for c in range(LC):
                    sc.wait_ge(gz_ready.sem, gz_ready.at(l, c + 1))
                    act_fn(tok2(ta[:, c, :]), halves(2 * (c % 2)), ACT.Tanh, bias=small[:, 10, c:c + 1], scale=0.5)
                    act_fn(tok2(tb[:, c, :]), halves(2 * (c % 2) + 1), ACT.Tanh, bias=small[:, 11, c:c + 1], scale=0.5)\
                        .then_inc(gate_tanh.sem, 1)
                sc.wait_ge(loga.sem, loga.at(l, 1))
                act_fn(ta[:, :, :], tc[:, :, :], ACT.Exp)
                act_fn(th[:, :, :], tc[:, :, :], ACT.Tanh, scale=-1.0).then_inc(decay.sem, 1)
                sc.wait_ge(radicand.sem, radicand.at(l, 1))
                act_fn(th[:, :, :], th[:, :, :], ACT.Sqrt).then_inc(root_b.sem, 1)
                sc.wait_ge(gelu_in.sem, gelu_in.at(l, 1))
                act_fn(tc[:, :, :], tc[:, :, :], ACT.Tanh).then_inc(gelu_tanh.sem, 1)

                def page_scores(pair):
                    for i in range(2):
                        sc.wait_ge(kp_used[i].sem, kp_used[i].at(l, pair + 1))
                        dst = sT3[:, bass.ds(pair * 2 + i, 1), 0:PAGES, :].rearrange("p a j c -> p (a j c)")
                        act_fn(dst, ps[:, 6 + i, :], ACT.Copy).then_inc(ks_read.sem, 1)

                page_scores(0)
                sc.wait_ge(new_pe.sem, new_pe.at(l, 1))
                sc.wait_ge(qs_ready.sem, qs_ready.at(l, 1))
                act_fn(sT3[0:NS, :, PAGES, :], ps[0:NS, 3, 0:NSEQ * 32].rearrange("p (s c) -> p s c", s=NSEQ), ACT.Copy)
                for k, (hd, i) in enumerate(DOTS):
                    sc.wait_ge(dots.sem, dots.at(l, k + 1))
                    sc.wait_ge(idx_sum.sem, idx_sum.at(l, k + 1 - 2))
                    act_fn(work[k % 2][:, 0:(i + 1) * P], ps[:, k % 2, 0:(i + 1) * P], ACT.Relu)\
                        .then_inc(relu_ready.sem, 1)
                with sc.Fori(1, NSEQ // 2) as pair:
                    page_scores(pair)

                def transposed(n):
                    i = n // HEADS
                    sc.wait_ge(t_pe.sem, t_pe.at(l, n + 1))
                    if n >= 2:
                        sc.wait_ge(pv_p.sem, pv_p.at(l, n - 1))
                    act_fn(probT[n % 2][:, 0:(i + 1) * P], ps[:, 6 + n % 2, 0:(i + 1) * P], ACT.Copy)\
                        .then_inc(t_read.sem, 1)

                def output(i):
                    sc.wait_ge(yt_pe.sem, yt_pe.at(l, i + 1))
                    act_fn(bias_p[:, i, :], ps[:, 1, :], ACT.Copy).then_inc(yt_read.sem, 1)

                sc.wait_ge(scT_pe.sem, scT_pe.at(l, 1))
                for n in range(TILES * HEADS):
                    i, hd = divmod(n, HEADS)
                    sc.wait_ge(s_masked.sem, s_masked.at(l, n + 1))
                    act_fn(prob[n % 2][:, 0:(i + 1) * P], prob[n % 2][:, 0:(i + 1) * P], ACT.Exp,
                           bias=nmax[:, hd:hd + 1], scale=HD ** -0.5, accum_out=den[:, i % 2, hd:hd + 1])\
                        .then_inc(s_exp.sem, 1)
                    transposed(n)
                    if i and hd == 3:
                        output(i - 1)
                output(TILES - 1)
                sc.wait_ge(mT_pe.sem, mT_pe.at(l, 1))
                sc.wait_ge(yt_read.sem, yt_read.at(l, TILES))
                for i in range(TILES):
                    last = act_fn(y[:, LC:DC, i * P:(i + 1) * P], bias_p[:, i, :].rearrange("p (c t) -> p c t", c=4),
                                  ACT.Copy)
                last.then_inc(yp_done.sem, 1)

                sc.wait_ge(sub_done.sem, sub_done.at(l, 1))
                act_fn(sT, sT, ACT.Exp, scale=HD ** -0.5).then_inc(exp_s.sem, 1)

                with sc.Fori(0, DC // RING) as u:
                    for i in range(RING):
                        sc.wait_ge(w_free[i].sem, w_free[i].at(l, u + (K_OUT + 1)))
                        for dst, fn in ((h, ACT.Copy), (sq, ACT.Square)):
                            last = act_fn(dst[:, bass.ds(u * RING + i, 1), :].rearrange("p a (b t) -> p (a b) t", b=2),
                                          halves(i % 2), fn)
                        last.then_inc(wo_read.sem, 1)
                root(l, 3)
                sc.wait_ge(res_done.sem, res_done.at(l, 2))
                squares_of_x(l, 4)
                root(l, 4)
                gain_and_shift(l, 2, 6)
                ffn(l, 1, K_GU2)
                root(l, 5)
                sc.wait_ge(kv_stored.sem, kv_stored.at(l, 3))

        @block.gpsimd
        def _(pool):
            pool.wait_ge(s_in.sem, 64)
            with pool.Fori(0, DEPTH) as l:
                key_loads(pool, 1, l, 0)
                pool.wait_ge(outs_ready.sem, outs_ready.at(l, 1))
                pool.dma_start(layer_of(a["convT"], l).rearrange("a p c n -> (a p) c n"), cout[:, :, :])\
                    .then_inc(states_stored.sem, 16)
                with pool.Fori(1, 2) as pair:
                    key_loads(pool, 1, l, pair)
                pool.wait_ge(outs_ready.sem, outs_ready.at(l, 2))
                pool.dma_start(layer_of(a["hT"], l).rearrange("a p c n -> (a p) c n"), hout[:, :, :])\
                    .then_inc(states_stored.sem, 16)
                with pool.Fori(2, NSEQ // 2) as pair:
                    key_loads(pool, 1, l, pair)
                hold(pool, passed[2], arena_free.sem, arena_free.at(l, 1))
                for s in range(V_POOL):
                    with pool.Fori(0, PAGES) as j:
                        load_page(pool, a["v_cache"], l, s * PAGES + j, vpage[s][:, bass.ds(j, 1), :], vp_full[s])
                hold(pool, passed[2], max_in.sem, max_in.at(l, 1))
                nc.gpsimd.partition_all_reduce(mxa, mx, P, RMAX).then_inc(pool_max.sem, 1)

        @block.vector
        def _(dve):
            v = nc.vector
            v.memset(eps[:, :], EPS).then_inc(eps_ready.sem, 1)
            v.memset(gates[:, :, :, :], 0.0).then_inc(cleared.sem, 1)
            v.memset(proj[HD:P, KW, :], 0.0).then_inc(cleared.sem, 1)
            for s in (vec_free, idx_part, ada_read, act_ready, s_masked, o_read, res_done, id_read, idx_sum):
                dve.sem_inc(s.sem, s.start)
            dve.wait_ge(s_in.sem, 64)
            with dve.Fori(0, DEPTH) as l:
                st = Steps(dve, dve_step, DVE_STEPS, l, passed[3])

                def steps_of(ap):
                    return ap.rearrange("p c (s t) -> p c s t", t=STEPS)

                def each_step(m):
                    return m[:, :, 1:NC_].unsqueeze(3).to_broadcast([P, DC, NSEQ, STEPS])

                def norm_g(k):
                    return vec[:, V_G + k * DC:V_G + (k + 1) * DC].unsqueeze(2).to_broadcast([P, DC, NC_])

                def pre_norm(k, r, scale, shift):
                    st.link(v.scalar_tensor_tensor(gain[:, :, :], mod[:, scale * DC:(scale + 1) * DC, :], 1.0,
                                                   norm_g(r), ALU.add, ALU.mult))
                    dve.wait_ge(root_ready.sem, root_ready.at(l, r + 1))
                    st.link(v.reciprocal(rinv[:, :], rinv[:, :]))
                    for c in range(DC):
                        v.tensor_tensor(h[:, c, :], x[:, c, :], rinv[:, :], ALU.mult).then_inc(xn_ready.sem, 1)
                    dve.wait_ge(xn_ready.sem, xn_ready.at(l, (k + 1) * DC))
                    hn = steps_of(h[:, :, SEQ:T])
                    st.link(v.tensor_tensor(hn, hn, each_step(gain), ALU.mult))
                    v.tensor_tensor(hn, hn, each_step(mod[:, shift * DC:(shift + 1) * DC, :]), ALU.add)\
                        .then_inc(h_dve.sem, 1)

                def residual(k, r, gate, factor):
                    dve.wait_ge(h_act.sem, h_act.at(l, DC * (1, 2, 3)[k]))
                    st.link(v.scalar_tensor_tensor(gain[:, :, :], mod[:, gate * DC:(gate + 1) * DC, :], factor,
                                                   norm_g(r), ALU.mult, ALU.mult))
                    dve.wait_ge(root_ready.sem, root_ready.at(l, r + 1))
                    st.link(v.reciprocal(rinv[:, :], rinv[:, :]))
                    st.link(v.tensor_tensor(h[:, :, :], h[:, :, :], rinv[:, :].unsqueeze(1).to_broadcast([P, DC, T]),
                                            ALU.mult))
                    hn, xs = steps_of(h[:, :, SEQ:T]), steps_of(x[:, :, SEQ:T])
                    st.link(v.tensor_tensor(hn, hn, each_step(gain), ALU.mult))
                    v.tensor_tensor(xs, xs, hn, ALU.add)
                    for c in range(DC):
                        last = v.scalar_tensor_tensor(x[:, c, 0:SEQ], h[:, c, 0:SEQ], gain[:, c, 0:1], x[:, c, 0:SEQ],
                                                      ALU.mult, ALU.add)
                    last.then_inc(res_done.sem, 1)
                    dve.wait_ge(res_done.sem, res_done.at(l, k + 1))

                def swiglu(f, k0):
                    with st.loop(U_GU, 2) as u:
                        for i in range(2):
                            dve.wait_ge(tanh_ready.sem, tanh_ready.at(l, u * 2 + (f * FC + i + 1)))
                            st.link(v.scalar_tensor_tensor(tok2(tsil[:, i, :]), tok2(tsil[:, i, :]), 1.0, halves(2 * i),
                                                           ALU.add, ALU.mult))
                            dve.wait_ge(w_free[2 * i + 1].sem, w_free[2 * i + 1].at(l, u + (k0 + 1)))
                            v.scalar_tensor_tensor(
                                act[:, bass.ds(u * 2 + i, 1), :].rearrange("p a (b t) -> p (a b) t", b=2),
                                tok2(tsil[:, i, :]), 0.5, halves(2 * i + 1), ALU.mult, ALU.mult)\
                                .then_inc(act_ready.sem, 1)

                def ada_bias(g, use):
                    dve.wait_ge(w_free[RING - 1].sem, w_free[RING - 1].at(l, use))
                    v.tensor_tensor(mod[:, bass.ds(g * DC, DC), :],
                                    ps[:, 0, 0:DC * NC_].rearrange("p (m c) -> p m c", c=NC_),
                                    vec[:, bass.ds(g * DC + V_BADA, DC)].unsqueeze(2).to_broadcast([P, DC, NC_]),
                                    ALU.add).then_inc(ada_read.sem, 1)

                def ada(use, first, after):
                    with dve.Fori(first, after) as g:
                        ada_bias(g, g * RPF + (use - first * RPF + RPF))
                    dve.wait_ge(ada_read.sem, ada_read.at(l, after))

                hold(dve, passed[3], vec_full.sem, vec_full.at(l, 2))
                ada(K_ADA0, 0, 2)
                pre_norm(0, 0, 1, 0)
                swiglu(0, K_GU1)
                ada(K_ADA1, 2, 5)
                residual(0, 1, 2, 0.5)
                pre_norm(1, 2, 4, 3)

                lam = vec[:, V_LAM:V_LAM + LC]
                neg, z, z2, poly = small[:, 0, :], small[:, 3, :], small[:, 4, :], small[:, 5, :]
                st.link(v.tensor_scalar(neg, lam, -1.0, None, ALU.mult))
                v.tensor_tensor(small[:, 1, :], neg, lam, ALU.max).then_inc(lam_in.sem, 1)
                v.tensor_scalar(small[:, 10, :], vec[:, V_BA:V_BA + LC], 0.5, None, ALU.mult)
                v.tensor_scalar(small[:, 11, :], vec[:, V_BX:V_BX + LC], 0.5, None, ALU.mult)

                def decay_rate():
                    dve.wait_ge(lam_exp.sem, lam_exp.at(l, 1))
                    st.link(v.tensor_scalar(z2, small[:, 2, :], 2.0, None, ALU.add))
                    st.link(v.reciprocal(z2, z2))
                    st.link(v.tensor_tensor(z, small[:, 2, :], z2, ALU.mult))
                    st.link(v.tensor_tensor(z2, z, z, ALU.mult))
                    st.link(v.tensor_scalar(poly, z2, 1.0 / 19, 1.0 / 17, ALU.mult, ALU.add))
                    for n in (15, 13, 11, 9, 7, 5, 3, 1):
                        st.link(v.tensor_tensor(poly, poly, z2, ALU.mult))
                        st.link(v.tensor_scalar(poly, poly, 1.0 / n, None, ALU.add))
                    st.link(v.tensor_tensor(poly, poly, z, ALU.mult))
                    st.link(v.tensor_scalar(neg, neg, 0.0, None, ALU.max))
                    st.link(v.scalar_tensor_tensor(poly, poly, 2.0, neg, ALU.mult, ALU.add))
                    st.link(v.tensor_scalar(small[:, 6, :], poly, -0.5 * 8.0, None, ALU.mult))

                def rotate(n):
                    c = ROPED[n]
                    rows = HD if c == KW else P
                    st.need(products[n])
                    v.tensor_tensor(proj[0:rows, c, :], proj[0:rows, c, :], rtmp[n % 2][0:rows, :], ALU.add)\
                        .then_inc(rope_done.sem, 1)

                products = []
                for n, c in enumerate(ROPED):
                    rows = HD if c == KW else P
                    dve.wait_ge(sw_ready.sem, sw_ready.at(l, n + 1))
                    if n >= 2:
                        dve.wait_ge(rope_done.sem, rope_done.at(l, n - 1))
                    v.tensor_tensor(tok2(rtmp[n % 2][0:rows, :]), ps[0:rows, 4 + 2 * (n % 2):6 + 2 * (n % 2), 0:TH],
                                    tok2(sinT[0:rows, :]), ALU.mult)
                    products.append(st.mark(v.tensor_tensor(proj[0:rows, c, :], proj[0:rows, c, :], cosT[0:rows, :],
                                                            ALU.mult)))
                    if n:
                        rotate(n - 1)
                rotate(len(ROPED) - 1)

                v.memset(qiS, 0.0)
                v.memset(sT3[:, :, PAGES, :], NEG)
                st.link(v.memset(qS, 0.0))
                dve.wait_ge(rope_done.sem, rope_done.at(l, len(ROPED)))
                for hd in range(IH):
                    for e in range(2):
                        half = hd % 2
                        v.tensor_copy(qiS[e * HD:(e + 1) * HD, :, e, hd * STEPS:(hd + 1) * STEPS],
                                      proj[half * HD:(half + 1) * HD, QI + hd // 2, SEQ:T]
                                      .rearrange("p (s t) -> p s t", t=STEPS))
                for hd in range(HEADS):
                    half, kv = hd % 2, hd // (HEADS // NKV)
                    last = v.tensor_copy(qS[kv * HD:(kv + 1) * HD, :, hd * STEPS:(hd + 1) * STEPS],
                                         proj[half * HD:(half + 1) * HD, QQ + hd // 2, SEQ:T]
                                         .rearrange("p (s t) -> p s t", t=STEPS))
                last.then_inc(qs_ready.sem, 1)

                xs = xp[:, :, 3 + SEQ:XPW].rearrange("p c (s w) -> p c s w", w=SW)
                xcs = xc[:, :, SEQ:T].rearrange("p c (s t) -> p c s t", t=STEPS)
                v.memset(xp[:, :, 0:3], 0.0)
                v.tensor_copy(xp[:, :, 3:3 + SEQ], proj[:, XL:XL + LC, 0:SEQ])
                v.tensor_copy(xs[:, :, :, 3:SW], steps_of(proj[:, XL:XL + LC, SEQ:T]))
                st.link(v.tensor_copy(xs[:, :, :, 0:3],
                                      state[:, ST_C:ST_ALL].rearrange("p (c s w) -> p c s w", c=LC, w=3)))
                v.tensor_copy(cout[:, :, 0:3], xp[:, :, SEQ:SEQ + 3])
                v.tensor_copy(cout[:, :, 3:3 * NC_].rearrange("p c (s w) -> p c s w", w=3), xs[:, :, :, STEPS:SW])\
                    .then_inc(outs_ready.sem, 1)
                dve.wait_ge(tok_pe.sem, tok_pe.at(l, 1))
                v.tensor_copy(vtok[:, 0:TILES, :], ps[:, 0, :].rearrange("p (j d) -> p j d", d=P))
                v.tensor_copy(vtok[0:NS, TILES, :], ps[0:NS, 1, 0:P])
                w_scale = HD ** -0.5 * IH ** -0.5
                v.tensor_scalar(wtok, ps[:, 4, :].rearrange("p (j d) -> p j d", d=P)[:, :, HD:HD + IH], w_scale, None,
                                ALU.mult)
                for hd in range(IH):
                    last = v.tensor_scalar(cbuf[:, :, hd * STEPS:(hd + 1) * STEPS],
                                           ps[:, 5, hd * NS:(hd + 1) * NS].rearrange("p (s t) -> p s t", t=STEPS),
                                           w_scale, None, ALU.mult)
                last.then_inc(tok_read.sem, 1)
                for j in range(CONV):
                    for c in range(LC):
                        tap = vec[:, V_CW + j * LC + c:V_CW + j * LC + c + 1]
                        for dst, src in ((xc[:, c, 0:SEQ], xp[:, c, j:j + SEQ]), (xcs[:, c], xs[:, c, :, j:j + STEPS])):
                            if j == 0:
                                last = v.tensor_scalar(dst, src, tap, vec[:, V_CB + c:V_CB + c + 1], ALU.mult, ALU.add)
                            else:
                                last = v.scalar_tensor_tensor(dst, src, tap, dst, ALU.mult, ALU.add)
                    if j < CONV - 1:
                        st.link(last)
                last.then_inc(conv_done.sem, 1)
                decay_rate()

                dve.wait_ge(gate_tanh.sem, gate_tanh.at(l, LC))
                for c in range(LC):
                    last = v.tensor_scalar(tc[:, c, :], ta[:, c, :], 1.0, small[:, 6, c:c + 1], ALU.add, ALU.mult)
                last.then_inc(loga.sem, 1)
                st.link(v.scalar_tensor_tensor(tb, tb, 1.0, xc, ALU.add, ALU.mult))

                def page_index(pair, i, between=lambda: None):
                    dve.wait_ge(kp_used[i].sem, kp_used[i].at(l, pair + 1))
                    dve.wait_ge(idx_part.sem, idx_part.at(l, pair * 2 + i))
                    c16 = cbuf[0:HD, bass.ds(pair * 2 + i, 1), :].to_broadcast([HD, 2 * PAGES, 16])
                    v.scalar_tensor_tensor(relu[0:HD], ps[0:HD, 4 + i, :].rearrange("p (b c) -> p b c", c=16), 0.0,
                                           c16, ALU.max, ALU.mult).then_inc(id_read.sem, 1)
                    between()
                    dve.wait_ge(id_read.sem, id_read.at(l, pair * 2 + (i + 1)))
                    v.tensor_reduce(scT[0:HD, 0:2 * PAGES, bass.ds(pair * (2 * STEPS) + i * STEPS, STEPS)],
                                           relu[0:HD].rearrange("p b (h t) -> p b t h", t=STEPS), AX.X, ALU.add)\
                        .then_inc(idx_part.sem, 1)

                for i in range(2):
                    page_index(0, i)

                dve.wait_ge(decay.sem, decay.at(l, 1))
                st.link(v.tensor_tensor(tc, ta, ta, ALU.mult))
                v.scalar_tensor_tensor(th, tc, 1.0, th, ALU.add, ALU.mult).then_inc(radicand.sem, 1)
                gl = proj[:, GL:GL + LC, :]
                dve.wait_ge(radicand.sem, radicand.at(l, 1))
                st.link(v.tensor_tensor(tc, gl, gl, ALU.mult))
                st.link(v.tensor_scalar(tc, tc, GELU_C * 0.044715, GELU_C, ALU.mult, ALU.add))
                v.tensor_tensor(tc, tc, gl, ALU.mult).then_inc(gelu_in.sem, 1)
                dve.wait_ge(root_b.sem, root_b.at(l, 1))
                st.link(v.scalar_tensor_tensor(tb, tb, 0.5, th, ALU.mult, ALU.mult))
                tas, tbs = steps_of(ta[:, :, SEQ:T]), steps_of(tb[:, :, SEQ:T])
                before = state[:, ST_H:ST_H + LC * NSEQ].rearrange("p (c s) -> p c s", c=LC)
                for t in range(STEPS):
                    product_step = st.mark(v.tensor_tensor(xcs[:, :, :, t], tas[:, :, :, t], before, ALU.mult))
                    v.tensor_tensor_scan(xc[:, t, 0:SEQ], ta[:, t, 0:SEQ], tb[:, t, 0:SEQ], 0.0, ALU.mult, ALU.add)
                    st.need(product_step)
                    st.link(v.tensor_tensor(xcs[:, :, :, t], xcs[:, :, :, t], tbs[:, :, :, t], ALU.add))
                    before = xcs[:, :, :, t]
                v.tensor_copy(hout[:, :, 0:1], xc[:, :, SEQ - 1:SEQ])
                v.tensor_copy(hout[:, :, 1:NC_], xcs[:, :, :, STEPS - 1]).then_inc(outs_ready.sem, 1)
                dve.wait_ge(gelu_tanh.sem, gelu_tanh.at(l, 1))
                st.link(v.scalar_tensor_tensor(tc, tc, 1.0, gl, ALU.add, ALU.mult))
                v.scalar_tensor_tensor(y[:, 0:LC, :], tc, 0.5, xc, ALU.mult, ALU.mult).then_inc(arena_free.sem, 1)
                dve.wait_ge(arena_free.sem, arena_free.at(l, 1))

                v.tensor_copy(kd[HD:P, 0, :], proj[0:HD, KK, 0:SEQ])
                v.tensor_copy(kd[0:HD, 1, :], proj[HD:P, KK, 0:SEQ])
                v.tensor_copy(kd[HD:P, 2, :], proj[0:HD, KW, 0:SEQ]).then_inc(q_ready.sem, 1)
                v.tensor_copy(bias_p[:, 0, 0:P], tri)
                dve.wait_ge(idx_part.sem, idx_part.at(l, 2))
                dve.wait_ge(new_pe.sem, new_pe.at(l, 1))
                new = relu[0:NS, 0:NSEQ, :]
                st.link(v.scalar_tensor_tensor(new, ps[0:NS, 2, 0:NSEQ * 16].rearrange("p (s c) -> p s c", c=16), 0.0,
                                               cbuf[0:NS, :, :], ALU.max, ALU.mult))
                st.link(v.tensor_reduce(scT[0:NS, 2 * PAGES, :].rearrange("p (s t) -> p s t", t=STEPS),
                                        new.rearrange("p s (h t) -> p s t h", t=STEPS), AX.X, ALU.add))

                for k, (hd, i) in enumerate(DOTS):
                    span = (i + 1) * P
                    dve.wait_ge(relu_ready.sem, relu_ready.at(l, k + 1))
                    if hd == 0:
                        ins = v.tensor_scalar(bias_p[:, i, 0:span], work[k % 2][:, 0:span], wtok[:, i, hd:hd + 1], None,
                                              ALU.mult)
                    else:
                        dve.wait_ge(idx_sum.sem, idx_sum.at(l, k + 1 - (TILES - 1)))
                        ins = v.scalar_tensor_tensor(bias_p[:, i, 0:span], work[k % 2][:, 0:span],
                                                     wtok[:, i, hd:hd + 1], bias_p[:, i, 0:span], ALU.mult, ALU.add)
                    ins.then_inc(idx_sum.sem, 1)
                dve.wait_ge(idx_sum.sem, idx_sum.at(l, len(DOTS)))
                tiles = range(1, TILES)
                for i in tiles:
                    st.mark(v.tensor_tensor(bias_p[:, i, i * P:(i + 1) * P], bias_p[:, i, i * P:(i + 1) * P], tri,
                                            ALU.add))

                def top_rounds(rounds):
                    for _ in range(rounds):
                        for i in tiles:
                            st.need_hold(st.n + 1 - len(tiles))
                            st.mark(v.max(top8[:, i, :], bias_p[:, i, 0:(i + 1) * P]))
                        for i in tiles:
                            st.need_hold(st.n + 1 - len(tiles))
                            st.mark(v.match_replace(bias_p[:, i, 0:(i + 1) * P], top8[:, i, :],
                                                    bias_p[:, i, 0:(i + 1) * P], TAKEN))

                ROUNDS = SEL_P // 8
                in_loop = ROUNDS // (NSEQ // 2 - 1)
                with st.loop(NSEQ // 2 - 1, 6 * in_loop, start=1) as pair:
                    for i in range(2):
                        n = in_loop * (i + 1) // 2 - in_loop * i // 2
                        page_index(pair, i, between=lambda: top_rounds(n))
                top_rounds(ROUNDS - in_loop * (NSEQ // 2 - 1))
                st.need(st.n)
                for i in tiles:
                    st.mark(v.tensor_scalar(bias_p[:, i, 0:(i + 1) * P], bias_p[:, i, 0:(i + 1) * P], 0.5 * TAKEN, NEG,
                                            ALU.is_gt, ALU.mult))
                dve.wait_ge(scT_pe.sem, scT_pe.at(l, 1))
                v.tensor_copy(scS[:, 0:PAGES * P].rearrange("p (b k) -> p b k", b=4), ps[0:NS, 4:8, :])
                v.tensor_tensor(scS[:, PAGES * P:PAGES * P + NS], ps[0:NS, 2, 0:NS], mask_new, ALU.add)\
                    .then_inc(scS_ready.sem, 1)

                top_s = top8[0:NS, 0, :]

                def tile_output(i):
                    dve.wait_ge(pv_p.sem, pv_p.at(l, (i + 1) * HEADS))
                    dve.wait_ge(yt_pe.sem, yt_pe.at(l, i))
                    st.link(v.reciprocal(den[:, i % 2, :], den[:, i % 2, :]))
                    v.tensor_tensor(ytok.rearrange("p (h d) -> p h d", d=HD),
                                    ps[:, 2 + i % 2, :].rearrange("p (h d) -> p h d", d=HD),
                                    den[:, i % 2, :].unsqueeze(2).to_broadcast([P, HEADS, HD]), ALU.mult)\
                        .then_inc(o_read.sem, 1)

                assert SEL_S // 8 == TILES * HEADS
                for n in range(TILES * HEADS):
                    i, hd = divmod(n, HEADS)
                    span = (i + 1) * P
                    if n >= 2:
                        dve.wait_ge(t_pe.sem, t_pe.at(l, n - 1))
                    hold(dve, passed[3], s_pe.sem, s_pe.at(l, n + 1))
                    masked = st.mark(v.tensor_tensor_reduce(prob[n % 2][:, 0:span], ps[:, 4 + n % 2, 0:span],
                                                            bias_p[:, i, 0:span], 1.0, TAKEN, ALU.add, ALU.max,
                                                            nmax[:, hd:hd + 1]))
                    if n:
                        st.need_hold(replaced)
                    else:
                        hold(dve, passed[3], scS_ready.sem, scS_ready.at(l, 1))
                    found = st.mark(v.max(top_s, scS))
                    st.need(masked)
                    v.tensor_scalar(nmax[:, hd:hd + 1], nmax[:, hd:hd + 1], -(HD ** -0.5), None, ALU.mult)\
                        .then_inc(s_masked.sem, 1)
                    if i and hd == 1:
                        tile_output(i - 1)
                    if n and n % HEADS == 0:
                        ada_bias(5 + i - 1, K_ADA2 + i * RPF)
                    st.need_hold(found)
                    replaced = st.mark(v.match_replace(scS, top_s, scS, TAKEN))
                st.need(replaced)
                v.tensor_scalar(scS, scS, 0.5 * TAKEN, NEG, ALU.is_gt, ALU.mult).then_inc(topk_done.sem, 1)
                tile_output(TILES - 1)
                ada_bias(NMOD - 1, K_ADA2 + TILES * RPF)

                dve.wait_ge(mT_pe.sem, mT_pe.at(l, 1))
                v.tensor_copy(maskT[:, 0:PAGES, :], ps[:, 4, :].rearrange("p (j c) -> p j c", c=NS))
                st.link(v.tensor_copy(maskT[0:NS, PAGES, :], ps[0:NS, 5, 0:NS]))
                for s in range(NSEQ):
                    m4 = maskT[:, 0:PAGES, s * STEPS:(s + 1) * STEPS].unsqueeze(2)\
                        .to_broadcast([P, PAGES, HEADS, STEPS])
                    dst = sT3[:, s, 0:PAGES, :].rearrange("p j (h t) -> p j h t", t=STEPS)
                    v.tensor_tensor(dst, dst, m4, ALU.add)
                dst = sT3[0:NS, :, PAGES, :].rearrange("p s (h t) -> p s h t", t=STEPS)
                st.link(v.tensor_tensor(dst, dst, maskT[0:NS, PAGES, :].rearrange("p (s t) -> p s t", t=STEPS).unsqueeze(2)
                                        .to_broadcast([NS, NSEQ, HEADS, STEPS]), ALU.add))
                mx3, mxa3 = (m.rearrange("p (s c) -> p s c", s=NSEQ) for m in (mx, mxa))
                v.tensor_reduce(mx3, sT3.rearrange("p s j c -> p s c j"), AX.X, ALU.max).then_inc(max_in.sem, 1)
                dve.wait_ge(pool_max.sem, pool_max.at(l, 1))
                v.tensor_tensor(sT3, sT3, mxa3.unsqueeze(2).to_broadcast([P, NSEQ, NB, 32]), ALU.subtract)\
                    .then_inc(sub_done.sem, 1)
                dve.wait_ge(exp_s.sem, exp_s.at(l, 1))
                v.tensor_reduce(mx3, sT3.rearrange("p s j c -> p s c j"), AX.X, ALU.add).then_inc(sums.sem, 1)
                dve.wait_ge(den_pe.sem, den_pe.at(l, 1))
                st.link(v.reciprocal(rden, ps[:, 6, 0:NSEQ * 32]))
                dve.wait_ge(pv_s.sem, pv_s.at(l, NSEQ))
                for hd in range(HEADS):
                    half, kv = hd % 2, hd // (HEADS // NKV)
                    src = slice(kv * HD, (kv + 1) * HD)
                    last = v.tensor_tensor(
                        y[half * HD:(half + 1) * HD, LC + hd // 2, SEQ:T].rearrange("p (s t) -> p s t", t=STEPS),
                        ps[src, 7, 0:NSEQ * 32].rearrange("p (s c) -> p s c", s=NSEQ)[:, :, hd * STEPS:(hd + 1) * STEPS],
                        rden[src, :].rearrange("p (s c) -> p s c", s=NSEQ)[:, :, hd * STEPS:(hd + 1) * STEPS], ALU.mult)
                last.then_inc(ysample.sem, 1)

                residual(1, 3, 5, 1.0)
                pre_norm(2, 4, 7, 6)
                swiglu(1, K_GU2)
                residual(2, 5, 8, 0.5)
                dve.sem_inc(vec_free.sem, 1)
                dve.wait_ge(kv_stored.sem, kv_stored.at(l, 3))
                dve.wait_ge(states_stored.sem, states_stored.at(l, 2))
                assert st.n == DVE_STEPS, st.n


def rope_tables():
    half = HD // 8
    freqs = np.float32(500000.0) ** (-(np.arange(half, dtype=np.float32) / np.float32(half)))
    pos = np.concatenate([np.arange(SEQ), np.tile(PAGES * PAGE + np.arange(STEPS), NSEQ)]).astype(np.float32)
    ang = freqs.astype(np.float32)[:, None] * pos[None, :]
    cos, sin = np.ones((HD, T), np.float32), np.zeros((HD, T), np.float32)
    cos[0:half] = cos[half:2 * half] = np.cos(ang)
    sin[0:half], sin[half:2 * half] = -np.sin(ang), np.sin(ang)
    return np.tile(cos, (2, 1)), np.tile(sin, (2, 1))


def constants():
    c = np.zeros((P, C_ALL), np.float32)
    c[:, C_ID:C_ID + P] = np.eye(P)
    c[:, C_ONE:C_ONE + P] = 1.0
    half = HD // 8
    for b in (0, HD):
        for r in range(half):
            c[b + half + r, C_SWAP + b + r] = c[b + r, C_SWAP + b + half + r] = 1.0
    c[:, C_COS:C_COS + T], c[:, C_SIN:C_SIN + T] = rope_tables()
    c[:, C_TRI:C_TRI + P] = np.where(np.arange(P)[None, :] <= np.arange(P)[:, None], 0.0, NEG)
    s, t = np.divmod(np.arange(NS), STEPS)
    c[0:NS, C_MS:C_MS + NS] = np.where((s[None, :] == s[:, None]) & (t[None, :] <= t[:, None]), 0.0, NEG)
    for hd in range(IH):
        c[HD + hd, C_SEL + hd * P:C_SEL + (hd + 1) * P] = 1.0
    return c


def by_partition(a, lead):
    s = a.shape
    a = a.reshape(*s[:lead], s[lead] // P, P, *s[lead + 1:])
    return np.ascontiguousarray(np.swapaxes(a, lead, lead + 1))


OUTS = {"yT": (P, DC, T), "kT": (DEPTH, P, T), "vT": (DEPTH, P, T), "kiT": (DEPTH, HD, T),
        "convT": (DEPTH, P, LC, 3 * NC_), "hT": (DEPTH, P, LC, NC_)}


def kernel(**inputs):
    import concourse.bacc as bacc
    from concourse.bass_utils import run_bass_kernel_spmd

    i = {k: np.asarray(v) for k, v in inputs.items()}
    flat = i["x_sample"].reshape(NS, D)
    feat = lambda v: by_partition(v.reshape(DEPTH, -1, P).transpose(0, 1, 2).reshape(DEPTH, -1), 1)
    arrays = {
        "cst": constants(),
        "xT": by_partition(np.concatenate([i["x_prompt"][0], flat]).T, 0),
        "cT": by_partition(np.concatenate([i["c_prompt"], i["c_sample"]]).T, 0),
        "page_table": i["page_table"].reshape(1, -1),
        "vec": np.concatenate([feat(i[k]) for k in ("b_ada", "norm_g", "conv_w", "conv_b", "lru_ba", "lru_bx",
                                                    "lru_lambda")], axis=2),
        "state": np.concatenate([
            by_partition(i["state_h"].transpose(0, 2, 1), 1).reshape(DEPTH, P, -1),
            by_partition(i["state_conv"].transpose(0, 3, 1, 2), 1).reshape(DEPTH, P, -1)], axis=2),
        "key_pages": np.concatenate([
            i["cache_k"].reshape(DEPTH, POOL, PAGE, P).transpose(0, 1, 3, 2),
            i["cache_kidx"].reshape(DEPTH, POOL, 2, PAGE // 2, HD).transpose(0, 1, 2, 4, 3)
            .reshape(DEPTH, POOL, P, PAGE // 2)], axis=3),
        "v_cache": i["cache_v"].reshape(DEPTH, POOL, PAGE, P),
    }
    arrays |= {k: i[k] for k in ("w_ada", "ffn_w_gu", "ffn_w_down", "w_in", "w_out", "lru_wa", "lru_wx")}
    nc = bacc.Bacc("TRN2", target_bir_lowering=False, num_devices=1)
    arrays = {k: np.ascontiguousarray(v) for k, v in arrays.items()}
    a = {k: nc.dram_tensor(k, v.shape, mybir.dt.from_np(v.dtype), kind="ExternalInput").ap() for k, v in arrays.items()}
    a |= {k: nc.dram_tensor(k, s, F32, kind="ExternalOutput").ap() for k, s in OUTS.items()}
    decoder(nc, a)
    r = run_bass_kernel_spmd(nc, [arrays], core_ids=[0]).results[0]

    def tokens(v):
        return v.transpose(2, 1, 0).reshape(v.shape[2], -1)

    y = tokens(r["yT"])
    k, v, ki = (r[n].transpose(0, 2, 1) for n in ("kT", "vT", "kiT"))
    heads = lambda t, lead: t.reshape(*lead, NKV, HD)
    hT = r["hT"].transpose(0, 3, 2, 1).reshape(DEPTH, NC_, -1)
    conv = r["convT"].reshape(DEPTH, P, LC, NC_, 3).transpose(0, 3, 4, 2, 1).reshape(DEPTH, NC_, 3, -1)
    outs = (y[:SEQ].reshape(1, SEQ, D), y[SEQ:].reshape(NSEQ, STEPS, D),
            heads(k[:, :SEQ], (DEPTH, 1, SEQ)), heads(v[:, :SEQ], (DEPTH, 1, SEQ)), ki[:, :SEQ].reshape(DEPTH, 1, SEQ, HD),
            hT[:, 0:1], conv[:, 0:1],
            heads(k[:, SEQ:], (DEPTH, NSEQ, STEPS)), heads(v[:, SEQ:], (DEPTH, NSEQ, STEPS)),
            ki[:, SEQ:].reshape(DEPTH, NSEQ, STEPS, HD), hT[:, 1:], conv[:, 1:])
    return tuple(np.ascontiguousarray(o) for o in outs)
```

```python
from contextlib import ExitStack, contextmanager

import numpy as np

import concourse.bass as bass
from concourse import mybir

F32 = mybir.dt.float32
F32R = mybir.dt.float32r
I32 = mybir.dt.int32
ALU = mybir.AluOpType
ACT = mybir.ActivationFunctionType
AX = mybir.AxisListType
RMAX = bass.bass_isa.ReduceOp.max

P = 128
DEPTH, D, SEQ, NSEQ, STEPS = 2, 1024, 512, 8, 4
NS = NSEQ * STEPS
T = SEQ + NS
TH = T // 2
DC = D // P
D_FF = 2816
FC = D_FF // P
LC = 4
CONV = 4
HEADS, HD, NKV = 8, 64, 2
IH = 4
NMOD = 9
NC_ = 1 + NSEQ
MC = NMOD * DC
IN_COLS = 2116
PC = IN_COLS // P
LAST = IN_COLS - PC * P
XL, GL, QQ, KK, VV, QI, KW = 0, 4, 8, 12, 13, 14, 16
PAGES, PAGE, POOL = 16, 128, 160
NB = PAGES + 1
TILES = SEQ // P
SEL_P, SEL_S = 128, 256
EPS = 1e-6
NEG = -1.0e30
TAKEN = -3.0e38
ROPED = [QQ, QQ + 1, QQ + 2, QQ + 3, KK, QI, QI + 1, KW]
GELU_C = float(np.sqrt(2.0 / np.pi))
SW = 3 + STEPS
XPW = 3 + SEQ + NSEQ * SW

C_ID, C_ONE, C_SWAP, C_COS, C_SIN = 0, P, 2 * P, 3 * P, 3 * P + T
C_TRI = C_SIN + T
C_MS = C_TRI + P
C_SEL = C_MS + NS
C_ALL = C_SEL + IH * P
V_BADA, V_G, V_CW, V_CB, V_BA, V_BX, V_LAM = 0, 72, 120, 136, 140, 144, 148
V_ALL = 152
ST_H, ST_C, ST_ALL = 0, LC * NSEQ, LC * NSEQ * 4

RING = 4
RPF = DC // RING
U_GU = FC // 2
DN_K = (8, 8, 6)


class Phase:
    full = [0] * RING
    ada = [0] * RING
    split = [0] * RING
    used = [0, 0]
    order = 0

    def __init__(self, rounds, per_round, slots, is_ada=False, tail=0):
        self.rounds, self.per_round, self.slots, self.tail = rounds, per_round, slots, tail
        self.full0, self.ada0, self.split0 = list(Phase.full), list(Phase.ada), list(Phase.split)
        self.used0, self.order0 = list(Phase.used), Phase.order
        for n in range(rounds * per_round + tail):
            i = n % slots
            Phase.full[i] += 1
            (Phase.ada if is_ada else Phase.split)[i] += 1
            if not is_ada:
                Phase.used[n % 2] += 1
                Phase.order += 1

    def has(self, u, n):
        return u * self.per_round + n < self.rounds * self.per_round + self.tail

    def raw(self, u, n):
        return n % self.slots, u * (self.per_round // self.slots) + n // self.slots

    def part(self, u, n):
        return n % 2, u * (self.per_round // 2) + n // 2


ADA0 = Phase(2 * RPF, RING, RING, is_ada=True)
GU1 = Phase(U_GU, RING, RING)
ADA1 = Phase(3 * RPF, RING, RING, is_ada=True)
DN1 = Phase(DC // 2, 2 * len(DN_K), len(DN_K))
IN = Phase(PC // RING, RING, RING, tail=1)
ADA2 = Phase(4 * RPF, RING, RING, is_ada=True)
OUT = Phase(DC // RING, RING, RING)
GU2 = Phase(U_GU, RING, RING)
DN2 = Phase(DC // 2, 2 * len(DN_K), len(DN_K))
PAGE_UNROLL = 4
ARENA = FC * T + 2048
D_USES = DC
KREC = PAGE + PAGE // 2

DVE_STEPS = 352



class Signal:

    def __init__(self, ctx, nc, name, per, unit=1, start=0):
        self.sem = ctx.enter_context(nc.semaphore(name))
        self.per, self.unit, self.start = per, unit, start

    def at(self, layer, k):
        return layer * (self.per * self.unit) + (k * self.unit + self.start)


def hold(eng, passed, sem, value):
    eng.wait_ge(sem, value)
    eng.sem_inc(passed, 1)


class Steps:

    def __init__(self, eng, sem, per, layer, passed):
        self.passed = passed
        self.eng, self.sem, self.per, self.layer, self.n, self.shift = eng, sem, per, layer, 0, 0

    def mark(self, ins):
        self.n += 1
        ins.then_inc(self.sem, 1)
        return self.n

    def need(self, n):
        self.eng.wait_ge(self.sem, self.layer * self.per + (n + self.shift))

    def need_hold(self, n):
        hold(self.eng, self.passed, self.sem, self.layer * self.per + (n + self.shift))

    def link(self, ins):
        self.need(self.mark(ins))

    def link_hold(self, ins):
        self.need_hold(self.mark(ins))

    @contextmanager
    def loop(self, times, body_steps, start=0):
        first = self.n
        with self.eng.Fori(start, start + times) as i:
            self.shift = i * body_steps + (-start * body_steps)
            yield i
        assert self.n - first == body_steps, (self.n - first, body_steps)
        self.n = first + times * body_steps
        self.shift = 0


def decoder(nc, a):
    with ExitStack() as ctx:
        def sb(name, shape, dt=F32):
            return ctx.enter_context(nc.sbuf_tensor("sb_" + name, shape, dt))

        def sig(name, per, unit=1, start=0):
            return Signal(ctx, nc, name, per, unit, start)

        ps = ctx.enter_context(nc.psum_tensor("ps", [P, 8, 512], F32))

        x = sb("x", [P, DC, T])
        rinv = sb("rinv", [P, T])
        wslot = [sb(f"wslot{i}", [P, DC, P]) for i in range(RING)]
        widths = (DC * T, ARENA, (PC + 1) * T, DC * T, 2 * PAGES * KREC)
        at_h, at_arena, at_proj, at_y, at_down = (sum(widths[:n]) for n in range(5))
        region_at = nc.sbuf_base
        h = sb("h", [P, DC, T])
        arena = sb("arena", [P, ARENA])
        proj = sb("proj", [P, PC + 1, T])
        y = sb("y", [P, DC, T])
        down = sb("down", [P, 2 * PAGES * KREC])
        assert nc.sbuf_base == region_at + 4 * sum(widths)

        def part(name, offset, *shape, dt=F32R):
            return nc.alloc_sbuf_tensor_at("sb_" + name, [P, *shape], dt, offset=region_at + 4 * offset)

        act_hi = part("act_hi", at_arena, FC, T)
        at_whi = at_arena + FC * T
        w_hi = [part(f"w_hi{i}", at_whi + i * DC * P, DC, P) for i in range(2)]
        h_hi = part("h_hi", at_proj, DC, T)
        h_lo = part("h_lo", at_h, DC, T)
        at_wlo = at_proj + DC * T
        w_lo_ffn = [part(f"w_lo_ffn{i}", at_wlo + i * DC * P, DC, P) for i in range(2)]
        at_tsil = at_wlo + 2 * DC * P
        at_alo = at_down + 2 * PAGES * KREC - FC * T
        assert at_tsil + 2 * T <= at_alo and at_whi + 2 * DC * P <= at_proj
        act_lo = part("act_lo", at_alo, FC, T)
        h_hi_mid = part("h_hi_mid", at_y, DC, T)
        y_hi = part("y_hi", at_arena, DC, T)
        y_lo = part("y_lo", at_y, DC, T)
        w_lo_mid = [part(f"w_lo_mid{i}", at_whi - (2 - i) * DC * P, DC, P) for i in range(2)]
        cst = sb("cst", [P, C_ALL])
        vec = sb("vec", [P, V_ALL])
        state = sb("state", [P, ST_ALL])
        cT = sb("cT", [P, DC, NC_])
        mod = sb("mod", [P, MC, NC_])
        modT = sb("modT", [NC_, DC, P])
        gain = sb("gain", [P, DC, NC_])
        pages = sb("pages", [1, NSEQ * PAGES], I32)
        gates = sb("gates", [P, 2, LC, P])
        small = sb("small", [P, 12, LC])
        eps = sb("eps", [P, 1])
        hout = sb("hout", [P, LC, NC_])
        cout = sb("cout", [P, LC, 3 * NC_])

        sq = proj[:, 0:DC, :]
        tsil = part("tsil", at_tsil, 2, T, dt=F32)
        rtmp = [y[:, DC - 1, :], y[:, DC - 2, :]]

        ident, ones, swap = cst[:, C_ID:C_ID + P], cst[:, C_ONE:C_ONE + P], cst[:, C_SWAP:C_SWAP + P]
        cosT, sinT, tri = cst[:, C_COS:C_COS + T], cst[:, C_SIN:C_SIN + T], cst[:, C_TRI:C_TRI + P]
        mask_new = cst[0:NS, C_MS:C_MS + NS]
        sel = cst[:, C_SEL:C_SEL + IH * P].rearrange("p (h m) -> p h m", h=IH)

        at = [0]

        def carve(*shape):
            n = int(np.prod(shape))
            v = arena[:, at[0]:at[0] + n]
            at[0] += n
            if len(shape) == 2:
                v = v.rearrange("p (a b) -> p a b", a=shape[0])
            if len(shape) == 3:
                v = v.rearrange("p (a b c) -> p a b c", a=shape[0], b=shape[1])
            return v

        xp, xc, tc = carve(LC, XPW), carve(LC, T), carve(LC, T)
        ta, tb = y[:, 0:LC, :], y[:, LC:DC, :]
        th = xp[:, :, 0:T]
        lru_end, at[0] = at[0], 0
        kd = carve(3, SEQ)
        bias_p = carve(TILES, SEQ)
        arena_v = [carve(PAGES, PAGE) for _ in range(3)]
        assert at[0] >= lru_end
        top8 = carve(4, 8)
        nmax = carve(HEADS)
        den = carve(2, HEADS)
        cbuf = carve(NSEQ, 16)
        qiS = carve(NSEQ, 2, 16)
        qS = carve(NSEQ, 32)
        vtok = carve(TILES + 1, P)
        wtok = carve(TILES, IH)
        rden = carve(NSEQ * 32)
        mxa = rden
        at_common = at[0]
        scT = carve(2 * PAGES + 1, NS)
        relu = carve(2 * PAGES, 16)
        work = [carve(SEQ) for _ in range(2)]
        assert at[0] <= ARENA, (at[0], ARENA)
        at[0] = at_common
        o_sample = arena[:, at_common:at_common + NSEQ * P].rearrange("p (s d) -> p s d", s=NSEQ)
        prob = [carve(SEQ) for _ in range(2)]
        probT = [carve(SEQ) for _ in range(2)]
        ytok = carve(SEQ)
        assert at[0] <= ARENA, (at[0], ARENA)
        maskT = rinv[:, :].rearrange("p (j c) -> p j c", c=NS)
        kpage = [down[:, i * PAGES * KREC:(i + 1) * PAGES * KREC].rearrange("p (j n) -> p j n", j=PAGES)
                 for i in range(2)]
        pflat = proj[:, 0:8, :].rearrange("p a b -> p (a b)")
        in_proj = [pflat[:, i * 2048:(i + 1) * 2048].rearrange("p (j n) -> p j n", j=PAGES) for i in range(2)]
        in_down = [down[:, i * 2048:(i + 1) * 2048].rearrange("p (j n) -> p j n", j=PAGES) for i in range(3)]
        vpage = in_proj + arena_v + in_down
        V_POOL = 5
        mx = pflat[:, 4096:4096 + NSEQ * 32]
        sT = h[:, :, :].rearrange("p a b -> p (a b)")
        sT3 = sT.rearrange("p (s j c) -> p s j c", s=NSEQ, j=NB)
        scS = y[0:NS, LC:DC, :].rearrange("p a b -> p (a b)")[:, 0:PAGES * P + NS]

        s_in = sig("s_in", 0)
        w_full = [sig(f"w_full{i}", Phase.full[i], 16) for i in range(RING)]
        ada_used = [sig(f"ada_used{i}", Phase.ada[i]) for i in range(RING)]
        w_hi_done = sig("w_hi_done", Phase.order)
        w_split = [sig(f"w_split{i}", Phase.split[i]) for i in range(RING)]
        w_used = [sig(f"w_used{i}", Phase.used[i]) for i in range(2)]
        vec_full = sig("vec_full", 2, 16)
        vec_free = sig("vec_free", 1, 1, 1)
        gate_full = sig("gate_full", 16, 16)
        KEYS_SP = 8
        kp_full = [sig(f"kp_full{i}", 4 * KEYS_SP, 16) for i in range(2)]
        kp_full_pool = [sig(f"kp_full_pool{i}", 4 * (PAGES - KEYS_SP), 16) for i in range(2)]
        kp_used = [sig(f"kp_used{i}", 4, 1, 1) for i in range(2)]
        vp_full = [sig(f"vp_full{i}", PAGES, 16) for i in range(NSEQ)]
        pv_s = sig("pv_s", NSEQ)
        pv_copied = sig("pv_copied", 2)
        pv_t = sig("pv_t", 1)
        arena_free = sig("arena_free", 1)
        modT_ready = sig("modT_ready", 2 * NMOD)
        mod_pe = sig("mod_pe", NMOD)
        ada_read = sig("ada_read", NMOD, 1, 1)
        ss_ready = sig("ss_ready", 6)
        sq_ready = sig("sq_ready", 3 * DC)
        root_ready = sig("root_ready", 6)
        xn_ready = sig("xn_ready", 3 * DC)
        h_act = sig("h_act", 3 * DC)
        tanh_ready = sig("tanh_ready", 2 * FC)
        act_raw = sig("act_raw", 2 * FC)
        act_hi_done = sig("act_hi_done", 2 * FC)
        h_parts = sig("h_parts", 3 * DC)
        y_hi_done = sig("y_hi_done", 2)
        y_parts = sig("y_parts", 1)
        act_ready = sig("act_ready", 2 * FC, 1, 2)
        dn_read = sig("dn_read", 2 * DC, 1, 2)
        res_done = sig("res_done", 3, 1, 1)
        pj_read = sig("pj_read", PC + 1, 1, 2)
        sw_ready = sig("sw_ready", 8)
        rope_done = sig("rope_done", 8)
        tok_pe = sig("tok_pe", 1)
        tok_read = sig("tok_read", 1)
        qs_ready = sig("qs_ready", 1)
        conv_done = sig("conv_done", 1)
        gz_ready = sig("gz_ready", LC)
        lam_in = sig("lam_in", 1)
        lam_exp = sig("lam_exp", 1)
        gate_tanh = sig("gate_tanh", LC, 1, 1)
        loga = sig("loga", 1)
        decay = sig("decay", 1)
        radicand = sig("radicand", 1)
        root_b = sig("root_b", 1)
        gelu_in = sig("gelu_in", 1)
        gelu_tanh = sig("gelu_tanh", 1)
        outs_ready = sig("outs_ready", 2)
        kv_stored = sig("kv_stored", 3, 16)
        states_stored = sig("states_stored", 2, 16)
        id_read = sig("id_read", NSEQ, 1, 2)
        ks_read = sig("ks_read", NSEQ, 1, 2)
        new_pe = sig("new_pe", 1)
        q_ready = sig("q_ready", 1)
        dots = sig("dots", (TILES - 1) * IH)
        relu_ready = sig("relu_ready", (TILES - 1) * IH, 1, 2)
        idx_sum = sig("idx_sum", (TILES - 1) * IH, 1, 2)
        idx_part = sig("idx_part", NSEQ, 1, 1)
        scT_pe = sig("scT_pe", 1)
        scS_ready = sig("scS_ready", 1)
        s_pe = sig("s_pe", TILES * HEADS)
        s_masked = sig("s_masked", TILES * HEADS, 1, 2)
        s_exp = sig("s_exp", TILES * HEADS)
        t_pe = sig("t_pe", TILES * HEADS)
        t_read = sig("t_read", TILES * HEADS, 1, 2)
        pv_p = sig("pv_p", TILES * HEADS)
        o_read = sig("o_read", TILES, 1, 2)
        yt_pe = sig("yt_pe", TILES)
        yt_read = sig("yt_read", TILES, 1, 1)
        topk_done = sig("topk_done", 1)
        mT_pe = sig("mT_pe", 1)
        yp_done = sig("yp_done", 1)
        max_in = sig("max_in", 1)
        pool_max = sig("pool_max", 1)
        sub_done = sig("sub_done", 1)
        exp_s = sig("exp_s", 1)
        sums = sig("sums", 1)
        den_pe = sig("den_pe", 1)
        ysample = sig("ysample", 1)
        wo_read = sig("wo_read", DC, 1, 2)
        dve_step = ctx.enter_context(nc.semaphore("dve_step"))
        eps_ready = sig("eps_ready", 0)
        cleared = sig("cleared", 0)
        passed = [ctx.enter_context(nc.semaphore(f"passed_{e}")) for e in ("sp", "pe", "pool", "dve")]
        y_out = sig("y_out", 0)
        DOTS = [(hd, i) for hd in range(IH) for i in range(1, TILES)]

        block = ctx.enter_context(nc.Block())

        def halves(pair):
            return ps[:, 2 * pair:2 * pair + 2, 0:TH]

        def tok2(v):
            return v.rearrange("p (b t) -> p b t", b=2)

        def layer_of(ap, l):
            return ap[bass.ds(l, 1)]

        def load_page(eng, tensor, l, seq_page, dst, full):
            page = eng.value_load(pages[0:1, bass.ds(seq_page, 1)], min_val=0, max_val=POOL - 1)
            src = layer_of(tensor, l)[:, bass.ds(page, 1)].rearrange("a b p n -> (a b p) n")
            eng.dma_start(dst.rearrange("p a n -> p (a n)"), src).then_inc(full.sem, 16)

        def load_pages(eng, tensor, l, seq_page, first, after, buf, full):
            with eng.Fori(0, (after - first) // PAGE_UNROLL) as j:
                for n in range(PAGE_UNROLL):
                    k = j * PAGE_UNROLL + (first + n)
                    load_page(eng, tensor, l, seq_page + k, buf[:, bass.ds(k, 1), :], full)

        def key_loads(eng, on_sp, l, pair):
            who, first, after, full = ((passed[0], 0, KEYS_SP, kp_full) if on_sp
                                       else (passed[2], KEYS_SP, PAGES, kp_full_pool))
            if isinstance(pair, int):
                hold(eng, who, dn_read.sem, dn_read.at(l, DC))
            for i in range(2):
                hold(eng, who, kp_used[i].sem, kp_used[i].at(l, pair))
                load_pages(eng, a["key_pages"], l, pair * (2 * PAGES) + i * PAGES, first, after, kpage[i], full[i])

        @block.sync
        def _(sp):
            sp.dma_start(cT[:, :, :], a["cT"]).then_inc(s_in.sem, 16)
            sp.dma_start(x[:, :, :], a["xT"]).then_inc(s_in.sem, 16)
            sp.dma_start(cst[:, :], a["cst"]).then_inc(s_in.sem, 16)
            sp.dma_start(pages[:, :], a["page_table"]).then_inc(s_in.sem, 16)
            sp.wait_ge(s_in.sem, 64)
            sp.wait_ge(cleared.sem, 1)
            with sp.Fori(0, DEPTH) as l:

                def rows(ap):
                    return ap.rearrange("a (c p) n -> p (a c) n", p=P)

                ada, w_in, w_out = (layer_of(a[n], l) for n in ("w_ada", "w_in", "w_out"))

                def piece(ph, u, n, src):
                    i, k = ph.raw(u, n)
                    is_ada = ph in (ADA0, ADA1, ADA2)
                    before = (ph.ada0[i], k + ph.split0[i]) if not is_ada else (k + ph.ada0[i], ph.split0[i])
                    hold(sp, passed[0], ada_used[i].sem, ada_used[i].at(l, before[0]))
                    sp.wait_ge(w_split[i].sem, w_split[i].at(l, before[1]))
                    sp.dma_start(wslot[i][:, 0:src.shape[1], 0:src.shape[2]], src).then_inc(w_full[i].sem, 16)

                def pieces(ph, src, first=0, start=0, rounds=None):
                    with sp.Fori(start, start + (rounds or ph.rounds)) as u:
                        for n in range(RING):
                            piece(ph, u, n, rows(src[:, :, bass.ds(u * (RING * P) + (first + n) * P, P)]))

                def ffn_loads(f, gu_ph, dn_ph, between):
                    gu = layer_of(a["ffn_w_gu"], l)[:, f]
                    dn = layer_of(a["ffn_w_down"], l)[:, f]
                    with sp.Fori(0, U_GU) as u:
                        for n in range(RING):
                            piece(gu_ph, u, n,
                                  rows(gu[:, :, bass.ds(u * (2 * P) + (n // 2) * P + (n % 2) * D_FF, P)]))
                    between()
                    with sp.Fori(0, DC // 2) as u:
                        for n in range(2 * len(DN_K)):
                            m, j = divmod(n, len(DN_K))
                            k0 = sum(DN_K[:j]) * P
                            piece(dn_ph, u, n,
                                  rows(dn[:, k0:k0 + DN_K[j] * P, bass.ds(u * (2 * P) + m * P, P)]))

                sp.wait_ge(vec_free.sem, vec_free.at(l, 0))
                sp.dma_start(vec[:, :], layer_of(a["vec"], l).rearrange("a p n -> (a p) n")).then_inc(vec_full.sem, 16)
                sp.dma_start(state[:, :], layer_of(a["state"], l).rearrange("a p n -> (a p) n")).then_inc(vec_full.sem, 16)
                pieces(ADA0, ada)
                ffn_loads(0, GU1, DN1, lambda: pieces(ADA1, ada, first=2 * DC))
                sp.wait_ge(gate_tanh.sem, gate_tanh.at(l, 0))
                for g, name in enumerate(("lru_wa", "lru_wx")):
                    for b in range(8):
                        half = (b % 2) * HD
                        sp.dma_start(gates[half:half + HD, g, b // 2, half:half + HD],
                                     layer_of(a[name], l)[:, b].rearrange("a i j -> (a i) j")).then_inc(gate_full.sem, 16)
                pieces(IN, w_in)
                piece(IN, PC // RING, 0, rows(w_in[:, :, PC * P:IN_COLS]))
                key_loads(sp, True, l, 0)
                sp.wait_ge(rope_done.sem, rope_done.at(l, 8))
                hold(sp, passed[0], pj_read.sem, pj_read.at(l, PC + 1))
                for name, c, n in (("kT", KK, P), ("vT", VV, P), ("kiT", KW, HD)):
                    sp.dma_start(layer_of(a[name], l).rearrange("a p t -> (a p) t"), proj[0:n, c, :])\
                        .then_inc(kv_stored.sem, 16)
                with sp.Fori(1, NSEQ // 2) as pair:
                    key_loads(sp, True, l, pair)
                pieces(ADA2, ada, first=5 * DC, rounds=RPF)
                sp.wait_ge(kp_used[0].sem, kp_used[0].at(l, 4))
                hold(sp, passed[0], kp_used[1].sem, kp_used[1].at(l, 4))
                for n, s in enumerate(range(V_POOL, NSEQ)):
                    load_pages(sp, a["v_cache"], l, s * PAGES, 0, PAGES, vpage[s], vp_full[s])
                    pieces(ADA2, ada, first=5 * DC, start=(n + 1) * RPF, rounds=RPF)
                pieces(OUT, w_out)
                ffn_loads(1, GU2, DN2, lambda: None)
            sp.wait_ge(res_done.sem, res_done.at(DEPTH - 1, 3))
            sp.dma_start(a["yT"], x[:, :, :]).then_inc(y_out.sem, 16)
            sp.wait_ge(y_out.sem, 16)
            sp.wait_ge(kv_stored.sem, kv_stored.at(DEPTH - 1, 3))
            sp.wait_ge(states_stored.sem, states_stored.at(DEPTH - 1, 2))

        @block.tensor
        def _(pe):
            mm = nc.tensor.matmul
            l_ = [None]

            def sums_of_squares(squares, l, k):
                for c in range(DC):
                    pe.wait_ge(squares.sem, squares.at(l, k + c + 1))
                    for b in range(2):
                        last = mm(ps[:, 6 + b, 0:TH], ones, sq[:, c, b * TH:(b + 1) * TH],
                                  start=(c == 0), stop=(c == DC - 1))
                last.then_inc(ss_ready.sem, 1)

            def product(pair, weights, moving):
                n = len(weights)
                m = weights[0].shape[-1]
                for b in range(2):
                    for kc in range(n):
                        last = mm(ps[0:m, 2 * pair + b, 0:TH], weights[kc], moving[kc][:, b * TH:(b + 1) * TH],
                                  start=(kc == 0), stop=(kc == n - 1))
                return last

            def piece(ph, u, n, pair, w_lo, hi, lo, k0=0, k1=DC, of=DC, norm=None):
                i, k = ph.raw(u, n)
                s, m = ph.part(u, n)
                pe.wait_ge(w_split[i].sem, w_split[i].at(l_[0], k + (ph.split0[i] + 1)))
                for b in range(2):
                    for kc in range(k0, k1):
                        wh, wl = w_hi[s][:, kc - k0, :], w_lo[s][:, kc - k0, :]
                        if norm is not None and b == 0 and kc % 2 == 0:
                            pe.wait_ge(h_parts.sem, h_parts.at(l_[0], norm * DC + kc + 2))
                        xh, xl = (v[:, kc, b * TH:(b + 1) * TH] for v in (hi, lo))
                        out = ps[:, 2 * pair + b, 0:TH]
                        mm(out, wh, xh, start=(kc == 0), stop=False)
                        mm(out, wh, xl, start=False, stop=False)
                        last = mm(out, wl, xh, start=False, stop=(kc == of - 1))
                last.then_inc(w_used[s].sem, 1)

            def ada_chunk(l, ph, use, m, bank):
                r, i = divmod(m, RING)
                pe.wait_ge(w_full[i].sem, w_full[i].at(l, use + (r + 1 + ph.full0[i])))
                for kc in range(DC):
                    last = mm(ps[0:NC_, bank, i * P:(i + 1) * P], cT[:, kc, :], wslot[i][:, kc, :],
                              start=(kc == 0), stop=(kc == DC - 1))
                last.then_inc(ada_used[i].sem, 1)

            def ada_transposes(l, g, bank):
                for half in range(2):
                    hold(pe, passed[1], modT_ready.sem, modT_ready.at(l, g * 2 + (half + 1)))
                    for m in range(half * RING, (half + 1) * RING):
                        last = nc.tensor.transpose(ps[:, bank, m * NC_:(m + 1) * NC_], modT[:, m, :],
                                                   ident[0:NC_, 0:NC_])
                last.then_inc(mod_pe.sem, 1)

            def ada(l, ph, first, after):
                with pe.Fori(first, after) as g:
                    for m in range(DC):
                        ada_chunk(l, ph, g * RPF + (-first * RPF), m, m // RING)
                    pe.wait_ge(ada_read.sem, ada_read.at(l, g))
                    ada_transposes(l, g, 2)
                hold(pe, passed[1], ada_read.sem, ada_read.at(l, after))

            def ffn(l, f, gu_ph, dn_ph, between):
                with pe.Fori(0, U_GU) as u:
                    for n in range(RING):
                        k = u * 2 + (f * FC + n // 2)
                        if n % 2 == 0:
                            pe.wait_ge(act_ready.sem, act_ready.at(l, k + 1 - 2))
                        piece(gu_ph, u, n, n, w_lo_ffn, h_hi, h_lo, norm=2 * f if n == 0 else None)
                hold(pe, passed[1], act_ready.sem, act_ready.at(l, (f + 1) * FC - 1))
                between()
                hold(pe, passed[1], act_ready.sem, act_ready.at(l, (f + 1) * FC))
                with pe.Fori(0, DC // 2) as u:
                    for n in range(2 * len(DN_K)):
                        m, j = divmod(n, len(DN_K))
                        if j == 0:
                            pe.wait_ge(dn_read.sem, dn_read.at(l, u * 2 + (f * DC + m + 1 - 2)))
                        k0 = sum(DN_K[:j])
                        piece(dn_ph, u, n, 1 + m, w_lo_ffn, act_hi, act_lo, k0, k0 + DN_K[j], FC)

            for s in kp_used:
                pe.sem_inc(s.sem, s.start)
            pe.wait_ge(s_in.sem, 64)
            pe.wait_ge(cleared.sem, 1)
            with pe.Fori(0, DEPTH) as l:
                l_[0] = l
                ada(l, ADA0, 0, 2)
                sums_of_squares(sq_ready, l, 0)
                ffn(l, 0, GU1, DN1, lambda: ada(l, ADA1, 2, 5))
                sums_of_squares(dn_read, l, 0)
                sums_of_squares(sq_ready, l, 8)

                with pe.Fori(0, PC // RING) as u:
                    for n in range(RING):
                        pe.wait_ge(pj_read.sem, pj_read.at(l, u * RING + (n + 1 - 2)))
                        piece(IN, u, n, n % 2, w_lo_mid, h_hi_mid, h_lo, norm=1 if n == 0 else None)
                pe.wait_ge(pj_read.sem, pj_read.at(l, PC + 1 - 2))
                piece(IN, PC // RING, 0, 0, w_lo_mid, h_hi_mid, h_lo)

                for n, c in enumerate(ROPED):
                    pe.wait_ge(pj_read.sem, pj_read.at(l, PC + 1 if c == KW else c + 1))
                    if n >= 2:
                        pe.wait_ge(rope_done.sem, rope_done.at(l, n - 1))
                    product(2 + n % 2, [swap], [proj[:, c, :]]).then_inc(sw_ready.sem, 1)
                pe.wait_ge(pj_read.sem, pj_read.at(l, PC + 1))
                for j in range(TILES):
                    nc.tensor.transpose(ps[:, 0, j * P:(j + 1) * P], proj[:, VV, j * P:(j + 1) * P], ident)
                nc.tensor.transpose(ps[0:NS, 1, 0:P], proj[:, VV, SEQ:T], ident)
                pe.wait_ge(rope_done.sem, rope_done.at(l, len(ROPED)))
                for j in range(TILES):
                    last = nc.tensor.transpose(ps[:, 4, j * P:(j + 1) * P], proj[:, KW, j * P:(j + 1) * P], ident)
                for hd in range(IH):
                    last = mm(ps[:, 5, hd * NS:(hd + 1) * NS], sel[:, hd, :], proj[:, KW, SEQ:T], start=True, stop=True)
                last.then_inc(tok_pe.sem, 1)

                pe.wait_ge(tok_read.sem, tok_read.at(l, 1))
                pe.wait_ge(gate_full.sem, gate_full.at(l, 16))
                pe.wait_ge(conv_done.sem, conv_done.at(l, 1))
                for c in range(LC):
                    if c >= 2:
                        pe.wait_ge(gate_tanh.sem, gate_tanh.at(l, c - 1))
                    product(2 * (c % 2), [gates[:, 0, c, :]], [xc[:, c, :]])
                    last = product(2 * (c % 2) + 1, [gates[:, 1, c, :]], [xc[:, c, :]])
                    last.then_inc(gz_ready.sem, 1)

                def page_products(pair):
                    for i in range(2):
                        pe.wait_ge(kp_full[i].sem, kp_full[i].at(l, pair * KEYS_SP + KEYS_SP))
                        pe.wait_ge(kp_full_pool[i].sem,
                                   kp_full_pool[i].at(l, pair * (PAGES - KEYS_SP) + (PAGES - KEYS_SP)))
                        pe.wait_ge(id_read.sem, id_read.at(l, pair * 2 + (i + 1 - 2)))
                        hold(pe, passed[1], ks_read.sem, ks_read.at(l, pair * 2 + (i + 1 - 2)))
                        for j in range(PAGES):
                            mm(ps[0:HD, 4 + i, j * 32:(j + 1) * 32], kpage[i][:, j, P:KREC],
                               qiS[:, bass.ds(pair * 2 + i, 1), :, :].rearrange("p a e c -> p (a e c)"), start=True, stop=True)
                            last = mm(ps[:, 6 + i, j * 32:(j + 1) * 32], kpage[i][:, j, 0:P],
                                      qS[:, bass.ds(pair * 2 + i, 1), :].rearrange("p a c -> p (a c)"), start=True, stop=True)
                        last.then_inc(kp_used[i].sem, 1)

                pe.wait_ge(qs_ready.sem, qs_ready.at(l, 1))
                hold(pe, passed[1], gate_tanh.sem, gate_tanh.at(l, LC))
                page_products(0)
                for s in range(NSEQ):
                    mm(ps[0:NS, 2, s * 16:(s + 1) * 16], proj[0:HD, KW, SEQ:T], qiS[0:HD, s, 0, :],
                       start=True, stop=True)
                    last = mm(ps[0:NS, 3, s * 32:(s + 1) * 32], proj[:, KK, SEQ:T], qS[:, s, :], start=True, stop=True)
                last.then_inc(new_pe.sem, 1)

                pe.wait_ge(q_ready.sem, q_ready.at(l, 1))
                for k, (hd, i) in enumerate(DOTS):
                    half, span = hd % 2, (i + 1) * P
                    pe.wait_ge(relu_ready.sem, relu_ready.at(l, k + 1 - 2))
                    keys = proj[0:HD, KW, 0:span] if half == 0 else kd[HD:P, 2, 0:span]
                    mm(ps[:, k % 2, 0:span], proj[half * HD:(half + 1) * HD, QI + hd // 2, i * P:(i + 1) * P], keys,
                       start=True, stop=True).then_inc(dots.sem, 1)
                hold(pe, passed[1], relu_ready.sem, relu_ready.at(l, len(DOTS)))
                with pe.Fori(1, NSEQ // 2) as pair:
                    page_products(pair)
                pe.wait_ge(idx_part.sem, idx_part.at(l, NSEQ))
                hold(pe, passed[1], ks_read.sem, ks_read.at(l, NSEQ))
                for j in range(2 * PAGES):
                    nc.tensor.transpose(ps[0:NS, 4 + j // 8, (j % 8) * HD:(j % 8 + 1) * HD], scT[0:HD, j, :],
                                        ident[0:HD, 0:HD])
                nc.tensor.transpose(ps[0:NS, 2, 0:NS], scT[0:NS, 2 * PAGES, :], ident[0:NS, 0:NS])\
                    .then_inc(scT_pe.sem, 1)

                head_keys = lambda half, kv, j0, j1: (proj[half * HD:(half + 1) * HD, KK, j0:j1] if half == kv
                                                      else kd[half * HD:(half + 1) * HD, kv, j0:j1])
                pe.wait_ge(scS_ready.sem, scS_ready.at(l, 1))

                def scores(n):
                    i, hd = divmod(n, HEADS)
                    half = hd % 2
                    pe.wait_ge(s_masked.sem, s_masked.at(l, n + 1 - 2))
                    mm(ps[:, 4 + n % 2, 0:(i + 1) * P],
                       proj[half * HD:(half + 1) * HD, QQ + hd // 2, i * P:(i + 1) * P],
                       head_keys(half, hd // (HEADS // NKV), 0, (i + 1) * P), start=True, stop=True)\
                        .then_inc(s_pe.sem, 1)

                def transposes(n):
                    pe.wait_ge(s_exp.sem, s_exp.at(l, n + 1))
                    pe.wait_ge(t_read.sem, t_read.at(l, n + 1 - 2))
                    for j in range(n // HEADS + 1):
                        last = nc.tensor.transpose(ps[:, 6 + n % 2, j * P:(j + 1) * P],
                                                   prob[n % 2][:, j * P:(j + 1) * P], ident)
                    last.then_inc(t_pe.sem, 1)

                def values(n):
                    i, hd = divmod(n, HEADS)
                    kv = hd // (HEADS // NKV)
                    pe.wait_ge(t_read.sem, t_read.at(l, n + 1))
                    if hd == 0:
                        pe.wait_ge(o_read.sem, o_read.at(l, i + 1 - 2))
                    for j in range(i + 1):
                        last = mm(ps[:, 2 + i % 2, hd * HD:(hd + 1) * HD], probT[n % 2][:, j * P:(j + 1) * P],
                                  vtok[:, j, kv * HD:(kv + 1) * HD], start=(j == 0), stop=(j == i))
                    last.then_inc(pv_p.sem, 1)

                def output(i):
                    pe.wait_ge(o_read.sem, o_read.at(l, i + 1))
                    pe.wait_ge(yt_read.sem, yt_read.at(l, i))
                    for c in range(4):
                        last = nc.tensor.transpose(ps[:, 1, c * P:(c + 1) * P], ytok[:, c * P:(c + 1) * P], ident)
                    last.then_inc(yt_pe.sem, 1)

                scores(0)
                for n in range(TILES * HEADS):
                    if n + 1 < TILES * HEADS:
                        scores(n + 1)
                    transposes(n)
                    if n:
                        values(n - 1)
                    i, hd = divmod(n, HEADS)
                    if i and hd == 3:
                        pe.wait_ge(ada_read.sem, ada_read.at(l, 5 + i))
                        output(i - 1)
                    if hd == 0 and i:
                        pe.wait_ge(yt_read.sem, yt_read.at(l, i - 1))
                        ada_transposes(l, 5 + i - 1, 1)
                    if hd == 4:
                        pe.wait_ge(modT_ready.sem, modT_ready.at(l, 2 * (5 + i) + 1))
                    ada_chunk(l, ADA2, i * RPF, hd, 0)
                values(TILES * HEADS - 1)
                output(TILES - 1)
                hold(pe, passed[1], modT_ready.sem, modT_ready.at(l, 2 * NMOD))
                ada_transposes(l, NMOD - 1, 0)

                pe.wait_ge(s_masked.sem, s_masked.at(l, TILES * HEADS))
                hold(pe, passed[1], topk_done.sem, topk_done.at(l, 1))
                for j in range(PAGES):
                    nc.tensor.transpose(ps[:, 4, j * NS:(j + 1) * NS], scS[:, j * P:(j + 1) * P], ident[0:NS, 0:NS])
                nc.tensor.transpose(ps[0:NS, 5, 0:NS], scS[:, PAGES * P:PAGES * P + NS], ident[0:NS, 0:NS])\
                    .then_inc(mT_pe.sem, 1)
                pe.wait_ge(t_read.sem, t_read.at(l, TILES * HEADS))
                hold(pe, passed[1], exp_s.sem, exp_s.at(l, 1))
                for s in range(NSEQ):
                    pe.wait_ge(vp_full[s].sem, vp_full[s].at(l, PAGES))
                    out = ps[0:32, 2 + s // 4, (s % 4) * P:(s % 4 + 1) * P]
                    for j in range(PAGES):
                        mm(out, sT3[:, s, j, :], vpage[s][:, j, :], start=(j == 0), stop=False)
                    mm(out, sT3[0:NS, s, PAGES, :], vtok[0:NS, TILES, :], start=False, stop=True)\
                        .then_inc(pv_s.sem, 1)
                pe.wait_ge(sums.sem, sums.at(l, 1))
                mm(ps[:, 6, 0:NSEQ * 32], ones, mx, start=True, stop=True).then_inc(den_pe.sem, 1)
                for half in range(2):
                    hold(pe, passed[1], pv_copied.sem, pv_copied.at(l, half + 1))
                    for s in range(half * 4, half * 4 + 4):
                        last = nc.tensor.transpose(ps[:, 7, s * 32:(s + 1) * 32], o_sample[0:32, s, :],
                                                   ident[0:32, 0:32])
                last.then_inc(pv_t.sem, 1)

                pe.wait_ge(ada_read.sem, ada_read.at(l, NMOD))
                hold(pe, passed[1], y_parts.sem, y_parts.at(l, 1))
                with pe.Fori(0, DC // RING) as u:
                    for n in range(RING):
                        pe.wait_ge(wo_read.sem, wo_read.at(l, u * RING + (n + 1 - 2)))
                        piece(OUT, u, n, n % 2, w_lo_mid, y_hi, y_lo)
                sums_of_squares(wo_read, l, 0)
                sums_of_squares(sq_ready, l, 16)
                ffn(l, 1, GU2, DN2, lambda: None)
                sums_of_squares(dn_read, l, 8)

        @block.scalar
        def _(sc):
            act_fn = nc.scalar.activation
            l_ = [None]

            def squares_of_x(l, k):
                for c in range(DC):
                    act_fn(sq[:, c, :], x[:, c, :], ACT.Square).then_inc(sq_ready.sem, 1)

            def root(l, k):
                sc.wait_ge(ss_ready.sem, ss_ready.at(l, k + 1))
                act_fn(tok2(rinv[:, :]), halves(3), ACT.Sqrt, bias=eps[:, 0:1], scale=1.0 / D).then_inc(root_ready.sem, 1)

            def gain_and_shift(l, k, shift):
                for c in range(DC):
                    sc.wait_ge(xn_ready.sem, xn_ready.at(l, k * DC + c + 1))
                    act_fn(h[:, c, 0:SEQ], h[:, c, 0:SEQ], ACT.Identity, bias=mod[:, shift * DC + c, 0:1],
                           scale=gain[:, c, 0:1]).then_inc(h_act.sem, 1)

            def split(ph, u, n, cols=P):
                i, k = ph.raw(u, n)
                s, m = ph.part(u, n)
                sc.wait_ge(w_full[i].sem, w_full[i].at(l_[0], k + (ph.full0[i] + 1)))
                sc.wait_ge(w_used[s].sem, w_used[s].at(l_[0], m + ph.used0[s]))
                rows = DN_K[n % len(DN_K)] if ph in (DN1, DN2) else DC
                act_fn(w_hi[s][:, 0:rows, 0:cols], wslot[i][:, 0:rows, 0:cols], ACT.Copy).then_inc(w_hi_done.sem, 1)

            def product_done(ph, u, n):
                s, m = ph.part(u, n)
                sc.wait_ge(w_used[s].sem, w_used[s].at(l_[0], m + (ph.used0[s] + 1)))

            def in_rounds(ph, body, peeled=1):
                with sc.Fori(0, ph.rounds - peeled) as u:
                    body(u, lambda n: True)
                for u in range(ph.rounds - peeled, ph.rounds):
                    body(u, lambda n: ph.has(u, n))

            def ffn(l, f, gu_ph, dn_ph):
                def gate_up(u, has):
                    for i in range(2):
                        k = u * 2 + (f * FC + i)
                        if has(2 * i + 2):
                            split(gu_ph, u, 2 * i + 2)
                        product_done(gu_ph, u, 2 * i)
                        sc.wait_ge(act_ready.sem, act_ready.at(l, k + 1 - 2))
                        act_fn(tok2(tsil[:, i, :]), halves(2 * i), ACT.Tanh, scale=0.5).then_inc(tanh_ready.sem, 1)
                        if has(2 * i + 3):
                            split(gu_ph, u, 2 * i + 3)
                        sc.wait_ge(act_raw.sem, act_raw.at(l, k + 1))
                        act_fn(act_hi[:, bass.ds(u * 2 + i, 1), :].rearrange("p a t -> p (a t)"), tsil[:, i, :], ACT.Copy)\
                            .then_inc(act_hi_done.sem, 1)

                in_rounds(gu_ph, gate_up)
                for n in range(2):
                    split(dn_ph, 0, n)

                def columns(u, has):
                    for n in range(2 * len(DN_K)):
                        if has(n + 2):
                            split(dn_ph, u, n + 2)
                        if n % len(DN_K) == len(DN_K) - 1:
                            m = n // len(DN_K)
                            product_done(dn_ph, u, n)
                            for dst, fn in ((h, ACT.Copy), (sq, ACT.Square)):
                                last = act_fn(dst[:, bass.ds(u * 2 + m, 1), :].rearrange("p a (b t) -> p (a b) t", b=2),
                                              halves(1 + m), fn)
                            last.then_inc(dn_read.sem, 1)

                in_rounds(dn_ph, columns)

            for s in (dn_read, pj_read, wo_read, t_read, yt_read, gate_tanh, relu_ready, ks_read):
                sc.sem_inc(s.sem, s.start)
            sc.wait_ge(s_in.sem, 64)
            sc.wait_ge(eps_ready.sem, 1)
            with sc.Fori(0, DEPTH) as l:
                l_[0] = l
                sc.wait_ge(res_done.sem, res_done.at(l, 0))
                squares_of_x(l, 0)
                for n in range(2):
                    split(GU1, 0, n)
                root(l, 0)
                gain_and_shift(l, 0, 0)
                ffn(l, 0, GU1, DN1)
                root(l, 1)
                sc.wait_ge(res_done.sem, res_done.at(l, 1))
                squares_of_x(l, 2)
                for n in range(2):
                    split(IN, 0, n)
                root(l, 2)
                gain_and_shift(l, 1, 3)

                def columns(u, has):
                    for n in range(RING):
                        if has(n + 2):
                            behind = isinstance(u, int) and u * RING + n + 2 == PC
                            split(IN, u, n + 2, cols=LAST if behind else P)
                        product_done(IN, u, n)
                        dst = proj[:, bass.ds(u * RING + n, 1), :].rearrange("p a (b t) -> p (a b) t", b=2)
                        act_fn(dst, halves(n % 2), ACT.Copy).then_inc(pj_read.sem, 1)

                in_rounds(IN, columns)
                product_done(IN, PC // RING, 0)
                act_fn(tok2(proj[:, KW, :]), halves(0), ACT.Copy).then_inc(pj_read.sem, 1)

                sc.wait_ge(lam_in.sem, lam_in.at(l, 1))
                act_fn(small[:, 2, :], small[:, 1, :], ACT.Exp, scale=-1.0).then_inc(lam_exp.sem, 1)
                for c in range(LC):
                    sc.wait_ge(gz_ready.sem, gz_ready.at(l, c + 1))
                    act_fn(tok2(ta[:, c, :]), halves(2 * (c % 2)), ACT.Tanh, bias=small[:, 10, c:c + 1], scale=0.5)
                    act_fn(tok2(tb[:, c, :]), halves(2 * (c % 2) + 1), ACT.Tanh, bias=small[:, 11, c:c + 1], scale=0.5)\
                        .then_inc(gate_tanh.sem, 1)
                sc.wait_ge(loga.sem, loga.at(l, 1))
                act_fn(ta[:, :, :], tc[:, :, :], ACT.Exp)
                act_fn(th[:, :, :], tc[:, :, :], ACT.Tanh, scale=-1.0).then_inc(decay.sem, 1)
                sc.wait_ge(radicand.sem, radicand.at(l, 1))
                act_fn(th[:, :, :], th[:, :, :], ACT.Sqrt).then_inc(root_b.sem, 1)
                sc.wait_ge(gelu_in.sem, gelu_in.at(l, 1))
                act_fn(tc[:, :, :], tc[:, :, :], ACT.Tanh).then_inc(gelu_tanh.sem, 1)

                def page_scores(pair):
                    for i in range(2):
                        sc.wait_ge(kp_used[i].sem, kp_used[i].at(l, pair + 1))
                        dst = sT3[:, bass.ds(pair * 2 + i, 1), 0:PAGES, :].rearrange("p a j c -> p (a j c)")
                        act_fn(dst, ps[:, 6 + i, :], ACT.Copy).then_inc(ks_read.sem, 1)

                page_scores(0)
                sc.wait_ge(new_pe.sem, new_pe.at(l, 1))
                sc.wait_ge(qs_ready.sem, qs_ready.at(l, 1))
                act_fn(sT3[0:NS, :, PAGES, :], ps[0:NS, 3, 0:NSEQ * 32].rearrange("p (s c) -> p s c", s=NSEQ), ACT.Copy)
                for k, (hd, i) in enumerate(DOTS):
                    sc.wait_ge(dots.sem, dots.at(l, k + 1))
                    sc.wait_ge(idx_sum.sem, idx_sum.at(l, k + 1 - 2))
                    act_fn(work[k % 2][:, 0:(i + 1) * P], ps[:, k % 2, 0:(i + 1) * P], ACT.Relu)\
                        .then_inc(relu_ready.sem, 1)
                with sc.Fori(1, NSEQ // 2) as pair:
                    page_scores(pair)

                def transposed(n):
                    i = n // HEADS
                    sc.wait_ge(t_pe.sem, t_pe.at(l, n + 1))
                    if n >= 2:
                        sc.wait_ge(pv_p.sem, pv_p.at(l, n - 1))
                    act_fn(probT[n % 2][:, 0:(i + 1) * P], ps[:, 6 + n % 2, 0:(i + 1) * P], ACT.Copy)\
                        .then_inc(t_read.sem, 1)

                def output(i):
                    sc.wait_ge(yt_pe.sem, yt_pe.at(l, i + 1))
                    act_fn(bias_p[:, i, :], ps[:, 1, :], ACT.Copy).then_inc(yt_read.sem, 1)

                sc.wait_ge(scT_pe.sem, scT_pe.at(l, 1))
                for n in range(TILES * HEADS):
                    i, hd = divmod(n, HEADS)
                    sc.wait_ge(s_masked.sem, s_masked.at(l, n + 1))
                    act_fn(prob[n % 2][:, 0:(i + 1) * P], prob[n % 2][:, 0:(i + 1) * P], ACT.Exp,
                           bias=nmax[:, hd:hd + 1], scale=HD ** -0.5, accum_out=den[:, i % 2, hd:hd + 1])\
                        .then_inc(s_exp.sem, 1)
                    transposed(n)
                    if i and hd == 3:
                        output(i - 1)
                output(TILES - 1)
                sc.wait_ge(mT_pe.sem, mT_pe.at(l, 1))
                sc.wait_ge(yt_read.sem, yt_read.at(l, TILES))
                for i in range(TILES):
                    last = act_fn(y[:, LC:DC, i * P:(i + 1) * P], bias_p[:, i, :].rearrange("p (c t) -> p c t", c=4),
                                  ACT.Copy)
                last.then_inc(yp_done.sem, 1)

                sc.wait_ge(sub_done.sem, sub_done.at(l, 1))
                act_fn(sT, sT, ACT.Exp, scale=HD ** -0.5).then_inc(exp_s.sem, 1)

                sc.wait_ge(ysample.sem, ysample.at(l, 1))
                for half in range(2):
                    c = half * LC
                    act_fn(y_hi[:, c:c + LC, :], y[:, c:c + LC, :], ACT.Copy).then_inc(y_hi_done.sem, 1)
                for n in range(2):
                    split(OUT, 0, n)
                sc.wait_ge(kv_stored.sem, kv_stored.at(l, 3))
                for n in range(DC):
                    if OUT.has(0, n + 2):
                        split(OUT, 0, n + 2)
                    product_done(OUT, 0, n)
                    act_fn(tok2(h[:, n, :]), halves(n % 2), ACT.Copy)
                    act_fn(tok2(sq[:, n, :]), halves(n % 2), ACT.Square).then_inc(wo_read.sem, 1)
                root(l, 3)
                sc.wait_ge(res_done.sem, res_done.at(l, 2))
                squares_of_x(l, 4)
                for n in range(2):
                    split(GU2, 0, n)
                root(l, 4)
                gain_and_shift(l, 2, 6)
                ffn(l, 1, GU2, DN2)
                root(l, 5)

        @block.gpsimd
        def _(pool):
            pool.wait_ge(s_in.sem, 64)
            with pool.Fori(0, DEPTH) as l:
                key_loads(pool, False, l, 0)
                pool.wait_ge(outs_ready.sem, outs_ready.at(l, 1))
                pool.dma_start(layer_of(a["convT"], l).rearrange("a p c n -> (a p) c n"), cout[:, :, :])\
                    .then_inc(states_stored.sem, 16)
                with pool.Fori(1, 2) as pair:
                    key_loads(pool, False, l, pair)
                pool.wait_ge(outs_ready.sem, outs_ready.at(l, 2))
                pool.dma_start(layer_of(a["hT"], l).rearrange("a p c n -> (a p) c n"), hout[:, :, :])\
                    .then_inc(states_stored.sem, 16)
                with pool.Fori(2, NSEQ // 2) as pair:
                    key_loads(pool, False, l, pair)
                hold(pool, passed[2], arena_free.sem, arena_free.at(l, 1))
                for s in range(V_POOL):
                    load_pages(pool, a["v_cache"], l, s * PAGES, 0, PAGES, vpage[s], vp_full[s])
                hold(pool, passed[2], max_in.sem, max_in.at(l, 1))
                nc.gpsimd.partition_all_reduce(mxa, mx, P, RMAX).then_inc(pool_max.sem, 1)

        @block.vector
        def _(dve):
            v = nc.vector
            v.memset(eps[:, :], EPS).then_inc(eps_ready.sem, 1)
            v.memset(gates[:, :, :, :], 0.0).then_inc(cleared.sem, 1)
            for s in (vec_free, idx_part, ada_read, act_ready, s_masked, o_read, res_done, id_read, idx_sum):
                dve.sem_inc(s.sem, s.start)
            dve.wait_ge(s_in.sem, 64)
            with dve.Fori(0, DEPTH) as l:
                st = Steps(dve, dve_step, DVE_STEPS, l, passed[3])

                def steps_of(ap):
                    return ap.rearrange("p c (s t) -> p c s t", t=STEPS)

                def each_step(m):
                    return m[:, :, 1:NC_].unsqueeze(3).to_broadcast([P, DC, NSEQ, STEPS])

                def norm_g(k):
                    return vec[:, V_G + k * DC:V_G + (k + 1) * DC].unsqueeze(2).to_broadcast([P, DC, NC_])

                def split(ph, u, n, w_lo, cols=P):
                    i, _ = ph.raw(u, n)
                    dve.wait_ge(w_hi_done.sem, w_hi_done.at(l, u * ph.per_round + (ph.order0 + n + 1)))
                    rows = DN_K[n % len(DN_K)] if ph in (DN1, DN2) else DC
                    s = n % 2
                    v.tensor_tensor(w_lo[s][:, 0:rows, 0:cols], wslot[i][:, 0:rows, 0:cols],
                                    w_hi[s][:, 0:rows, 0:cols].bitcast(F32), ALU.subtract).then_inc(w_split[i].sem, 1)

                def pre_norm(k, r, scale, shift, hi, ph, w_lo):
                    st.link(v.scalar_tensor_tensor(gain[:, :, :], mod[:, scale * DC:(scale + 1) * DC, :], 1.0,
                                                   norm_g(r), ALU.add, ALU.mult))
                    for n in range(2):
                        split(ph, 0, n, w_lo)
                    dve.wait_ge(root_ready.sem, root_ready.at(l, r + 1))
                    st.link(v.reciprocal(rinv[:, :], rinv[:, :]))
                    for c in range(DC):
                        v.tensor_tensor(h[:, c, :], x[:, c, :], rinv[:, :], ALU.mult).then_inc(xn_ready.sem, 1)
                    dve.wait_ge(xn_ready.sem, xn_ready.at(l, (k + 1) * DC))
                    hn = steps_of(h[:, :, SEQ:T])
                    st.link(v.tensor_tensor(hn, hn, each_step(gain), ALU.mult))
                    st.link(v.tensor_tensor(hn, hn, each_step(mod[:, shift * DC:(shift + 1) * DC, :]), ALU.add))
                    rounded = []
                    for c in range(DC + 1):
                        if c < DC:
                            dve.wait_ge(h_act.sem, h_act.at(l, k * DC + c + 1))
                            rounded.append(st.mark(v.tensor_copy(hi[:, c, :], h[:, c, :])))
                        if c:
                            st.need(rounded[c - 1])
                            v.tensor_tensor(h_lo[:, c - 1, :], h[:, c - 1, :], hi[:, c - 1, :].bitcast(F32),
                                            ALU.subtract).then_inc(h_parts.sem, 1)

                def residual(k, r, gate, factor):
                    dve.wait_ge(h_act.sem, h_act.at(l, DC * (1, 2, 3)[k]))
                    st.link(v.scalar_tensor_tensor(gain[:, :, :], mod[:, gate * DC:(gate + 1) * DC, :], factor,
                                                   norm_g(r), ALU.mult, ALU.mult))
                    dve.wait_ge(root_ready.sem, root_ready.at(l, r + 1))
                    st.link(v.reciprocal(rinv[:, :], rinv[:, :]))
                    st.link(v.tensor_tensor(h[:, :, :], h[:, :, :], rinv[:, :].unsqueeze(1).to_broadcast([P, DC, T]),
                                            ALU.mult))
                    hn, xs = steps_of(h[:, :, SEQ:T]), steps_of(x[:, :, SEQ:T])
                    st.link(v.tensor_tensor(hn, hn, each_step(gain), ALU.mult))
                    v.tensor_tensor(xs, xs, hn, ALU.add)
                    for c in range(DC):
                        last = v.scalar_tensor_tensor(x[:, c, 0:SEQ], h[:, c, 0:SEQ], gain[:, c, 0:1], x[:, c, 0:SEQ],
                                                      ALU.mult, ALU.add)
                    last.then_inc(res_done.sem, 1)
                    dve.wait_ge(res_done.sem, res_done.at(l, k + 1))

                def ffn_operands(f, gu_ph, dn_ph, between):
                    def gate_up(u, has):
                        for i in range(2):
                            k = u * 2 + (f * FC + i)
                            if has(2 * i + 2):
                                split(gu_ph, u, 2 * i + 2, w_lo_ffn)
                            dve.wait_ge(tanh_ready.sem, tanh_ready.at(l, k + 1))
                            st.link(v.scalar_tensor_tensor(tok2(tsil[:, i, :]), tok2(tsil[:, i, :]), 1.0, halves(2 * i),
                                                           ALU.add, ALU.mult))
                            s, m = gu_ph.part(u, 2 * i + 1)
                            dve.wait_ge(w_used[s].sem, w_used[s].at(l, m + (gu_ph.used0[s] + 1)))
                            v.scalar_tensor_tensor(tok2(tsil[:, i, :]), tok2(tsil[:, i, :]), 0.5, halves(2 * i + 1),
                                                   ALU.mult, ALU.mult).then_inc(act_raw.sem, 1)
                            if has(2 * i + 3):
                                split(gu_ph, u, 2 * i + 3, w_lo_ffn)
                            dve.wait_ge(act_hi_done.sem, act_hi_done.at(l, k + 1))
                            c = bass.ds(u * 2 + i, 1)
                            v.tensor_tensor(act_lo[:, c, :].rearrange("p a t -> p (a t)"), tsil[:, i, :],
                                            act_hi[:, c, :].rearrange("p a t -> p (a t)").bitcast(F32), ALU.subtract)\
                                .then_inc(act_ready.sem, 1)

                    with st.loop(U_GU - 1, 2) as u:
                        gate_up(u, lambda n: True)
                    gate_up(U_GU - 1, lambda n: gu_ph.has(U_GU - 1, n))
                    between()
                    for n in range(2):
                        split(dn_ph, 0, n, w_lo_ffn)
                    with dve.Fori(0, dn_ph.rounds - 1) as u:
                        for n in range(dn_ph.per_round):
                            split(dn_ph, u, n + 2, w_lo_ffn)
                    for n in range(dn_ph.per_round - 2):
                        split(dn_ph, dn_ph.rounds - 1, n + 2, w_lo_ffn)

                def ada_half(g, half, ph, rounds, bank):
                    dve.wait_ge(ada_used[RING - 1].sem, ada_used[RING - 1].at(l, rounds + ph.ada0[RING - 1]))
                    v.tensor_copy(modT[:, half * RING:(half + 1) * RING, :],
                                  ps[0:NC_, bank, :].rearrange("p (m n) -> p m n", n=P)).then_inc(modT_ready.sem, 1)

                def ada_bias(g, bank):
                    dve.wait_ge(mod_pe.sem, mod_pe.at(l, g + 1))
                    v.tensor_tensor(mod[:, bass.ds(g * DC, DC), :],
                                    ps[:, bank, 0:DC * NC_].rearrange("p (m c) -> p m c", c=NC_),
                                    vec[:, bass.ds(g * DC + V_BADA, DC)].unsqueeze(2).to_broadcast([P, DC, NC_]),
                                    ALU.add).then_inc(ada_read.sem, 1)

                def ada(ph, first, after):
                    with dve.Fori(first, after) as g:
                        for half in range(2):
                            ada_half(g, half, ph, g * RPF + (half + 1 - first * RPF), half)
                        ada_bias(g, 2)
                    dve.wait_ge(ada_read.sem, ada_read.at(l, after))

                hold(dve, passed[3], vec_full.sem, vec_full.at(l, 2))
                ada(ADA0, 0, 2)
                pre_norm(0, 0, 1, 0, h_hi, GU1, w_lo_ffn)
                ffn_operands(0, GU1, DN1, lambda: ada(ADA1, 2, 5))
                residual(0, 1, 2, 0.5)
                pre_norm(1, 2, 4, 3, h_hi_mid, IN, w_lo_mid)

                lam = vec[:, V_LAM:V_LAM + LC]
                neg, z, z2, poly = small[:, 0, :], small[:, 3, :], small[:, 4, :], small[:, 5, :]
                st.link(v.tensor_scalar(neg, lam, -1.0, None, ALU.mult))
                v.tensor_tensor(small[:, 1, :], neg, lam, ALU.max).then_inc(lam_in.sem, 1)
                v.tensor_scalar(small[:, 10, :], vec[:, V_BA:V_BA + LC], 0.5, None, ALU.mult)
                v.tensor_scalar(small[:, 11, :], vec[:, V_BX:V_BX + LC], 0.5, None, ALU.mult)

                def decay_rate():
                    dve.wait_ge(lam_exp.sem, lam_exp.at(l, 1))
                    st.link(v.tensor_scalar(z2, small[:, 2, :], 2.0, None, ALU.add))
                    st.link(v.reciprocal(z2, z2))
                    st.link(v.tensor_tensor(z, small[:, 2, :], z2, ALU.mult))
                    st.link(v.tensor_tensor(z2, z, z, ALU.mult))
                    st.link(v.tensor_scalar(poly, z2, 1.0 / 19, 1.0 / 17, ALU.mult, ALU.add))
                    for n in (15, 13, 11, 9, 7, 5, 3, 1):
                        st.link(v.tensor_tensor(poly, poly, z2, ALU.mult))
                        st.link(v.tensor_scalar(poly, poly, 1.0 / n, None, ALU.add))
                    st.link(v.tensor_tensor(poly, poly, z, ALU.mult))
                    st.link(v.tensor_scalar(neg, neg, 0.0, None, ALU.max))
                    st.link(v.scalar_tensor_tensor(poly, poly, 2.0, neg, ALU.mult, ALU.add))
                    st.link(v.tensor_scalar(small[:, 6, :], poly, -0.5 * 8.0, None, ALU.mult))

                with dve.Fori(0, IN.rounds - 1) as u:
                    for n in range(RING):
                        split(IN, u, n + 2, w_lo_mid)
                for n in range(2):
                    split(IN, IN.rounds - 1, n + 2, w_lo_mid)
                split(IN, IN.rounds, 0, w_lo_mid, cols=LAST)

                def rotate(n):
                    c = ROPED[n]
                    rows = HD if c == KW else P
                    st.need(products[n])
                    v.tensor_tensor(proj[0:rows, c, :], proj[0:rows, c, :], rtmp[n % 2][0:rows, :], ALU.add)\
                        .then_inc(rope_done.sem, 1)

                products = []
                for n, c in enumerate(ROPED):
                    rows = HD if c == KW else P
                    dve.wait_ge(sw_ready.sem, sw_ready.at(l, n + 1))
                    if n >= 2:
                        dve.wait_ge(rope_done.sem, rope_done.at(l, n - 1))
                    v.tensor_tensor(tok2(rtmp[n % 2][0:rows, :]), ps[0:rows, 4 + 2 * (n % 2):6 + 2 * (n % 2), 0:TH],
                                    tok2(sinT[0:rows, :]), ALU.mult)
                    products.append(st.mark(v.tensor_tensor(proj[0:rows, c, :], proj[0:rows, c, :], cosT[0:rows, :],
                                                            ALU.mult)))
                    if n:
                        rotate(n - 1)
                rotate(len(ROPED) - 1)

                v.memset(qiS, 0.0)
                v.memset(sT3[:, :, PAGES, :], NEG)
                st.link(v.memset(qS, 0.0))
                dve.wait_ge(rope_done.sem, rope_done.at(l, len(ROPED)))
                for hd in range(IH):
                    for e in range(2):
                        half = hd % 2
                        v.tensor_copy(qiS[e * HD:(e + 1) * HD, :, e, hd * STEPS:(hd + 1) * STEPS],
                                      proj[half * HD:(half + 1) * HD, QI + hd // 2, SEQ:T]
                                      .rearrange("p (s t) -> p s t", t=STEPS))
                for hd in range(HEADS):
                    half, kv = hd % 2, hd // (HEADS // NKV)
                    last = v.tensor_copy(qS[kv * HD:(kv + 1) * HD, :, hd * STEPS:(hd + 1) * STEPS],
                                         proj[half * HD:(half + 1) * HD, QQ + hd // 2, SEQ:T]
                                         .rearrange("p (s t) -> p s t", t=STEPS))
                last.then_inc(qs_ready.sem, 1)

                xs = xp[:, :, 3 + SEQ:XPW].rearrange("p c (s w) -> p c s w", w=SW)
                xcs = xc[:, :, SEQ:T].rearrange("p c (s t) -> p c s t", t=STEPS)
                v.memset(xp[:, :, 0:3], 0.0)
                v.tensor_copy(xp[:, :, 3:3 + SEQ], proj[:, XL:XL + LC, 0:SEQ])
                v.tensor_copy(xs[:, :, :, 3:SW], steps_of(proj[:, XL:XL + LC, SEQ:T]))
                st.link(v.tensor_copy(xs[:, :, :, 0:3],
                                      state[:, ST_C:ST_ALL].rearrange("p (c s w) -> p c s w", c=LC, w=3)))
                v.tensor_copy(cout[:, :, 0:3], xp[:, :, SEQ:SEQ + 3])
                v.tensor_copy(cout[:, :, 3:3 * NC_].rearrange("p c (s w) -> p c s w", w=3), xs[:, :, :, STEPS:SW])\
                    .then_inc(outs_ready.sem, 1)
                dve.wait_ge(tok_pe.sem, tok_pe.at(l, 1))
                v.tensor_copy(vtok[:, 0:TILES, :], ps[:, 0, :].rearrange("p (j d) -> p j d", d=P))
                v.tensor_copy(vtok[0:NS, TILES, :], ps[0:NS, 1, 0:P])
                w_scale = HD ** -0.5 * IH ** -0.5
                v.tensor_scalar(wtok, ps[:, 4, :].rearrange("p (j d) -> p j d", d=P)[:, :, HD:HD + IH], w_scale, None,
                                ALU.mult)
                for hd in range(IH):
                    last = v.tensor_scalar(cbuf[:, :, hd * STEPS:(hd + 1) * STEPS],
                                           ps[:, 5, hd * NS:(hd + 1) * NS].rearrange("p (s t) -> p s t", t=STEPS),
                                           w_scale, None, ALU.mult)
                last.then_inc(tok_read.sem, 1)
                for j in range(CONV):
                    for c in range(LC):
                        tap = vec[:, V_CW + j * LC + c:V_CW + j * LC + c + 1]
                        for dst, src in ((xc[:, c, 0:SEQ], xp[:, c, j:j + SEQ]), (xcs[:, c], xs[:, c, :, j:j + STEPS])):
                            if j == 0:
                                last = v.tensor_scalar(dst, src, tap, vec[:, V_CB + c:V_CB + c + 1], ALU.mult, ALU.add)
                            else:
                                last = v.scalar_tensor_tensor(dst, src, tap, dst, ALU.mult, ALU.add)
                    if j < CONV - 1:
                        st.link(last)
                last.then_inc(conv_done.sem, 1)
                decay_rate()

                dve.wait_ge(gate_tanh.sem, gate_tanh.at(l, LC))
                for c in range(LC):
                    last = v.tensor_scalar(tc[:, c, :], ta[:, c, :], 1.0, small[:, 6, c:c + 1], ALU.add, ALU.mult)
                last.then_inc(loga.sem, 1)
                st.link(v.scalar_tensor_tensor(tb, tb, 1.0, xc, ALU.add, ALU.mult))

                def page_index(pair, i, between=lambda: None):
                    dve.wait_ge(kp_used[i].sem, kp_used[i].at(l, pair + 1))
                    dve.wait_ge(idx_part.sem, idx_part.at(l, pair * 2 + i))
                    c16 = cbuf[0:HD, bass.ds(pair * 2 + i, 1), :].to_broadcast([HD, 2 * PAGES, 16])
                    v.scalar_tensor_tensor(relu[0:HD], ps[0:HD, 4 + i, :].rearrange("p (b c) -> p b c", c=16), 0.0,
                                           c16, ALU.max, ALU.mult).then_inc(id_read.sem, 1)
                    between()
                    dve.wait_ge(id_read.sem, id_read.at(l, pair * 2 + (i + 1)))
                    v.tensor_reduce(scT[0:HD, 0:2 * PAGES, bass.ds(pair * (2 * STEPS) + i * STEPS, STEPS)],
                                           relu[0:HD].rearrange("p b (h t) -> p b t h", t=STEPS), AX.X, ALU.add)\
                        .then_inc(idx_part.sem, 1)

                for i in range(2):
                    page_index(0, i)

                dve.wait_ge(decay.sem, decay.at(l, 1))
                st.link(v.tensor_tensor(tc, ta, ta, ALU.mult))
                v.scalar_tensor_tensor(th, tc, 1.0, th, ALU.add, ALU.mult).then_inc(radicand.sem, 1)
                gl = proj[:, GL:GL + LC, :]
                dve.wait_ge(radicand.sem, radicand.at(l, 1))
                st.link(v.tensor_tensor(tc, gl, gl, ALU.mult))
                st.link(v.tensor_scalar(tc, tc, GELU_C * 0.044715, GELU_C, ALU.mult, ALU.add))
                v.tensor_tensor(tc, tc, gl, ALU.mult).then_inc(gelu_in.sem, 1)
                dve.wait_ge(root_b.sem, root_b.at(l, 1))
                st.link(v.scalar_tensor_tensor(tb, tb, 0.5, th, ALU.mult, ALU.mult))
                tas, tbs = steps_of(ta[:, :, SEQ:T]), steps_of(tb[:, :, SEQ:T])
                before = state[:, ST_H:ST_H + LC * NSEQ].rearrange("p (c s) -> p c s", c=LC)
                for t in range(STEPS):
                    product_step = st.mark(v.tensor_tensor(xcs[:, :, :, t], tas[:, :, :, t], before, ALU.mult))
                    v.tensor_tensor_scan(xc[:, t, 0:SEQ], ta[:, t, 0:SEQ], tb[:, t, 0:SEQ], 0.0, ALU.mult, ALU.add)
                    st.need(product_step)
                    st.link(v.tensor_tensor(xcs[:, :, :, t], xcs[:, :, :, t], tbs[:, :, :, t], ALU.add))
                    before = xcs[:, :, :, t]
                v.tensor_copy(hout[:, :, 0:1], xc[:, :, SEQ - 1:SEQ])
                v.tensor_copy(hout[:, :, 1:NC_], xcs[:, :, :, STEPS - 1]).then_inc(outs_ready.sem, 1)
                dve.wait_ge(gelu_tanh.sem, gelu_tanh.at(l, 1))
                st.link(v.scalar_tensor_tensor(tc, tc, 1.0, gl, ALU.add, ALU.mult))
                v.scalar_tensor_tensor(y[:, 0:LC, :], tc, 0.5, xc, ALU.mult, ALU.mult).then_inc(arena_free.sem, 1)
                dve.wait_ge(arena_free.sem, arena_free.at(l, 1))

                v.tensor_copy(kd[HD:P, 0, :], proj[0:HD, KK, 0:SEQ])
                v.tensor_copy(kd[0:HD, 1, :], proj[HD:P, KK, 0:SEQ])
                v.tensor_copy(kd[HD:P, 2, :], proj[0:HD, KW, 0:SEQ]).then_inc(q_ready.sem, 1)
                v.tensor_copy(bias_p[:, 0, 0:P], tri)
                dve.wait_ge(idx_part.sem, idx_part.at(l, 2))
                dve.wait_ge(new_pe.sem, new_pe.at(l, 1))
                new = relu[0:NS, 0:NSEQ, :]
                st.link(v.scalar_tensor_tensor(new, ps[0:NS, 2, 0:NSEQ * 16].rearrange("p (s c) -> p s c", c=16), 0.0,
                                               cbuf[0:NS, :, :], ALU.max, ALU.mult))
                st.link(v.tensor_reduce(scT[0:NS, 2 * PAGES, :].rearrange("p (s t) -> p s t", t=STEPS),
                                        new.rearrange("p s (h t) -> p s t h", t=STEPS), AX.X, ALU.add))

                for k, (hd, i) in enumerate(DOTS):
                    span = (i + 1) * P
                    dve.wait_ge(relu_ready.sem, relu_ready.at(l, k + 1))
                    if hd == 0:
                        ins = v.tensor_scalar(bias_p[:, i, 0:span], work[k % 2][:, 0:span], wtok[:, i, hd:hd + 1], None,
                                              ALU.mult)
                    else:
                        dve.wait_ge(idx_sum.sem, idx_sum.at(l, k + 1 - (TILES - 1)))
                        ins = v.scalar_tensor_tensor(bias_p[:, i, 0:span], work[k % 2][:, 0:span],
                                                     wtok[:, i, hd:hd + 1], bias_p[:, i, 0:span], ALU.mult, ALU.add)
                    ins.then_inc(idx_sum.sem, 1)
                dve.wait_ge(idx_sum.sem, idx_sum.at(l, len(DOTS)))
                tiles = range(1, TILES)
                for i in tiles:
                    st.mark(v.tensor_tensor(bias_p[:, i, i * P:(i + 1) * P], bias_p[:, i, i * P:(i + 1) * P], tri,
                                            ALU.add))

                def top_rounds(rounds):
                    for _ in range(rounds):
                        for i in tiles:
                            st.need_hold(st.n + 1 - len(tiles))
                            st.mark(v.max(top8[:, i, :], bias_p[:, i, 0:(i + 1) * P]))
                        for i in tiles:
                            st.need_hold(st.n + 1 - len(tiles))
                            st.mark(v.match_replace(bias_p[:, i, 0:(i + 1) * P], top8[:, i, :],
                                                    bias_p[:, i, 0:(i + 1) * P], TAKEN))

                ROUNDS = SEL_P // 8
                in_loop = ROUNDS // (NSEQ // 2 - 1)
                with st.loop(NSEQ // 2 - 1, 6 * in_loop, start=1) as pair:
                    for i in range(2):
                        n = in_loop * (i + 1) // 2 - in_loop * i // 2
                        page_index(pair, i, between=lambda: top_rounds(n))
                top_rounds(ROUNDS - in_loop * (NSEQ // 2 - 1))
                st.need(st.n)
                for i in tiles:
                    st.mark(v.tensor_scalar(bias_p[:, i, 0:(i + 1) * P], bias_p[:, i, 0:(i + 1) * P], 0.5 * TAKEN, NEG,
                                            ALU.is_gt, ALU.mult))
                dve.wait_ge(scT_pe.sem, scT_pe.at(l, 1))
                v.tensor_copy(scS[:, 0:PAGES * P].rearrange("p (b k) -> p b k", b=4), ps[0:NS, 4:8, :])
                v.tensor_tensor(scS[:, PAGES * P:PAGES * P + NS], ps[0:NS, 2, 0:NS], mask_new, ALU.add)\
                    .then_inc(scS_ready.sem, 1)

                top_s = top8[0:NS, 0, :]

                def tile_output(i):
                    dve.wait_ge(pv_p.sem, pv_p.at(l, (i + 1) * HEADS))
                    dve.wait_ge(yt_pe.sem, yt_pe.at(l, i))
                    st.link(v.reciprocal(den[:, i % 2, :], den[:, i % 2, :]))
                    v.tensor_tensor(ytok.rearrange("p (h d) -> p h d", d=HD),
                                    ps[:, 2 + i % 2, :].rearrange("p (h d) -> p h d", d=HD),
                                    den[:, i % 2, :].unsqueeze(2).to_broadcast([P, HEADS, HD]), ALU.mult)\
                        .then_inc(o_read.sem, 1)

                assert SEL_S // 8 == TILES * HEADS
                for n in range(TILES * HEADS):
                    i, hd = divmod(n, HEADS)
                    span = (i + 1) * P
                    if n >= 2:
                        dve.wait_ge(t_pe.sem, t_pe.at(l, n - 1))
                    hold(dve, passed[3], s_pe.sem, s_pe.at(l, n + 1))
                    masked = st.mark(v.tensor_tensor_reduce(prob[n % 2][:, 0:span], ps[:, 4 + n % 2, 0:span],
                                                            bias_p[:, i, 0:span], 1.0, TAKEN, ALU.add, ALU.max,
                                                            nmax[:, hd:hd + 1]))
                    if n:
                        st.need_hold(replaced)
                    else:
                        hold(dve, passed[3], scS_ready.sem, scS_ready.at(l, 1))
                    found = st.mark(v.max(top_s, scS))
                    st.need(masked)
                    v.tensor_scalar(nmax[:, hd:hd + 1], nmax[:, hd:hd + 1], -(HD ** -0.5), None, ALU.mult)\
                        .then_inc(s_masked.sem, 1)
                    if i and hd == 1:
                        tile_output(i - 1)
                    if hd == 4:
                        ada_half(5 + i, 0, ADA2, i * RPF + 1, 0)
                    if i and hd == 0:
                        ada_half(5 + i - 1, 1, ADA2, i * RPF, 0)
                    if i and hd == 2:
                        ada_bias(5 + i - 1, 1)
                    st.need_hold(found)
                    replaced = st.mark(v.match_replace(scS, top_s, scS, TAKEN))
                st.need(replaced)
                v.tensor_scalar(scS, scS, 0.5 * TAKEN, NEG, ALU.is_gt, ALU.mult).then_inc(topk_done.sem, 1)
                tile_output(TILES - 1)
                ada_half(NMOD - 1, 1, ADA2, TILES * RPF, 0)
                ada_bias(NMOD - 1, 0)

                dve.wait_ge(mT_pe.sem, mT_pe.at(l, 1))
                v.tensor_copy(maskT[:, 0:PAGES, :], ps[:, 4, :].rearrange("p (j c) -> p j c", c=NS))
                st.link(v.tensor_copy(maskT[0:NS, PAGES, :], ps[0:NS, 5, 0:NS]))
                for s in range(NSEQ):
                    m4 = maskT[:, 0:PAGES, s * STEPS:(s + 1) * STEPS].unsqueeze(2)\
                        .to_broadcast([P, PAGES, HEADS, STEPS])
                    dst = sT3[:, s, 0:PAGES, :].rearrange("p j (h t) -> p j h t", t=STEPS)
                    v.tensor_tensor(dst, dst, m4, ALU.add)
                dst = sT3[0:NS, :, PAGES, :].rearrange("p s (h t) -> p s h t", t=STEPS)
                st.link(v.tensor_tensor(dst, dst, maskT[0:NS, PAGES, :].rearrange("p (s t) -> p s t", t=STEPS).unsqueeze(2)
                                        .to_broadcast([NS, NSEQ, HEADS, STEPS]), ALU.add))
                mx3, mxa3 = (m.rearrange("p (s c) -> p s c", s=NSEQ) for m in (mx, mxa))
                v.tensor_reduce(mx3, sT3.rearrange("p s j c -> p s c j"), AX.X, ALU.max).then_inc(max_in.sem, 1)
                dve.wait_ge(pool_max.sem, pool_max.at(l, 1))
                v.tensor_tensor(sT3, sT3, mxa3.unsqueeze(2).to_broadcast([P, NSEQ, NB, 32]), ALU.subtract)\
                    .then_inc(sub_done.sem, 1)
                dve.wait_ge(exp_s.sem, exp_s.at(l, 1))
                v.tensor_reduce(mx3, sT3.rearrange("p s j c -> p s c j"), AX.X, ALU.add).then_inc(sums.sem, 1)
                for half in range(2):
                    dve.wait_ge(pv_s.sem, pv_s.at(l, 4 * (half + 1)))
                    v.tensor_copy(o_sample[0:32, 4 * half:4 * half + 4, :],
                                  ps[0:32, 2 + half, :].rearrange("p (s d) -> p s d", d=P)).then_inc(pv_copied.sem, 1)
                dve.wait_ge(den_pe.sem, den_pe.at(l, 1))
                st.link(v.reciprocal(rden, ps[:, 6, 0:NSEQ * 32]))
                dve.wait_ge(pv_t.sem, pv_t.at(l, 1))
                for hd in range(HEADS):
                    half, kv = hd % 2, hd // (HEADS // NKV)
                    src = slice(kv * HD, (kv + 1) * HD)
                    last = v.tensor_tensor(
                        y[half * HD:(half + 1) * HD, LC + hd // 2, SEQ:T].rearrange("p (s t) -> p s t", t=STEPS),
                        ps[src, 7, 0:NSEQ * 32].rearrange("p (s c) -> p s c", s=NSEQ)[:, :, hd * STEPS:(hd + 1) * STEPS],
                        rden[src, :].rearrange("p (s c) -> p s c", s=NSEQ)[:, :, hd * STEPS:(hd + 1) * STEPS], ALU.mult)
                last.then_inc(ysample.sem, 1)

                for half in range(2):
                    c = half * LC
                    dve.wait_ge(y_hi_done.sem, y_hi_done.at(l, half + 1))
                    last = v.tensor_tensor(y_lo[:, c:c + LC, :], y[:, c:c + LC, :], y_hi[:, c:c + LC, :].bitcast(F32),
                                           ALU.subtract)
                last.then_inc(y_parts.sem, 1)
                for n in range(DC):
                    split(OUT, 0, n, w_lo_mid)

                residual(1, 3, 5, 1.0)
                pre_norm(2, 4, 7, 6, h_hi, GU2, w_lo_ffn)
                ffn_operands(1, GU2, DN2, lambda: None)
                residual(2, 5, 8, 0.5)
                dve.sem_inc(vec_free.sem, 1)
                dve.wait_ge(kv_stored.sem, kv_stored.at(l, 3))
                dve.wait_ge(states_stored.sem, states_stored.at(l, 2))
                assert st.n == DVE_STEPS, st.n


def rope_tables():
    half = HD // 8
    freqs = np.float32(500000.0) ** (-(np.arange(half, dtype=np.float32) / np.float32(half)))
    pos = np.concatenate([np.arange(SEQ), np.tile(PAGES * PAGE + np.arange(STEPS), NSEQ)]).astype(np.float32)
    ang = freqs.astype(np.float32)[:, None] * pos[None, :]
    cos, sin = np.ones((HD, T), np.float32), np.zeros((HD, T), np.float32)
    cos[0:half] = cos[half:2 * half] = np.cos(ang)
    sin[0:half], sin[half:2 * half] = -np.sin(ang), np.sin(ang)
    return np.tile(cos, (2, 1)), np.tile(sin, (2, 1))


def constants():
    c = np.zeros((P, C_ALL), np.float32)
    c[:, C_ID:C_ID + P] = np.eye(P)
    c[:, C_ONE:C_ONE + P] = 1.0
    half = HD // 8
    for b in (0, HD):
        for r in range(half):
            c[b + half + r, C_SWAP + b + r] = c[b + r, C_SWAP + b + half + r] = 1.0
    c[:, C_COS:C_COS + T], c[:, C_SIN:C_SIN + T] = rope_tables()
    c[:, C_TRI:C_TRI + P] = np.where(np.arange(P)[None, :] <= np.arange(P)[:, None], 0.0, NEG)
    s, t = np.divmod(np.arange(NS), STEPS)
    c[0:NS, C_MS:C_MS + NS] = np.where((s[None, :] == s[:, None]) & (t[None, :] <= t[:, None]), 0.0, NEG)
    for hd in range(IH):
        c[HD + hd, C_SEL + hd * P:C_SEL + (hd + 1) * P] = 1.0
    return c


def by_partition(a, lead):
    s = a.shape
    a = a.reshape(*s[:lead], s[lead] // P, P, *s[lead + 1:])
    return np.ascontiguousarray(np.swapaxes(a, lead, lead + 1))


OUTS = {"yT": (P, DC, T), "kT": (DEPTH, P, T), "vT": (DEPTH, P, T), "kiT": (DEPTH, HD, T),
        "convT": (DEPTH, P, LC, 3 * NC_), "hT": (DEPTH, P, LC, NC_)}


def kernel(**inputs):
    import concourse.bacc as bacc
    from concourse.bass_utils import run_bass_kernel_spmd

    i = {k: np.asarray(v) for k, v in inputs.items()}
    flat = i["x_sample"].reshape(NS, D)
    feat = lambda v: by_partition(v.reshape(DEPTH, -1, P).transpose(0, 1, 2).reshape(DEPTH, -1), 1)
    arrays = {
        "cst": constants(),
        "xT": by_partition(np.concatenate([i["x_prompt"][0], flat]).T, 0),
        "cT": by_partition(np.concatenate([i["c_prompt"], i["c_sample"]]).T, 0),
        "page_table": i["page_table"].reshape(1, -1),
        "vec": np.concatenate([feat(i[k]) for k in ("b_ada", "norm_g", "conv_w", "conv_b", "lru_ba", "lru_bx",
                                                    "lru_lambda")], axis=2),
        "state": np.concatenate([
            by_partition(i["state_h"].transpose(0, 2, 1), 1).reshape(DEPTH, P, -1),
            by_partition(i["state_conv"].transpose(0, 3, 1, 2), 1).reshape(DEPTH, P, -1)], axis=2),
        "key_pages": np.concatenate([
            i["cache_k"].reshape(DEPTH, POOL, PAGE, P).transpose(0, 1, 3, 2),
            i["cache_kidx"].reshape(DEPTH, POOL, 2, PAGE // 2, HD).transpose(0, 1, 2, 4, 3)
            .reshape(DEPTH, POOL, P, PAGE // 2)], axis=3),
        "v_cache": i["cache_v"].reshape(DEPTH, POOL, PAGE, P),
    }
    arrays |= {k: i[k] for k in ("w_ada", "ffn_w_gu", "ffn_w_down", "w_in", "w_out", "lru_wa", "lru_wx")}
    nc = bacc.Bacc("TRN2", target_bir_lowering=False, num_devices=1)
    arrays = {k: np.ascontiguousarray(v) for k, v in arrays.items()}
    a = {k: nc.dram_tensor(k, v.shape, mybir.dt.from_np(v.dtype), kind="ExternalInput").ap() for k, v in arrays.items()}
    a |= {k: nc.dram_tensor(k, s, F32, kind="ExternalOutput").ap() for k, s in OUTS.items()}
    decoder(nc, a)
    r = run_bass_kernel_spmd(nc, [arrays], core_ids=[0]).results[0]

    def tokens(v):
        return v.transpose(2, 1, 0).reshape(v.shape[2], -1)

    y = tokens(r["yT"])
    k, v, ki = (r[n].transpose(0, 2, 1) for n in ("kT", "vT", "kiT"))
    heads = lambda t, lead: t.reshape(*lead, NKV, HD)
    hT = r["hT"].transpose(0, 3, 2, 1).reshape(DEPTH, NC_, -1)
    conv = r["convT"].reshape(DEPTH, P, LC, NC_, 3).transpose(0, 3, 4, 2, 1).reshape(DEPTH, NC_, 3, -1)
    outs = (y[:SEQ].reshape(1, SEQ, D), y[SEQ:].reshape(NSEQ, STEPS, D),
            heads(k[:, :SEQ], (DEPTH, 1, SEQ)), heads(v[:, :SEQ], (DEPTH, 1, SEQ)), ki[:, :SEQ].reshape(DEPTH, 1, SEQ, HD),
            hT[:, 0:1], conv[:, 0:1],
            heads(k[:, SEQ:], (DEPTH, NSEQ, STEPS)), heads(v[:, SEQ:], (DEPTH, NSEQ, STEPS)),
            ki[:, SEQ:].reshape(DEPTH, NSEQ, STEPS, HD), hT[:, 1:], conv[:, 1:])
    return tuple(np.ascontiguousarray(o) for o in outs)
```
